# Optimizing a Trainium2 kernel written in Bass

```python
import jax, jax.numpy as jnp
from jax import lax
import numpy as np

D_MODEL = 1024
BATCH = 1
SEQ = 512
DEPTH = 2
DEC_BATCH = 8
DEC_SEQ = 4
PAST_LEN = 2048
PAGE_SIZE = 128

N_EVEN = (DEPTH + 1) // 2
N_ODD = DEPTH // 2
D_SCONV = D_MODEL // 2
SCONV_W = 3
RET_HEADS = 4
RET_DK = (D_MODEL // 2) // RET_HEADS
RET_DV = RET_DK
RET_CHUNK = 128
ROPE_BASE = 10000.0
NSA_HEADS = 16
NSA_KV = 4
NSA_GROUP = NSA_HEADS // NSA_KV
NSA_DH = D_MODEL // NSA_HEADS
CMP_LEN = 32
CMP_STRIDE = 16
CMP_HIDDEN = 2 * NSA_DH
SLC_BLOCK = 64
SLC_TOPN = 16
WINDOW = 512
Q_BLOCK = 128
D_FF = 256 * ((8 * D_MODEL // 3 + 255) // 256)
FFN_W = 3
ALPHA = (2.0 * DEPTH) ** 0.25
BETA = (8.0 * DEPTH) ** -0.25
LN_EPS = 1e-5
NEG_INF = -1e30
FORCE_BONUS = 1e4

EVEN_SPLITS = [D_SCONV, D_SCONV, D_SCONV, RET_HEADS * RET_DK, RET_HEADS * RET_DK, RET_HEADS * RET_DV, RET_HEADS * RET_DV]
D_IN_EVEN = sum(EVEN_SPLITS)
D_MIX_EVEN = D_SCONV + RET_HEADS * RET_DV
ODD_SPLITS = [NSA_HEADS * NSA_DH] + [NSA_KV * NSA_DH] * 6 + [3 * NSA_HEADS]
D_IN_ODD = sum(ODD_SPLITS)
D_MIX_ODD = NSA_HEADS * NSA_DH

kernel_name = "hybrid_sconv_retention_nsa_convffn_step"

def _split(z, sizes):
    cuts = [int(c) for c in np.cumsum(sizes)[:-1]]
    return jnp.split(z, cuts, axis=-1)

def layer_norm(x, g, b):
    xf = x.astype(jnp.float32)
    mu = jnp.mean(xf, axis=-1, keepdims=True)
    var = jnp.mean(jnp.square(xf - mu), axis=-1, keepdims=True)
    return ((xf - mu) * lax.rsqrt(var + LN_EPS) * g + b).astype(x.dtype)

def causal_dwconv(u, hist, w, b):
    t = u.shape[1]
    full = jnp.concatenate([hist.astype(u.dtype), u], axis=1)
    y = b + full[:, 0:t] * w[0]
    for j in range(1, w.shape[0]):
        y = y + full[:, j:j + t] * w[j]
    return y, full[:, t:]

def rope(x, pos):
    half = x.shape[-1] // 2
    inv = ROPE_BASE ** (-jnp.arange(half, dtype=jnp.float32) / half)
    ang = pos.astype(jnp.float32)[:, None] * inv
    cos = jnp.cos(ang)[None, :, None, :]
    sin = jnp.sin(ang)[None, :, None, :]
    x1, x2 = x[..., :half], x[..., half:]
    return jnp.concatenate([x1 * cos - x2 * sin, x1 * sin + x2 * cos], axis=-1)

def retention_chunk(state, q, k, v, log_gamma):
    c = q.shape[1]
    n = jnp.arange(c, dtype=jnp.float32)
    diff = n[:, None] - n[None, :]
    decay = jnp.where(diff >= 0, jnp.exp(log_gamma[:, None, None] * jnp.maximum(diff, 0.0)), 0.0)
    scores = jnp.einsum("bnhd,bmhd->bhnm", q, k) * decay
    intra = jnp.einsum("bhnm,bmhe->bnhe", scores, v)
    q_dec = jnp.exp((n[:, None] + 1.0) * log_gamma[None, :])
    k_dec = jnp.exp((c - 1.0 - n[:, None]) * log_gamma[None, :])
    cross = jnp.einsum("bnhd,bhde->bnhe", q, state) * q_dec[None, :, :, None]
    new_state = state * jnp.exp(c * log_gamma)[None, :, None, None] + jnp.einsum(
        "bmhd,bmhe->bhde", k * k_dec[None, :, :, None], v)
    return intra + cross, new_state

def retention(q, k, v, state, log_gamma):
    b, t, h, _ = q.shape
    c = RET_CHUNK if t % RET_CHUNK == 0 else t
    nc = t // c

    def to_chunks(a):
        return a.reshape(b, nc, c, h, a.shape[-1]).swapaxes(0, 1)

    def step(s, qkv):
        o, s = retention_chunk(s, qkv[0], qkv[1], qkv[2], log_gamma)
        return s, o

    state, out = lax.scan(step, state, (to_chunks(q), to_chunks(k), to_chunks(v)))
    return out.swapaxes(0, 1).reshape(b, t, h, -1), state

def even_mixer(x, pos, conv_hist, ret_state, w_in, conv_w, conv_b, gn_g, w_out):
    b, t, _ = x.shape
    f32 = jnp.float32
    h, gate_b, gate_c, q, k, v, g = _split(x @ w_in, EVEN_SPLITS)
    u, conv_hist = causal_dwconv(gate_c * h, conv_hist, conv_w, conv_b)
    y_a = gate_b * u
    q = rope(q.reshape(b, t, RET_HEADS, RET_DK).astype(f32), pos) * (RET_DK ** -0.5)
    k = rope(k.reshape(b, t, RET_HEADS, RET_DK).astype(f32), pos)
    v = v.reshape(b, t, RET_HEADS, RET_DV).astype(f32)
    log_gamma = jnp.log1p(-jnp.exp2(-5.0 - jnp.arange(RET_HEADS, dtype=f32)))
    o, ret_state = retention(q, k, v, ret_state.astype(f32), log_gamma)
    mu = jnp.mean(o, axis=-1, keepdims=True)
    var = jnp.mean(jnp.square(o - mu), axis=-1, keepdims=True)
    o = ((o - mu) * lax.rsqrt(var + LN_EPS)).reshape(b, t, -1) * gn_g
    y_b = jax.nn.silu(g.astype(f32)) * o
    y = jnp.concatenate([y_a.astype(x.dtype), y_b.astype(x.dtype)], axis=-1) @ w_out
    return y, conv_hist, ret_state

def compress(rows, pe, w1, w2):
    b, l, g, dh = rows.shape
    r = CMP_LEN // CMP_STRIDE
    n_chunks = l // CMP_STRIDE
    n_cmp = n_chunks - r + 1
    chunks = rows[:, :n_chunks * CMP_STRIDE].reshape(b, n_chunks, CMP_STRIDE, g, dh)
    chunks = chunks.transpose(0, 1, 3, 2, 4).reshape(b, n_chunks, g, CMP_STRIDE * dh)
    w1_parts = w1.reshape(r, CMP_STRIDE * dh, CMP_HIDDEN)
    pre = pe.reshape(-1) @ w1
    for m in range(r):
        pre = pre + jnp.einsum("bngf,fh->bngh", chunks[:, m:m + n_cmp], w1_parts[m])
    return jax.nn.gelu(pre) @ w2

def cmp_attention(q, kc, vc, q_pos):
    b, t = q.shape[:2]
    n = kc.shape[1]
    qg = q.reshape(b, t, NSA_KV, NSA_GROUP, NSA_DH)
    s = jnp.einsum("btgjd,bngd->bgjtn", qg, kc).astype(jnp.float32) * (NSA_DH ** -0.5)
    blk_end = jnp.arange(n) * CMP_STRIDE + CMP_LEN - 1
    valid = blk_end[None, :] <= q_pos[:, None]
    p = jnp.where(valid, jax.nn.softmax(jnp.where(valid, s, NEG_INF), axis=-1), 0.0)
    o = jnp.einsum("bgjtn,bngd->btgjd", p.astype(vc.dtype), vc).reshape(b, t, NSA_HEADS, NSA_DH)
    return o, p

def cmp_to_slc(n_cmp, n_slc):
    i = np.arange(n_cmp)[:, None]
    j = np.arange(n_slc)[None, :]
    start = i * CMP_STRIDE
    return ((start < (j + 1) * SLC_BLOCK) & (start + CMP_LEN > j * SLC_BLOCK)).astype(np.float32)

def select_blocks(p, q_pos, n_slc):
    overlap = jnp.asarray(cmp_to_slc(p.shape[-1], n_slc))
    imp = jnp.einsum("bgjtn,nm->bgtm", p, overlap)
    blk = jnp.arange(n_slc)[None, :]
    cur = (q_pos // SLC_BLOCK)[:, None]
    causal = blk <= cur
    forced = (blk == 0) | (blk == cur) | (blk == cur - 1)
    score = jnp.where(causal, imp + jnp.where(forced, FORCE_BONUS, 0.0), NEG_INF)
    _, idx = lax.top_k(score, min(SLC_TOPN, n_slc))
    ok = jnp.take_along_axis(jnp.broadcast_to(causal, score.shape), idx, axis=-1)
    return idx, ok

def gather_blocks(blocks, idx):
    return jax.vmap(jax.vmap(lambda a, i: a[i]))(blocks, idx)

def gather_paged(pool, page_table, new, kpos, past):
    b_idx = jnp.arange(kpos.shape[0]).reshape(-1, 1, 1, 1, 1)
    g_idx = jnp.arange(NSA_KV).reshape(1, -1, 1, 1, 1)
    page = jnp.clip(kpos // PAGE_SIZE, 0, page_table.shape[1] - 1)
    row = page_table[b_idx, page] * PAGE_SIZE + kpos % PAGE_SIZE
    old = pool.reshape(-1, NSA_KV, NSA_DH)[row, g_idx]
    fresh = new[b_idx, jnp.clip(kpos - past, 0, new.shape[1] - 1), g_idx]
    return jnp.where((kpos < past)[..., None], old, fresh)

def selected_attention(q, ks, vs, q_pos, k_pos, blk_ok):
    b, t = q.shape[:2]
    kk, bl = ks.shape[3], ks.shape[4]
    qg = q.reshape(b, t, NSA_KV, NSA_GROUP, NSA_DH)
    s = jnp.einsum("btgjd,bgtkld->bgjtkl", qg, ks).astype(jnp.float32) * (NSA_DH ** -0.5)
    valid = (blk_ok[..., None] & (k_pos <= q_pos[None, None, :, None, None]))[:, :, None]
    s = jnp.where(valid, s, NEG_INF).reshape(b, NSA_KV, NSA_GROUP, t, kk * bl)
    p = jax.nn.softmax(s, axis=-1).reshape(b, NSA_KV, NSA_GROUP, t, kk, bl)
    o = jnp.einsum("bgjtkl,bgtkld->btgjd", p.astype(vs.dtype), vs)
    return o.reshape(b, t, NSA_HEADS, NSA_DH)

def window_attention(q, k, v, q_pos, k_pos):
    b, t = q.shape[:2]
    qg = q.reshape(b, t, NSA_KV, NSA_GROUP, NSA_DH)
    s = jnp.einsum("btgjd,bsgd->bgjts", qg, k).astype(jnp.float32) * (NSA_DH ** -0.5)
    dist = q_pos[:, None] - k_pos[None, :]
    valid = (dist >= 0) & (dist < WINDOW) & (k_pos[None, :] >= 0)
    p = jax.nn.softmax(jnp.where(valid, s, NEG_INF), axis=-1)
    o = jnp.einsum("bgjts,bsgd->btgjd", p.astype(v.dtype), v)
    return o.reshape(b, t, NSA_HEADS, NSA_DH)

def nsa_project(x, w_in):
    b, t, _ = x.shape
    q, kc, vc, ks, vs, kw, vw, gates = _split(x @ w_in, ODD_SPLITS)

    def kv(a):
        return a.reshape(b, t, NSA_KV, NSA_DH)

    g = jax.nn.sigmoid(gates.astype(jnp.float32)).reshape(b, t, 3, NSA_HEADS)
    return q.reshape(b, t, NSA_HEADS, NSA_DH), kv(kc), kv(vc), kv(ks), kv(vs), kv(kw), kv(vw), g

def nsa_merge(o_cmp, o_slc, o_win, g, w_out):
    o = g[:, :, 0, :, None] * o_cmp + g[:, :, 1, :, None] * o_slc + g[:, :, 2, :, None] * o_win
    b, t = o.shape[:2]
    return o.reshape(b, t, -1).astype(w_out.dtype) @ w_out

def nsa_prompt(q, kc, vc, ks, vs, kw, vw, pe, w1, w2):
    b, s = q.shape[:2]
    pos = jnp.arange(s)
    kcc = compress(kc, pe[0], w1[0], w2[0])
    vcc = compress(vc, pe[1], w1[1], w2[1])
    o_cmp, p = cmp_attention(q, kcc, vcc, pos)
    n_slc = s // SLC_BLOCK
    idx, ok = select_blocks(p, pos, n_slc)
    kb = ks.reshape(b, n_slc, SLC_BLOCK, NSA_KV, NSA_DH).transpose(0, 3, 1, 2, 4)
    vb = vs.reshape(b, n_slc, SLC_BLOCK, NSA_KV, NSA_DH).transpose(0, 3, 1, 2, 4)
    pad = ((0, 0), (WINDOW, 0), (0, 0), (0, 0))
    kwp = jnp.pad(kw, pad)
    vwp = jnp.pad(vw, pad)

    def block(i):
        t0 = i * Q_BLOCK
        qb = lax.dynamic_slice_in_dim(q, t0, Q_BLOCK, axis=1)
        qpos = t0 + jnp.arange(Q_BLOCK)
        ib = lax.dynamic_slice_in_dim(idx, t0, Q_BLOCK, axis=2)
        okb = lax.dynamic_slice_in_dim(ok, t0, Q_BLOCK, axis=2)
        kpos = ib[..., None] * SLC_BLOCK + jnp.arange(SLC_BLOCK)
        o_slc = selected_attention(qb, gather_blocks(kb, ib), gather_blocks(vb, ib), qpos, kpos, okb)
        kwb = lax.dynamic_slice_in_dim(kwp, t0, WINDOW + Q_BLOCK, axis=1)
        vwb = lax.dynamic_slice_in_dim(vwp, t0, WINDOW + Q_BLOCK, axis=1)
        o_win = window_attention(qb, kwb, vwb, qpos, t0 - WINDOW + jnp.arange(WINDOW + Q_BLOCK))
        return o_slc, o_win

    o_slc, o_win = lax.map(block, jnp.arange(s // Q_BLOCK))
    o_slc = o_slc.swapaxes(0, 1).reshape(b, s, NSA_HEADS, NSA_DH)
    o_win = o_win.swapaxes(0, 1).reshape(b, s, NSA_HEADS, NSA_DH)
    return o_cmp, o_slc, o_win

def nsa_sample(q, kc, vc, ks, vs, kw, vw, pool_ck, pool_cv, pool_sk, pool_sv, win_k, win_v, page_table, pe, w1, w2):
    b, t = q.shape[:2]
    past = page_table.shape[1] * PAGE_SIZE
    pos = past + jnp.arange(t)

    def history(pool, new):
        return jnp.concatenate([pool[page_table].reshape(b, past, NSA_KV, NSA_DH), new], axis=1)

    kcc = compress(history(pool_ck, kc), pe[0], w1[0], w2[0])
    vcc = compress(history(pool_cv, vc), pe[1], w1[1], w2[1])
    o_cmp, p = cmp_attention(q, kcc, vcc, pos)
    n_slc = -(-(past + t) // SLC_BLOCK)
    idx, ok = select_blocks(p, pos, n_slc)
    kpos = idx[..., None] * SLC_BLOCK + jnp.arange(SLC_BLOCK)
    k_sel = gather_paged(pool_sk, page_table, ks, kpos, past)
    v_sel = gather_paged(pool_sv, page_table, vs, kpos, past)
    o_slc = selected_attention(q, k_sel, v_sel, pos, kpos, ok)
    wb = win_k.shape[1]
    kw_all = jnp.concatenate([win_k, kw], axis=1)
    vw_all = jnp.concatenate([win_v, vw], axis=1)
    o_win = window_attention(q, kw_all, vw_all, pos, past - wb + jnp.arange(wb + t))
    keep = min(WINDOW, wb + t)
    return o_cmp, o_slc, o_win, kw_all[:, -keep:], vw_all[:, -keep:]

def conv_ffn(x, hist, w_up, conv_w, conv_b, w_down):
    a, gate = jnp.split(x @ w_up, 2, axis=-1)
    a_conv, hist = causal_dwconv(a, hist, conv_w, conv_b)
    return (jax.nn.gelu(a_conv) * gate) @ w_down, hist

def setup_inputs(seed: int = 0) -> dict:
    key = jax.random.key(seed)
    keys = iter(jax.random.split(key, 40))

    def nrm(shape, scale=1.0):
        return jax.random.normal(next(keys), shape, jnp.float32) * scale

    n_pages = PAST_LEN // PAGE_SIZE
    n_phys = (5 * DEC_BATCH * n_pages) // 4
    win_buf = min(WINDOW, PAST_LEN)
    pool = (N_ODD, n_phys, PAGE_SIZE, NSA_KV, NSA_DH)
    perm = jax.random.permutation(next(keys), n_phys)
    page_table = perm[:DEC_BATCH * n_pages].reshape(DEC_BATCH, n_pages).astype(jnp.int32)
    return {
        "x_prompt": nrm((BATCH, SEQ, D_MODEL)),
        "x_sample": nrm((DEC_BATCH, DEC_SEQ, D_MODEL)),
        "state_sconv": nrm((N_EVEN, DEC_BATCH, SCONV_W - 1, D_SCONV)),
        "state_ret": nrm((N_EVEN, DEC_BATCH, RET_HEADS, RET_DK, RET_DV)),
        "cache_cmp_k": nrm(pool),
        "cache_cmp_v": nrm(pool),
        "cache_slc_k": nrm(pool),
        "cache_slc_v": nrm(pool),
        "cache_win_k": nrm((N_ODD, DEC_BATCH, win_buf, NSA_KV, NSA_DH)),
        "cache_win_v": nrm((N_ODD, DEC_BATCH, win_buf, NSA_KV, NSA_DH)),
        "state_ffn_conv": nrm((DEPTH, DEC_BATCH, FFN_W - 1, D_FF)),
        "page_table": page_table,
        "w_in_even": nrm((N_EVEN, D_MODEL, D_IN_EVEN), D_MODEL ** -0.5),
        "sconv_w": nrm((N_EVEN, SCONV_W, D_SCONV), SCONV_W ** -0.5),
        "sconv_b": nrm((N_EVEN, D_SCONV), 0.01),
        "ret_gn_g": 1.0 + nrm((N_EVEN, RET_HEADS * RET_DV), 0.01),
        "w_out_even": nrm((N_EVEN, D_MIX_EVEN, D_MODEL), BETA * D_MIX_EVEN ** -0.5),
        "w_in_odd": nrm((N_ODD, D_MODEL, D_IN_ODD), D_MODEL ** -0.5),
        "cmp_pe": nrm((N_ODD, 2, CMP_LEN, NSA_DH), 0.1),
        "cmp_w1": nrm((N_ODD, 2, CMP_LEN * NSA_DH, CMP_HIDDEN), (CMP_LEN * NSA_DH) ** -0.5),
        "cmp_w2": nrm((N_ODD, 2, CMP_HIDDEN, NSA_DH), CMP_HIDDEN ** -0.5),
        "w_out_odd": nrm((N_ODD, D_MIX_ODD, D_MODEL), BETA * D_MIX_ODD ** -0.5),
        "ln_mix_g": 1.0 + nrm((DEPTH, D_MODEL), 0.01),
        "ln_mix_b": nrm((DEPTH, D_MODEL), 0.01),
        "ffn_w_up": nrm((DEPTH, D_MODEL, 2 * D_FF), D_MODEL ** -0.5),
        "ffn_conv_w": nrm((DEPTH, FFN_W, D_FF), FFN_W ** -0.5),
        "ffn_conv_b": nrm((DEPTH, D_FF), 0.01),
        "ffn_w_down": nrm((DEPTH, D_FF, D_MODEL), BETA * D_FF ** -0.5),
        "ln_ffn_g": 1.0 + nrm((DEPTH, D_MODEL), 0.01),
        "ln_ffn_b": nrm((DEPTH, D_MODEL), 0.01),
    }

def reference(x_prompt, x_sample, state_sconv, state_ret, cache_cmp_k, cache_cmp_v, cache_slc_k, cache_slc_v,
              cache_win_k, cache_win_v, state_ffn_conv, page_table,
              w_in_even, sconv_w, sconv_b, ret_gn_g, w_out_even,
              w_in_odd, cmp_pe, cmp_w1, cmp_w2, w_out_odd,
              ln_mix_g, ln_mix_b, ffn_w_up, ffn_conv_w, ffn_conv_b, ffn_w_down, ln_ffn_g, ln_ffn_b):
    xp, xs = x_prompt, x_sample
    b_p, s_p, _ = xp.shape
    b_s, t_s, _ = xs.shape
    past = page_table.shape[1] * PAGE_SIZE
    pos_p = jnp.arange(s_p)
    pos_s = past + jnp.arange(t_s)
    sconv_p, sconv_s, ret_p, ret_s = [], [], [], []
    cmp_k_p, cmp_v_p, slc_k_p, slc_v_p = [], [], [], []
    cmp_k_s, cmp_v_s, slc_k_s, slc_v_s = [], [], [], []
    win_k_p, win_v_p, win_k_s, win_v_s = [], [], [], []
    ffn_p, ffn_s = [], []
    for layer in range(DEPTH):
        if layer % 2 == 0:
            e = layer // 2
            w = (w_in_even[e], sconv_w[e], sconv_b[e], ret_gn_g[e], w_out_even[e])
            mix_p, hc, st = even_mixer(xp, pos_p, jnp.zeros((b_p, SCONV_W - 1, D_SCONV), xp.dtype),
                                       jnp.zeros((b_p, RET_HEADS, RET_DK, RET_DV), jnp.float32), *w)
            sconv_p.append(hc)
            ret_p.append(st)
            mix_s, hc, st = even_mixer(xs, pos_s, state_sconv[e], state_ret[e], *w)
            sconv_s.append(hc)
            ret_s.append(st)
        else:
            o = layer // 2
            q, kc, vc, ks, vs, kw, vw, g = nsa_project(xp, w_in_odd[o])
            oc, osl, ow = nsa_prompt(q, kc, vc, ks, vs, kw, vw, cmp_pe[o], cmp_w1[o], cmp_w2[o])
            mix_p = nsa_merge(oc, osl, ow, g, w_out_odd[o])
            keep = min(WINDOW, s_p)
            cmp_k_p.append(kc)
            cmp_v_p.append(vc)
            slc_k_p.append(ks)
            slc_v_p.append(vs)
            win_k_p.append(kw[:, -keep:])
            win_v_p.append(vw[:, -keep:])
            q, kc, vc, ks, vs, kw, vw, g = nsa_project(xs, w_in_odd[o])
            oc, osl, ow, wk, wv = nsa_sample(q, kc, vc, ks, vs, kw, vw, cache_cmp_k[o], cache_cmp_v[o],
                                             cache_slc_k[o], cache_slc_v[o], cache_win_k[o], cache_win_v[o],
                                             page_table, cmp_pe[o], cmp_w1[o], cmp_w2[o])
            mix_s = nsa_merge(oc, osl, ow, g, w_out_odd[o])
            cmp_k_s.append(kc)
            cmp_v_s.append(vc)
            slc_k_s.append(ks)
            slc_v_s.append(vs)
            win_k_s.append(wk)
            win_v_s.append(wv)
        xp = layer_norm(ALPHA * xp + mix_p, ln_mix_g[layer], ln_mix_b[layer])
        xs = layer_norm(ALPHA * xs + mix_s, ln_mix_g[layer], ln_mix_b[layer])
        wf = (ffn_w_up[layer], ffn_conv_w[layer], ffn_conv_b[layer], ffn_w_down[layer])
        f_p, h_p = conv_ffn(xp, jnp.zeros((b_p, FFN_W - 1, D_FF), xp.dtype), *wf)
        f_s, h_s = conv_ffn(xs, state_ffn_conv[layer], *wf)
        ffn_p.append(h_p)
        ffn_s.append(h_s)
        xp = layer_norm(ALPHA * xp + f_p, ln_ffn_g[layer], ln_ffn_b[layer])
        xs = layer_norm(ALPHA * xs + f_s, ln_ffn_g[layer], ln_ffn_b[layer])
    st = jnp.stack
    return (xp, xs, st(sconv_p), st(sconv_s), st(ret_p), st(ret_s),
            st(cmp_k_p), st(cmp_v_p), st(slc_k_p), st(slc_v_p),
            st(cmp_k_s), st(cmp_v_s), st(slc_k_s), st(slc_v_s),
            st(win_k_p), st(win_v_p), st(win_k_s), st(win_v_s),
            st(ffn_p), st(ffn_s))


_drawn_inputs = setup_inputs


def setup_inputs(seed=0):
    import zlib

    import numpy as np

    out = dict(_drawn_inputs(seed))
    spreads = {}
    factors = {'cache_cmp_k': 5.715,
     'cache_cmp_v': 4.66,
     'cache_slc_k': 6.723,
     'cache_slc_v': 5.425,
     'sconv_b': 8.0,
     'ret_gn_g': 8.0,
     'cmp_pe': 5.304,
     'ln_mix_g': 3.757,
     'ln_mix_b': 3.841,
     'ffn_conv_b': 8.0,
     'ln_ffn_g': 3.823,
     'ln_ffn_b': 3.754}
    for name, (base, spread) in spreads.items():
        noise = np.random.default_rng([zlib.crc32(name.encode()), seed]).standard_normal(out[name].shape)
        drawn = base * np.exp(spread * noise) if base else spread * noise
        out[name] = __import__('jax').numpy.asarray(drawn.astype(out[name].dtype))
    for name, factor in factors.items():
        out[name] = (out[name] * factor).astype(out[name].dtype)
    return out
```

```python
from contextlib import ExitStack

import numpy as np
import concourse.bass as bass
from concourse import mybir

F32 = mybir.dt.float32
I32 = mybir.dt.int32
ALU = mybir.AluOpType
ACT = mybir.ActivationFunctionType
AX = mybir.AxisListType

D = 1024
SEQ, NB, NT = 512, 8, 4
NS = NB * NT
T = SEQ + NS
HT = T // 2
KC = D // 128
DFF = 2816
FC = DFF // 128
RH = 4
PAST, PAGE = 2048, 128
NPG = PAST // PAGE
NPHYS = 160
NC = PAST // 16
NCMP = NC - 1
NCP = SEQ // 16
NSLC = 33
TOPN = 16
W = 512
NEG = -1e30
ALPHA = 4.0 ** 0.25
EPS = 1e-5
CW = 2 + SEQ + NB * (2 + NT)
CO = CW - 2
SO = SEQ + 2

GEMMS = [("in0", 28, 28), ("out0", 8, 8), ("up0", 44, 44), ("down0", 24, 8),
         ("in1", 20, 20), ("out1", 8, 8), ("up1", 44, 44), ("down1", 24, 8)]
PB, SB = {}, {}
_p = _s = 0
for _n, _a, _b in GEMMS:
    PB[_n], SB[_n] = _p, _s // 2
    _p += _a
    _s += _b


class Steps:

    def __init__(self, sem, names):
        self.sem, self.n = sem, len(names)
        self.index = {name: k for k, name in enumerate(names)}

    def at(self, name, r=0):
        return r * self.n + (self.index[name] + 1)


def layout_consts():
    c = {}
    c["ident"] = np.eye(128)
    c["mean_d"] = np.full((128, 128), 1.0 / D)
    c["mean_h"] = np.full((128, 128), 1.0 / 128)
    pos = np.concatenate([np.arange(SEQ), np.tile(PAST + np.arange(NT), NB)]).astype(np.float32)
    inv = (np.float32(10000.0) ** (-np.arange(64, dtype=np.float32) / np.float32(64))).astype(np.float32)
    ang = (pos[None, :] * inv[:, None]).astype(np.float32).astype(np.float64)
    c["rope_cos"] = np.concatenate([np.cos(ang)] * 2)
    c["rope_sin"] = np.concatenate([-np.sin(ang), np.sin(ang)])
    swap = np.zeros((128, 128))
    swap[(np.arange(128) + 64) % 128, np.arange(128)] = 1.0
    c["swap"] = swap
    lg = np.log1p(-np.exp2(-5.0 - np.arange(RH)))
    scale = 128 ** -0.5
    m, n = np.arange(128)[:, None], np.arange(128)[None, :]
    c["decay"] = np.concatenate([np.where(n >= m, np.exp(g * np.maximum(n - m, 0)), 0) * scale for g in lg], 1)
    c["qdec"] = np.concatenate([np.tile(np.exp((np.arange(128) + 1.0) * g) * scale, (128, 1)) for g in lg], 1)
    c["kdec"] = np.stack([np.exp((127.0 - np.arange(128)) * g) for g in lg], 1)
    t = np.arange(NS)
    same = (t[:, None] // NT) == (t[None, :] // NT)
    dt = t[None, :] - t[:, None]
    ds_ = np.concatenate([np.where(same & (dt >= 0), np.exp(g * np.maximum(dt, 0)), 0) * scale for g in lg], 1)
    c["decay_s"] = np.pad(ds_, ((0, 96), (0, 0)))
    c["qdec_s"] = np.concatenate([np.tile(np.exp((t % NT + 1.0) * g) * scale, (128, 1)) for g in lg], 1)
    c["kdec_s"] = np.pad(np.stack([np.exp((NT - 1.0 - t % NT) * g) for g in lg], 1), ((0, 96), (0, 0)))
    c["seq_of"] = np.pad((t[:, None] // NT == np.arange(NB)[None, :]).astype(float), ((0, 96), (0, 0)))
    row = np.arange(128)
    rb, rgp, rg2, rj, rt = row // 64, row // 32 % 2, row // 16 % 2, row // 4 % 4, row % 4
    c["causal"] = np.where(n <= m, 0.0, NEG)
    blk = np.arange(32)[None, :] * 16 + 31
    tok = (np.arange(4)[None, :] * 128 + np.arange(128)[:, None])[:, :, None]
    ok = (blk[None] <= tok) & (np.arange(32) < NCP - 1)[None, None]
    c["cmp_mask"] = np.where(ok, 0.0, NEG).reshape(128, 128)
    c["cmp_valid"] = ok.astype(float).reshape(128, 128)
    sel = np.zeros((128, 3, 128))
    for br in range(3):
        sel[br * 16 + rgp * 8 + rj * 2 + rg2, br, row] = 1.0
    c["head_of_row"] = sel.reshape(128, 384)
    pair, b2, tt = t // 8, t // 4 % 2, t % 4
    c["token_of_row"] = ((b2[None, :] == rb[:, None]) & (tt[None, :] == rt[:, None])).astype(float)
    key = (rb * 4 + rgp * 2 + rg2) * 4 + rt
    c["heads_sum"] = (key[:, None] == key[None, :]).astype(float)
    j = np.arange(NSLC)
    c["bonus"] = np.tile(np.where((j == 0) | (j >= NSLC - 2), 1e4, 0.0), (128, 1))
    c["earlier"] = np.tile((j[None, :] < j[:, None]).astype(float).reshape(1, -1), (128, 1))
    fm = np.zeros((128, 4, NS))
    for r in range(4):
        own = (pair[None, :] == r) & (b2[None, :] == rb[:, None]) & (tt[None, :] <= rt[:, None])
        fm[:, r] = np.where(own, 0.0, NEG)
    c["fresh_mask"] = fm.reshape(128, 128)
    c["win_mask"] = np.where(np.arange(32)[None, :] > rt[:, None], 0.0, NEG)
    return {k: np.ascontiguousarray(v, dtype=np.float32) for k, v in c.items()}


CONSTS = layout_consts()
KEEP = ["ident", "mean_d", "causal", "cmp_mask", "cmp_valid", "head_of_row", "token_of_row", "heads_sum",
        "bonus", "earlier", "fresh_mask", "win_mask"]
EARLY = ["mean_h", "rope_cos", "rope_sin", "swap", "decay", "qdec", "kdec", "decay_s", "qdec_s", "kdec_s", "seq_of"]
VECS = [("sconv", 16), ("gn_g", 4), ("ln_g", 32), ("ln_b", 32), ("fconv", 2 * FC * 4), ("pe", 32)]


def build(nc, A):
    ctx = ExitStack()
    with ctx:
        def sem(name):
            return ctx.enter_context(nc.semaphore(name))

        sb = ctx.enter_context(nc.sbuf_tensor("sb", [128, 53000], F32))
        ptab = ctx.enter_context(nc.sbuf_tensor("ptab", [1, NB * NPG], I32))
        ps = ctx.enter_context(nc.psum_tensor("ps", [128, 8, 512], F32))
        top = [0]

        def alloc(n, base=None):
            b = top if base is None else base
            v = sb[:, b[0]:b[0] + n]
            b[0] += n
            assert b is not top or top[0] <= 53000, top
            return v

        x = alloc(KC * T).rearrange("p (k t) -> p k t", k=KC)
        y_at = top[0]
        y = alloc(KC * T).rearrange("p (k t) -> p k t", k=KC)
        big = alloc(28 * T).rearrange("p (k t) -> p k t", k=28)
        ring = alloc(4 * 1024).rearrange("p (s n) -> p s n", s=4)
        slot_at = top[0]
        slots = alloc(4 * 4096).rearrange("p (s n) -> p s n", s=4)
        w1 = alloc(2 * 2048).rearrange("p (v n) -> p v n", v=2)
        w2 = alloc(2 * 64).rearrange("p (v n) -> p v n", v=2)
        wg = alloc(KC * 48).rearrange("p (k n) -> p k n", k=KC)
        keep_w = sum(CONSTS[k].shape[1] for k in KEEP)
        keep_all = alloc(keep_w)
        K = {}
        at = 0
        for k in KEEP:
            n = CONSTS[k].shape[1]
            K[k] = keep_all[:, at:at + n]
            at += n
        vec_w = sum(n for _, n in VECS)
        vec_all = alloc(vec_w)
        at = 0
        for k, n in VECS:
            K[k] = vec_all[:, at:at + n]
            at += n
        eps = alloc(1)
        fresh_v = alloc(512).rearrange("p (v n) -> p v n", v=2)
        grow = alloc(12)

        e = [slot_at]
        ret_states = alloc(NB * RH * 128, e).rearrange("p (b h e) -> p b h e", b=NB, h=RH)
        early_w = sum(CONSTS[k].shape[1] for k in EARLY)
        early_all = alloc(early_w, e)
        at = 0
        for k in EARLY:
            n = CONSTS[k].shape[1]
            K[k] = early_all[:, at:at + n]
            at += n
        sconv_hist = alloc(4 * 16, e).rearrange("p (c b w) -> p c b w", c=4, b=NB)
        sconv_out = alloc(4 * 18, e).rearrange("p (c w) -> p c w", c=4)
        rope_t = alloc(T, e)
        k_nat, v_nat, s_dec, q_dec, state = (alloc(512, e) for _ in range(5))
        v_blk = alloc(NB * 128, e)
        conv_u, conv_c, conv_d = alloc(CW, e), alloc(CO + 2, e), alloc(CO, e)
        gn_sq, gn_sd = alloc(T, e), alloc(T, e)
        assert e[0] <= slot_at + 3 * 4096 + 4096 - 0, e[0] - slot_at
        e = [slot_at + 3 * 4096]
        ffn_a = alloc(2 * CW, e).rearrange("p (u n) -> p u n", u=2)
        ffn_c = alloc(2 * (CO + 2), e).rearrange("p (u n) -> p u n", u=2)
        ffn_g = alloc(2 * T, e).rearrange("p (u n) -> p u n", u=2)
        ffn_hist = alloc(FC * 16, e).rearrange("p (c b w) -> p c b w", c=FC, b=NB)
        ffn_out = alloc(FC * 18, e).rearrange("p (c w) -> p c w", c=FC)
        assert e[0] <= slot_at + 4 * 4096

        def ln_row(r, k):
            return big[:, (8 if r == 2 else 24) + k, :]

        w_in = [sem(f"w_in{s}") for s in range(4)]
        pieces = sem("pieces")
        freed = [sem(f"freed{s}") for s in range(2)]
        consts_in = sem("consts_in")
        early_in = sem("early_in")
        x_in = sem("x_in")
        nsa_in = sem("nsa_in")
        hist_in = sem("hist_in")
        ln_sum, ln_mean, ln_cen, ln_sq, ln_var, ln_std, ln_rs, ln_nrm, ln_x = (
            sem(n) for n in ("ln_sum", "ln_mean", "ln_cen", "ln_sq", "ln_var", "ln_std", "ln_rs", "ln_nrm", "ln_x"))
        ln_zero = sem("ln_zero")
        out_done = sem("out_done")
        pool_set = sem("pool_set")

        def half(v):
            return v.rearrange("p (h t) -> p h t", h=2)

        def pset(s):
            return ps[:, 2 * s:2 * s + 2, 0:HT]

        rope_pe = sem("rope_pe")
        RD = Steps(sem("rope_dve"), ["sin", "cos", "add"])
        RP = Steps(sem("ret_pe"), ["kT", "vT", "sc", "o", "kv"])
        RV = Steps(sem("ret_dve"), ["kn", "st", "qd", "state"])
        RA = Steps(sem("ret_act"), ["vn", "o"])
        SP_ = Steps(sem("rets_pe"), ["kT", "vT", "sc", "o"])
        SV = Steps(sem("rets_dve"), ["kn", "st", "qd", "vb"])
        SA = Steps(sem("rets_act"), ["vn", "o"])
        kv_s = sem("kv_s")
        st_s = sem("st_s")
        GP = Steps(sem("gn_pe"), ["mean", "var"])
        GV = Steps(sem("gn_dve"), ["cen", "rs", "nrm", "gn", "mul"])
        GA = Steps(sem("gn_act"), ["sq", "std"])
        gn_gate = sem("gn_gate")
        yb_done = sem("yb_done")
        ya = Steps(sem("conv_pool"), ["hist", "up", "us", "t0", "t1", "s1", "t2", "s2", "keep", "yp", "ys"])
        ret_in = sem("ret_in")
        zero_u = sem("zero_u")
        QZ, KZ, VZ, GZ, CZ, HZ, BZ = 0, 4, 8, 12, 16, 20, 24

        def in0_done(row):
            return PB["in0"] + row + 1

        fa = Steps(sem("ffn_act"), ["a", "gelu"])
        fd = Steps(sem("ffn_dve"), ["c0", "c1", "c2"])
        fp = Steps(sem("ffn_pool"), ["in", "out"])
        hist_load = sem("hist_load")
        ffn_zero = sem("ffn_zero")
        hist_store = sem("hist_store")

        def conv_sample(c):
            return c[:, SO:SO + 6 * NB].rearrange("p (b w) -> p b w", b=NB)[:, :, 0:NT]

        KVR = 8
        KS, VS, KW, VW, OR = 12, 14, 16, 18, 20
        cbias = alloc(2)
        soft = alloc(48)
        e = [y_at]
        v_nat_p = alloc(2048, e).rearrange("p (v t n) -> p v t n", v=2, t=4)
        c_p = alloc(2048, e).rearrange("p (v c g n) -> p v c g n", v=2, c=8, g=4)
        gtok = alloc(192, e).rearrange("p (q b h) -> p q b h", q=4, b=3)
        e = [slot_at + 3 * 4096]
        kcc_p = alloc(64, e).rearrange("p (g n) -> p g n", g=2)
        vcc_p = alloc(256, e)
        q_st = alloc(512, e)
        prob = alloc(2 * 1056, e).rearrange("p (u n) -> p u n", u=2)
        pt_p = alloc(9 * 128, e).rearrange("p (t n) -> p t n", t=9)
        bs_p, hid_p = pt_p[:, 0, :].rearrange("p (g n) -> p g n", g=4), pt_p[:, 1, :].rearrange("p (g n) -> p g n", g=4)
        gate_t = big[0:48, 27, :]
        grow_m = pt_p[:, 2, 0:96].rearrange("p (b w t) -> p b w t", b=3, w=4)
        nmax = soft[:, 0:6].rearrange("p (u n) -> p u n", u=2)
        rsum = soft[:, 6:12].rearrange("p (u n) -> p u n", u=2)
        fac = soft[:, 12:18].rearrange("p (u n) -> p u n", u=2)
        growv = grow.rearrange("p (b w) -> p b w", b=3)
        e = [y_at]
        sc_s = alloc(2048 + NS, e)
        sc_w = alloc(W + NS, e)
        kcc = alloc(512, e).rearrange("p (b g n) -> p b g n", b=2, g=2)
        vcc = alloc(512, e).rearrange("p (b n) -> p b n", b=2)
        qb = alloc(256, e).rearrange("p (b g n) -> p b g n", b=2, g=2)
        pc = alloc(128, e)
        pj = alloc(136, e)
        score, rank_a, rank_b = alloc(NSLC, e), alloc(NSLC, e), alloc(NSLC, e)
        cmpx = sc_s[:, 0:NSLC * NSLC].rearrange("p (m n) -> p m n", m=NSLC)
        assert e[0] <= y_at + KC * T
        pt_s = [big[:, t // 4, (t % 4) * 128:(t % 4) * 128 + 128] for t in range(16)]
        pt_w = [big[:, 5, t * 128:t * 128 + 128] for t in range(4)]
        pt_c, pt_fs, pt_fw = (big[:, 6, t * 128:t * 128 + 128] for t in range(3))
        win_k = big[:, 8:12, 0:W].rearrange("p (b g) n -> p b g n", b=2)
        bs_s = [big[:, 16, 0:512], big[:, 19, 0:512]]
        hid_s = [big[:, 17, 0:512], big[:, 18, 0:512]]
        s_nm, s_sum, s_fac = soft[:, 20:23], soft[:, 23:26], soft[:, 26:29]

        tab_in = sem("tab_in")
        turn, turn_v = sem("turn"), sem("turn_v")
        slot_in = [sem(f"slot_in{s}") for s in range(4)]
        kv_store = sem("kv_store")
        NP = Steps(sem("prep_pe"), ["gate", "gT", "grow", "V0", "V1", "V2", "V3", "F", "bias", "k1", "v1", "k2", "v2"])
        NA = Steps(sem("prep_act"), ["sig", "V0", "V2", "bias", "C", "Bk", "hk", "Bv", "hv"])
        ND = Steps(sem("prep_dve"), ["C", "gtok", "gm", "grow", "V1", "V3", "F", "prek", "prev", "kcc", "vcc"])
        U = range(8)

        def of(names, u):
            return [f"{a}{u}" for a in names.split()] if 0 <= u < 8 else []

        TP = Steps(sem("att_pe"), of("s", 0) + of("s", 1) + sum((of("t", u) + of("s", u + 2) + of("o", u) for u in U), []))
        TA = Steps(sem("att_act"), ["q"] + of("e", 0) + of("e", 1) + sum((of("ta", u) + of("e", u + 2) for u in U), []) + ["ov"])
        TD = Steps(sem("att_dve"), of("dm cm mx my", 0) + of("dm cm mx my", 1) + of("rc fa p", 0)
                   + sum((of("tb", u) + of("rc fa p", u + 1) + of("dm cm mx my", u + 2) for u in U), []))
        XP = Steps(sem("smp_pe"), ["ck0", "ck1", "k20", "k21", "sc", "cv0", "cv1", "J", "v20", "v21", "ss0", "ss1", "ws",
                                   "tc", "ts0", "ts1", "ts2", "ts3", "tw", "pv0", "pv1"])
        XD = Steps(sem("smp_dve"), ["pre0", "pre1", "kc0", "kc1", "cmx", "crc", "cp", "pre2", "pre3", "pj", "im", "sc1", "sc2",
                                    "eq", "tri", "r1", "gt", "r2", "rk", "mk", "cf", "pg", "vc0", "vc1", "sv", "sf", "smx",
                                    "wv", "wf", "wmx", "src", "sfa", "sP", "wrc", "wfa", "wP", "ts0", "ts1", "ov"])
        XA = Steps(sem("smp_act"), ["B0", "h0", "B1", "h1", "ce", "B2", "h2", "B3", "h3", "se", "we", "tc", "ts2", "ts3", "tw"])
        XQ = sem("qb_ready")
        win_in = sem("win_in")
        win_out = sem("win_out")
        smp_zero = sem("smp_zero")

        def load_pages(eng, cache, slot, r, b):
            for g in range(NPG):
                v = eng.value_load(ptab[0:1, bass.ds(r * 32 + (b * NPG + g), 1)], min_val=0, max_val=NPHYS - 1)
                eng.dma_start(slots[:, slot, g * 256:(g + 1) * 256],
                              A[cache][bass.ds(v, 1), :, :].rearrange("a p n -> (a p) n")).then_inc(slot_in[slot], 16)

        def pair_pages(eng, caches, slot, r, last, first, carry):
            for b in range(2):
                if not isinstance(r, int):
                    eng.wait_ge(XP.sem, XP.at(last[b], r - 1))
                    eng.sem_inc(carry, 1)
                load_pages(eng, caches[0], slot + b, r, b)
            for b in range(2):
                eng.wait_ge(XP.sem, XP.at(first[b], r))
                eng.sem_inc(carry, 1)
                load_pages(eng, caches[1], slot + b, r, b)

        def NSA_SP(sp, stream):
            stream("in1")
            sp.dma_start(ptab[:, :], A["page_table"]).then_inc(tab_in, 16)
            sp.wait_ge(tab_in, 16)
            pair_pages(sp, ("cmp_k", "slc_k"), 0, 0, ("ss0", "ss1"), ("ck0", "ck1"), turn)
            with sp.Fori(1, 4) as r:
                pair_pages(sp, ("cmp_k", "slc_k"), 0, r, ("ss0", "ss1"), ("ck0", "ck1"), turn)
            stream("out1")

        def NSA_PE(pe, product):
            pe.wait_ge(nsa_in, 48)
            for h in range(2):
                for k in range(KC):
                    mm = pe.matmul(ps[0:48, 4 + h, 0:HT], wg[:, k, :], x[:, k, h * HT:(h + 1) * HT], start=k == 0, stop=k == KC - 1)
            mm.then_inc(NP.sem, 1)
            pe.wait_ge(NA.sem, NA.at("sig"))
            for t in range(4):
                mm = pe.transpose(ps[:, 6, t * 48:t * 48 + 48], gate_t[:, t * 128:(t + 1) * 128], K["ident"][0:48, 0:48])
            mm.then_inc(NP.sem, 1)
            for b in range(3):
                mm = pe.matmul(ps[:, 7, b * 32:b * 32 + 32], K["head_of_row"][0:48, b * 128:(b + 1) * 128], gate_t[:, SEQ:T],
                               start=True, stop=True)
            mm.then_inc(NP.sem, 1)
            pe.wait_ge(freed[0], SB["out1"])
            pe.wait_ge(freed[1], SB["out1"])
            for t in range(4):
                for v, row in enumerate((VS, VW)):
                    for g in range(2):
                        c = (v * 2 + g) * 128
                        mm = pe.transpose(ps[:, t, c:c + 128], big[:, row + g, t * 128:(t + 1) * 128], K["ident"])
                mm.then_inc(NP.sem, 1)
            for v, row in enumerate((VS, VW)):
                for g in range(2):
                    c = (v * 2 + g) * 128
                    mm = pe.transpose(ps[0:32, 4, c:c + 128], big[:, row + g, SEQ:T], K["ident"])
            mm.then_inc(NP.sem, 1)
            for v in range(2):
                for t in range(16):
                    mm = pe.matmul(ps[:, 5, v:v + 1], w1[:, v, t * 128:(t + 1) * 128], K["pe"][:, v * 16 + t:v * 16 + t + 1],
                                   start=t == 0, stop=t == 15)
            mm.then_inc(NP.sem, 1)
            pe.wait_ge(ND.sem, ND.at("grow"))
            for v in range(2):
                if v == 0:
                    pe.wait_ge(ND.sem, ND.at("C"))
                else:
                    pe.wait_ge(NA.sem, NA.at("C"))
                    pe.wait_ge(ND.sem, ND.at("V1"))
                for part in range(2):
                    bank = (6, 0)[v] + part
                    for c in range(8):
                        mm = pe.matmul(ps[:, bank, 0:128], w1[:, v, (part * 8 + c) * 128:(part * 8 + c + 1) * 128],
                                       c_p[:, v, c, :, :].rearrange("p g n -> p (g n)"), start=c == 0, stop=c == 7)
                mm.then_inc(NP.sem, 1)
            pe.wait_ge(NA.sem, NA.at("hk"))
            hg = hid_p.rearrange("p (g h) n -> p g h n", g=2)
            for g2 in range(2):
                mm = pe.matmul(ps[64 * g2:64 * g2 + 64, 2, 0:62].rearrange("p (g n) -> p g n", g=2), w2[:, 0, :],
                               hg[:, :, g2, 0:31], start=True, stop=True)
            mm.then_inc(NP.sem, 1)
            pe.wait_ge(NA.sem, NA.at("hv"))
            for g in range(4):
                mm = pe.matmul(ps[0:31, 3, g * 64:(g + 1) * 64], hid_p[:, g, 0:31], w2[:, 1, :], start=True, stop=True)
            mm.then_inc(NP.sem, 1)
            pe.wait_ge(ND.sem, ND.at("vcc"))

            for gp in range(2):
                def s(R, u):
                    qt, g2 = u // 2, u % 2
                    p0 = slice(64 * g2, 64 * g2 + 64)
                    q = q_st[p0, qt * 128:qt * 128 + 128]
                    n = (qt + 1) * 128
                    if u == 0:
                        pe.wait_ge(TA.sem, TA.at("q", R))
                    if u >= 2:
                        pe.wait_ge(TA.sem, TA.at(f"e{u - 2}", R))
                    pe.matmul(ps[:, 2 * g2, 0:n], q, big[p0, KS + gp, 0:n], start=True, stop=True)
                    pe.matmul(ps[:, 2 * g2 + 1, 0:n], q, big[p0, KW + gp, 0:n], start=True, stop=True)
                    if u:
                        pe.wait_ge(TD.sem, TD.at(f"cm{u - 1}", R))
                    if u >= 2:
                        pe.wait_ge(TD.sem, TD.at(f"tb{u - 2}", R))
                    pe.matmul(ps[:, 4, g2 * 32:g2 * 32 + 31], q, kcc_p[p0, gp, 0:31], start=True, stop=True).then_inc(TP.sem, 1)

                def t(R, u):
                    qt, g2 = u // 2, u % 2
                    pe.wait_ge(TD.sem, TD.at(f"p{u}", R))
                    for kt in range(qt + 1):
                        pe.transpose(ps[:, 5, kt * 128:(kt + 1) * 128], prob[:, g2, kt * 128:(kt + 1) * 128], K["ident"])
                    for kt in range(qt + 1):
                        pe.transpose(ps[:, 6, kt * 128:(kt + 1) * 128], prob[:, g2, 512 + kt * 128:512 + (kt + 1) * 128], K["ident"])
                    if u < 7:
                        pe.wait_ge(TD.sem, TD.at(f"cm{u + 1}", R))
                    pe.transpose(ps[0:31, 4, 128:256], prob[:, g2, 1024:1055], K["ident"]).then_inc(TP.sem, 1)

                def o(R, u):
                    qt, g2 = u // 2, u % 2
                    out = ps[64 * g2:64 * g2 + 64, 7, qt * 128:(qt + 1) * 128]
                    vc = slice(gp * 128 + g2 * 64, gp * 128 + g2 * 64 + 64)
                    if u == 0 and not (isinstance(R, int) and R == 0):
                        pe.wait_ge(TA.sem, TA.at("ov", R - 1))
                    pe.wait_ge(TA.sem, TA.at(f"ta{u}", R))
                    pe.wait_ge(TD.sem, TD.at(f"tb{u}", R))
                    for kt in range(qt + 1):
                        pe.matmul(out, v_nat_p[:, 0, kt, vc], pt_p[:, kt, :], start=kt == 0, stop=False)
                    for kt in range(qt + 1):
                        pe.matmul(out, v_nat_p[:, 1, kt, vc], pt_p[:, 4 + kt, :], start=False, stop=False)
                    pe.matmul(out, vcc_p[0:31, vc], pt_p[0:31, 8, :], start=False, stop=True).then_inc(TP.sem, 1)

                def round_(R):
                    s(R, 0)
                    s(R, 1)
                    for u in U:
                        t(R, u)
                        if u < 6:
                            s(R, u + 2)
                        o(R, u)

                if gp == 0:
                    round_(0)
                with pe.Fori(1 - gp, 4) as j:
                    round_(j + gp * 4)

            def pair(r):
                prev = not (isinstance(r, int) and r == 0)

                def compress(v, b, part_slots):
                    sl = 2 * v + b
                    pe.wait_ge(slot_in[sl], 256 * (1 + 2 * r))
                    rows = slots[:, sl, :].rearrange("p (pg c g n) -> p pg c g n", pg=NPG, c=8, g=4)
                    for part in range(2):
                        dst = ps[:, 2 * b + part, :].rearrange("p (g pg n) -> p pg g n", g=4, pg=NPG)
                        for c in range(8):
                            mm = pe.matmul(dst, w1[:, v, (part * 8 + c) * 128:(part * 8 + c + 1) * 128], rows[:, :, c, :, :],
                                           start=c == 0, stop=c == 7)
                    mm.then_inc(XP.sem, 1)

                if not prev:
                    pe.wait_ge(smp_zero, 3)
                if prev:
                    pe.wait_ge(XD.sem, XD.at("ov", r - 1))
                    pe.wait_ge(XA.sem, XA.at("tw", r - 1))
                for b in range(2):
                    compress(0, b, None)
                for b in range(2):
                    pe.wait_ge(XA.sem, XA.at(f"h{b}", r))
                    hg = hid_s[b].rearrange("p (g h n) -> p g h n", g=2, h=2)
                    for g2 in range(2):
                        mm = pe.matmul(ps[64 * g2:64 * g2 + 64, 4, b * 256:b * 256 + 254].rearrange("p (g n) -> p g n", g=2),
                                       w2[:, 0, :], hg[:, :, g2, 0:NCMP], start=True, stop=True)
                    mm.then_inc(XP.sem, 1)
                pe.wait_ge(XQ, 1 + r)
                pe.wait_ge(XD.sem, XD.at("kc1", r))
                for b in range(2):
                    for g in range(2):
                        mm = pe.matmul(ps[64 * b:64 * b + 64, 6, 0:NCMP], qb[:, b, g, :], kcc[:, b, g, 0:NCMP], start=g == 0, stop=g == 1)
                mm.then_inc(XP.sem, 1)
                for b in range(2):
                    pe.wait_ge(XD.sem, XD.at(f"pre{b}", r))
                    compress(1, b, None)
                pe.wait_ge(XD.sem, XD.at("cp", r))
                pe.matmul(ps[:, 6, 128:128 + NCMP], K["heads_sum"], pc[:, 0:NCMP], start=True, stop=True).then_inc(XP.sem, 1)
                for b in range(2):
                    pe.wait_ge(XA.sem, XA.at(f"h{2 + b}", r))
                    for g in range(4):
                        mm = pe.matmul(ps[0:NCMP, 5, b * 256 + g * 64:b * 256 + g * 64 + 64], hid_s[b][:, g * 128:g * 128 + NCMP],
                                       w2[:, 1, :], start=True, stop=True)
                    mm.then_inc(XP.sem, 1)
                for b in range(2):
                    pe.wait_ge(slot_in[b], 256 * (2 + 2 * r))
                    if b == 0:
                        pe.wait_ge(XD.sem, XD.at("pre3", r))
                    rows = slots[:, b, :].rearrange("p (pg g n) -> p pg g n", pg=NPG, g=2)
                    p0 = slice(64 * b, 64 * b + 64)
                    for t in range(4):
                        for g in range(2):
                            pe.matmul(ps[p0, t, :].rearrange("p (pg n) -> p pg n", pg=4), qb[:, b, g, :],
                                      rows[:, 4 * t:4 * t + 4, g, :], start=g == 0, stop=g == 1)
                    for g in range(2):
                        mm = pe.matmul(ps[p0, 4, 0:32], qb[:, b, g, :], big[:, KS + g, SEQ:T], start=g == 0, stop=g == 1)
                    mm.then_inc(XP.sem, 1)
                pe.wait_ge(win_in, 96 * (1 + r))
                pe.wait_ge(XD.sem, XD.at("vc1", r))
                for b in range(2):
                    p0 = slice(64 * b, 64 * b + 64)
                    for g in range(2):
                        pe.matmul(ps[p0, 5, :], qb[:, b, g, :], win_k[:, b, g, :], start=g == 0, stop=g == 1)
                    for g in range(2):
                        mm = pe.matmul(ps[p0, 7, 256:288], qb[:, b, g, :], big[:, KW + g, SEQ:T], start=g == 0, stop=g == 1)
                mm.then_inc(XP.sem, 1)
                pe.wait_ge(XD.sem, XD.at("pg", r))
                pe.transpose(ps[0:NCMP, 6, 256:384], pc[:, 0:NCMP], K["ident"]).then_inc(XP.sem, 1)
                pe.wait_ge(XD.sem, XD.at("sP", r))
                for q in range(4):
                    for t in range(4):
                        k0 = (4 * q + t) * 128
                        mm = pe.transpose(ps[:, q, t * 128:(t + 1) * 128], sc_s[:, k0:k0 + 128], K["ident"])
                    if q == 3:
                        pe.wait_ge(XA.sem, XA.at("tc", r))
                        mm = pe.transpose(ps[0:32, 6, 384:512], sc_s[:, 2048:2080], K["ident"])
                    mm.then_inc(XP.sem, 1)
                pe.wait_ge(XD.sem, XD.at("wP", r))
                for t in range(4):
                    pe.transpose(ps[:, 5, t * 128:(t + 1) * 128], sc_w[:, t * 128:(t + 1) * 128], K["ident"])
                pe.transpose(ps[0:32, 4, 128:256], sc_w[:, 512:544], K["ident"]).then_inc(XP.sem, 1)
                pe.wait_ge(XD.sem, XD.at("ts1", r))
                pe.wait_ge(XA.sem, XA.at("tw", r))
                for b in range(2):
                    pe.wait_ge(slot_in[2 + b], 256 * (2 + 2 * r))
                    for g in range(2):
                        out = ps[:, 7, (b * 2 + g) * 32:(b * 2 + g) * 32 + 32]
                        rows = slice(64 * b + 32 * g, 64 * b + 32 * g + 32)
                        vc = slice(g * 128, g * 128 + 128)
                        pe.matmul(out, vcc[0:NCMP, b, vc], pt_c[0:NCMP, rows], start=True, stop=False)
                        for t in range(16):
                            pe.matmul(out, slots[:, 2 + b, t * 256 + g * 128:t * 256 + g * 128 + 128], pt_s[t][:, rows],
                                      start=False, stop=False)
                        pe.matmul(out, fresh_v[0:32, 0, vc], pt_fs[0:32, rows], start=False, stop=False)
                        for t in range(4):
                            wv = big[:, 12 + 2 * b + t // 2, (t % 2) * 256 + g * 128:(t % 2) * 256 + g * 128 + 128]
                            pe.matmul(out, wv, pt_w[t][:, rows], start=False, stop=False)
                        mm = pe.matmul(out, fresh_v[0:32, 1, vc], pt_fw[0:32, rows], start=False, stop=True)
                    mm.then_inc(XP.sem, 1)

            pair(0)
            with pe.Fori(1, 4) as r:
                pair(r)
            pe.wait_ge(XD.sem, XD.at("ov", 3))
            product("out1", lambda k: big[:, OR + k, :])

        def NSA_ACT(act, take):
            with act.Fori(0, 2) as i:
                take("in1", i, 0, 0.125)
                take("in1", i, 2, 0.125)
            with act.Fori(2, 5) as i:
                take("in1", i, 0)
                take("in1", i, 2)
            act.wait_ge(NP.sem, NP.at("gate"))
            act.activation(gate_t.rearrange("p (h t) -> p h t", h=2), ps[0:48, 4:6, 0:HT], ACT.Sigmoid).then_inc(NA.sem, 1)
            for t in (0, 2):
                act.wait_ge(NP.sem, NP.at(f"V{t}"))
                act.activation(v_nat_p[:, :, t, :], ps[:, t, :].rearrange("p (v n) -> p v n", v=2), ACT.Copy).then_inc(NA.sem, 1)
            act.wait_ge(NP.sem, NP.at("bias"))
            act.activation(cbias, ps[:, 5, 0:2], ACT.Copy).then_inc(NA.sem, 1)
            act.wait_ge(freed[1], SB["out1"])
            for g in range(4):
                for par in range(2):
                    src = big[64 * (g % 2):64 * (g % 2) + 64, KVR + 2 + g // 2, 0:SEQ].rearrange("p (n c r) -> p r c n", c=8, r=2)
                    op = act.activation(c_p[64 * par:64 * par + 64, 1, :, g, :], src[:, par, :, :], ACT.Copy)
            op.then_inc(NA.sem, 1)
            for v in range(2):
                act.wait_ge(NP.sem, NP.at(("k1", "v1")[v]))
                if v == 0:
                    act.wait_ge(NA.sem, NA.at("bias"))
                else:
                    act.wait_ge(ND.sem, ND.at("prek"))
                act.activation(bs_p, ps[:, (7, 1)[v], 0:128].rearrange("p (g n) -> p g n", g=4), ACT.Identity,
                               bias=cbias[:, v:v + 1]).then_inc(NA.sem, 1)
                act.wait_ge(ND.sem, ND.at(("prek", "prev")[v]))
                act.activation(hid_p[:, :, 0:31], hid_p[:, :, 0:31], ACT.Gelu_apprx_tanh).then_inc(NA.sem, 1)

            for gp in range(2):
                def e(R, u):
                    qt, g2 = u // 2, u % 2
                    n = (qt + 1) * 128
                    act.wait_ge(TD.sem, TD.at(f"my{u}", R))
                    if u >= 2:
                        act.wait_ge(TP.sem, TP.at(f"t{u - 2}", R))
                    for k in range(2):
                        act.activation(prob[:, g2, 512 * k:512 * k + n], ps[:, 2 * g2 + k, 0:n], ACT.Exp,
                                       bias=nmax[:, g2, k + 1:k + 2], accum_out=rsum[:, g2, k + 1:k + 2])
                    act.activation(prob[:, g2, 1024:1055], prob[:, g2, 1024:1055], ACT.Exp,
                                   bias=nmax[:, g2, 0:1], accum_out=rsum[:, g2, 0:1]).then_inc(TA.sem, 1)

                def ta(R, u):
                    qt = u // 2
                    act.wait_ge(TP.sem, TP.at(f"t{u}", R))
                    if u:
                        act.wait_ge(TP.sem, TP.at(f"o{u - 1}", R))
                    n = (qt + 1) * 128
                    act.activation(pt_p[:, 0:8, :].rearrange("p (k t) n -> p k (t n)", k=2)[:, :, 0:n], ps[:, 5:7, 0:n],
                                   ACT.Copy).then_inc(TA.sem, 1)

                def round_(R):
                    if not (isinstance(R, int) and R == 0):
                        act.wait_ge(TP.sem, TP.at("o7", R - 1))
                    act.activation(q_st.unsqueeze(1), big[:, bass.ds(R, 1), 0:SEQ], ACT.Copy).then_inc(TA.sem, 1)
                    e(R, 0)
                    e(R, 1)
                    for u in U:
                        ta(R, u)
                        if u < 6:
                            e(R, u + 2)
                    act.wait_ge(TP.sem, TP.at("o7", R))
                    act.activation(big[:, bass.ds(R + OR, 1), 0:SEQ], ps[:, 7, :].unsqueeze(1), ACT.Copy).then_inc(TA.sem, 1)

                if gp == 0:
                    act.wait_ge(ND.sem, ND.at("vcc"))
                    round_(0)
                with act.Fori(1 - gp, 4) as j:
                    round_(j + gp * 4)

            def pair(r):
                def first(c):
                    b = c % 2
                    act.wait_ge(XP.sem, XP.at(("ck0", "ck1", "cv0", "cv1")[c], r))
                    if c >= 2:
                        act.wait_ge(XD.sem, XD.at(f"pre{c - 2}", r))
                    act.activation(bs_s[b], ps[:, 2 * b + 1, :], ACT.Identity, bias=cbias[:, c // 2:c // 2 + 1]).then_inc(XA.sem, 1)
                    act.wait_ge(XD.sem, XD.at(f"pre{c}", r))
                    h = hid_s[b].rearrange("p (g n) -> p g n", g=4)[:, :, 0:NCMP]
                    act.activation(h, h, ACT.Gelu_apprx_tanh).then_inc(XA.sem, 1)
                first(0)
                first(1)
                act.wait_ge(XD.sem, XD.at("cmx", r))
                act.activation(pc[:, 0:NCMP], ps[:, 6, 0:NCMP], ACT.Exp, bias=s_nm[:, 0:1], accum_out=s_sum[:, 0:1]).then_inc(XA.sem, 1)
                first(2)
                first(3)
                act.wait_ge(XD.sem, XD.at("smx", r))
                act.activation(sc_s, sc_s, ACT.Exp, bias=s_nm[:, 1:2], accum_out=s_sum[:, 1:2]).then_inc(XA.sem, 1)
                act.wait_ge(XD.sem, XD.at("wmx", r))
                act.activation(sc_w, sc_w, ACT.Exp, bias=s_nm[:, 2:3], accum_out=s_sum[:, 2:3]).then_inc(XA.sem, 1)
                act.wait_ge(XP.sem, XP.at("tc", r))
                act.activation(pt_c[0:NCMP, :], ps[0:NCMP, 6, 256:384], ACT.Copy).then_inc(XA.sem, 1)
                act.wait_ge(XP.sem, XP.at("ts2", r))
                act.activation(big[:, 2, 0:512], ps[:, 2, :], ACT.Copy).then_inc(XA.sem, 1)
                act.wait_ge(XP.sem, XP.at("ts3", r))
                act.activation(big[:, 3, 0:512], ps[:, 3, :], ACT.Copy)
                act.activation(pt_fs[0:32, :], ps[0:32, 6, 384:512], ACT.Copy).then_inc(XA.sem, 1)
                act.wait_ge(XP.sem, XP.at("tw", r))
                act.activation(big[:, 5, 0:512], ps[:, 5, :], ACT.Copy)
                act.activation(pt_fw[0:32, :], ps[0:32, 4, 128:256], ACT.Copy).then_inc(XA.sem, 1)

            with act.Fori(0, 4) as r:
                pair(r)

        def NSA_DVE(ve, take):
            with ve.Fori(0, 2) as i:
                take("in1", i, 1, 0.125)
                take("in1", i, 3, 0.125)
            with ve.Fori(2, 5) as i:
                take("in1", i, 1)
                take("in1", i, 3)
            ve.wait_ge(freed[0], SB["out1"])
            for g in range(4):
                for par in range(2):
                    src = big[64 * (g % 2):64 * (g % 2) + 64, KVR + g // 2, 0:SEQ].rearrange("p (n c r) -> p r c n", c=8, r=2)
                    op = ve.tensor_copy(c_p[64 * par:64 * par + 64, 0, :, g, :], src[:, par, :, :])
            op.then_inc(ND.sem, 1)
            ve.wait_ge(NP.sem, NP.at("gT"))
            ve.tensor_copy(gtok, ps[:, 6, 0:192].rearrange("p (q b h) -> p q b h", q=4, b=3)).then_inc(ND.sem, 1)
            ve.wait_ge(NP.sem, NP.at("grow"))
            ve.tensor_tensor(grow_m.rearrange("p b w t -> p b (w t)"), ps[:, 7, 0:96].rearrange("p (b t) -> p b t", b=3),
                             K["token_of_row"].unsqueeze(1).to_broadcast([128, 3, 32]), ALU.mult).then_inc(ND.sem, 1)
            ve.wait_ge(ND.sem, ND.at("gm"))
            ve.tensor_reduce(growv, grow_m, AX.X, ALU.add).then_inc(ND.sem, 1)
            for t in (1, 3):
                ve.wait_ge(NP.sem, NP.at(f"V{t}"))
                ve.tensor_copy(v_nat_p[:, :, t, :], ps[:, t, :].rearrange("p (v n) -> p v n", v=2)).then_inc(ND.sem, 1)
            ve.wait_ge(NP.sem, NP.at("F"))
            ve.tensor_copy(fresh_v[0:32, :, :], ps[0:32, 4, :].rearrange("p (v n) -> p v n", v=2)).then_inc(ND.sem, 1)
            for v in range(2):
                if v:
                    ve.wait_ge(NP.sem, NP.at("k2"))
                ve.wait_ge(NA.sem, NA.at(("Bk", "Bv")[v]))
                ve.tensor_tensor(hid_p[:, :, 0:31], ps[:, (6, 0)[v], 0:128].rearrange("p (g n) -> p g n", g=4)[:, :, 0:31],
                                 bs_p[:, :, 1:32], ALU.add).then_inc(ND.sem, 1)
            ve.wait_ge(NP.sem, NP.at("k2"))
            ve.tensor_copy(kcc_p[:, :, 0:31], ps[:, 2, 0:62].rearrange("p (g n) -> p g n", g=2)).then_inc(ND.sem, 1)
            ve.wait_ge(NP.sem, NP.at("v2"))
            ve.tensor_copy(vcc_p[0:31, :], ps[0:31, 3, 0:256]).then_inc(ND.sem, 1)

            for gp in range(2):
                def a(R, u):
                    qt, g2 = u // 2, u % 2
                    n = (qt + 1) * 128
                    ve.wait_ge(TP.sem, TP.at(f"s{u}", R))
                    d = ps[:, 2 * g2:2 * g2 + 2, qt * 128:n]
                    ve.tensor_tensor(d, d, K["causal"].unsqueeze(1).to_broadcast([128, 2, 128]), ALU.add).then_inc(TD.sem, 1)
                    if u >= 2:
                        ve.wait_ge(TP.sem, TP.at(f"t{u - 2}", R))
                    ve.tensor_tensor(prob[:, g2, 1024:1055], ps[:, 4, g2 * 32:g2 * 32 + 31], K["cmp_mask"][:, qt * 32:qt * 32 + 31],
                                     ALU.add).then_inc(TD.sem, 1)
                    ve.wait_ge(TD.sem, TD.at(f"dm{u}", R))
                    ve.tensor_reduce(nmax[:, g2, 1:3], ps[:, 2 * g2:2 * g2 + 2, 0:n], AX.X, ALU.max, negate=True).then_inc(TD.sem, 1)
                    ve.wait_ge(TD.sem, TD.at(f"cm{u}", R))
                    ve.tensor_reduce(nmax[:, g2, 0:1], prob[:, g2, 1024:1055], AX.X, ALU.max, negate=True).then_inc(TD.sem, 1)

                def b(R, u):
                    qt, g2 = u // 2, u % 2
                    n = (qt + 1) * 128
                    j = R - gp * 4
                    ve.wait_ge(TA.sem, TA.at(f"e{u}", R))
                    ve.reciprocal(fac[:, g2, :], rsum[:, g2, :]).then_inc(TD.sem, 1)
                    ve.wait_ge(TD.sem, TD.at(f"rc{u}", R))
                    ve.tensor_tensor(fac[:, g2, :].unsqueeze(2), fac[:, g2, :].unsqueeze(2),
                                     gtok[:, qt, :, bass.ds(gp * 8 + j * 2 + g2, 1)], ALU.mult).then_inc(TD.sem, 1)
                    ve.wait_ge(TD.sem, TD.at(f"fa{u}", R))
                    for k in range(2):
                        pr = prob[:, g2, 512 * k:512 * k + n]
                        ve.tensor_scalar(pr, pr, fac[:, g2, k + 1:k + 2], None, ALU.mult)
                    pr = prob[:, g2, 1024:1055]
                    ve.scalar_tensor_tensor(out=pr, in0=pr, scalar=fac[:, g2, 0:1], in1=K["cmp_valid"][:, qt * 32:qt * 32 + 31],
                                            op0=ALU.mult, op1=ALU.mult).then_inc(TD.sem, 1)

                def c(R, u):
                    ve.wait_ge(TP.sem, TP.at(f"t{u}", R))
                    if u:
                        ve.wait_ge(TP.sem, TP.at(f"o{u - 1}", R))
                    ve.tensor_copy(pt_p[0:31, 8, :], ps[0:31, 4, 128:256]).then_inc(TD.sem, 1)

                def round_(R):
                    a(R, 0)
                    a(R, 1)
                    b(R, 0)
                    for u in U:
                        c(R, u)
                        if u < 7:
                            b(R, u + 1)
                        if u < 6:
                            a(R, u + 2)

                with ve.Fori(0, 4) as j:
                    round_(j + gp * 4)

            def pair(r):
                def pre(c):
                    b = c % 2
                    ve.wait_ge(XA.sem, XA.at(f"B{c}", r))
                    if c >= 2:
                        ve.wait_ge(XP.sem, XP.at(f"k2{b}", r))
                    ve.tensor_tensor(hid_s[b].rearrange("p (g n) -> p g n", g=4)[:, :, 0:NCMP],
                                     ps[:, 2 * b, :].rearrange("p (g n) -> p g n", g=4)[:, :, 0:NCMP],
                                     bs_s[b].rearrange("p (g n) -> p g n", g=4)[:, :, 1:NC], ALU.add).then_inc(XD.sem, 1)

                def step(name, op):
                    op.then_inc(XD.sem, 1)
                    ve.wait_ge(XD.sem, XD.at(name, r))

                pre(0)
                pre(1)
                for b in range(2):
                    ve.wait_ge(XP.sem, XP.at("k21", r))
                    ve.tensor_copy(kcc[:, b, :, 0:NCMP], ps[:, 4, b * 256:b * 256 + 254].rearrange("p (g n) -> p g n", g=2)).then_inc(XD.sem, 1)
                ve.wait_ge(XP.sem, XP.at("sc", r))
                ve.tensor_reduce(s_nm[:, 0:1], ps[:, 6, 0:NCMP], AX.X, ALU.max, negate=True).then_inc(XD.sem, 1)
                ve.wait_ge(XA.sem, XA.at("ce", r))
                step("crc", ve.reciprocal(s_fac[:, 0:1], s_sum[:, 0:1]))
                ve.tensor_scalar(pc[:, 0:NCMP], pc[:, 0:NCMP], s_fac[:, 0:1], None, ALU.mult).then_inc(XD.sem, 1)
                pre(2)
                pre(3)
                ve.wait_ge(XP.sem, XP.at("J", r))
                step("pj", ve.tensor_copy(pj[:, 1:1 + NCMP], ps[:, 6, 128:128 + NCMP]))
                step("im", ve.tensor_reduce(score, pj[:, 0:132].rearrange("p (m n) -> p m n", n=4), AX.X, ALU.add))
                step("sc1", ve.tensor_tensor(score, score, pj[:, 4:136].rearrange("p (m n) -> p m n", n=4)[:, :, 0], ALU.add))
                step("sc2", ve.tensor_tensor(score, score, K["bonus"], ALU.add))
                other = score.unsqueeze(1).to_broadcast([128, NSLC, NSLC])
                own = score.unsqueeze(2).to_broadcast([128, NSLC, NSLC])
                step("eq", ve.tensor_tensor(cmpx, other, own, ALU.is_equal))
                step("tri", ve.tensor_tensor(cmpx, cmpx, K["earlier"].rearrange("p (m n) -> p m n", m=NSLC), ALU.mult))
                step("r1", ve.tensor_reduce(rank_a, cmpx, AX.X, ALU.add))
                step("gt", ve.tensor_tensor(cmpx, other, own, ALU.is_gt))
                step("r2", ve.tensor_reduce(rank_b, cmpx, AX.X, ALU.add))
                step("rk", ve.tensor_tensor(rank_a, rank_a, rank_b, ALU.add))
                step("mk", ve.tensor_scalar(rank_a, rank_a, TOPN - 0.5, NEG, ALU.is_gt, ALU.mult))
                step("cf", ve.tensor_copy(s_fac[:, 0:1].unsqueeze(1), growv[:, 0:1, bass.ds(r, 1)]))
                ve.tensor_scalar(pc[:, 0:NCMP], pc[:, 0:NCMP], s_fac[:, 0:1], None, ALU.mult).then_inc(XD.sem, 1)
                for b in range(2):
                    ve.wait_ge(XP.sem, XP.at("v21", r))
                    ve.tensor_copy(vcc[0:NCMP, b, :], ps[0:NCMP, 5, b * 256:b * 256 + 256]).then_inc(XD.sem, 1)
                ve.wait_ge(XP.sem, XP.at("ss1", r))
                ve.tensor_tensor(sc_s[:, 0:2048].rearrange("p (m n) -> p m n", n=64),
                                 ps[:, 0:4, :].rearrange("p k (m n) -> p (k m) n", n=64),
                                 rank_a[:, 0:32].unsqueeze(2).to_broadcast([128, 32, 64]), ALU.add).then_inc(XD.sem, 1)
                fm = K["fresh_mask"].rearrange("p (w t) -> p w t", w=4)[:, bass.ds(r, 1), :]
                step("sf", ve.tensor_tensor(sc_s[:, 2048:2080].unsqueeze(1), ps[:, 4, 0:32].unsqueeze(1), fm, ALU.add))
                ve.tensor_reduce(s_nm[:, 1:2], sc_s, AX.X, ALU.max, negate=True).then_inc(XD.sem, 1)
                ve.wait_ge(XP.sem, XP.at("ws", r))
                ve.tensor_tensor(sc_w[:, 0:32], ps[:, 5, 0:32], K["win_mask"], ALU.add)
                ve.tensor_copy(sc_w[:, 32:512], ps[:, 5, 32:512]).then_inc(XD.sem, 1)
                step("wf", ve.tensor_tensor(sc_w[:, 512:544].unsqueeze(1), ps[:, 7, 256:288].unsqueeze(1), fm, ALU.add))
                ve.tensor_reduce(s_nm[:, 2:3], sc_w, AX.X, ALU.max, negate=True).then_inc(XD.sem, 1)
                for k, (name, buf) in enumerate((("s", sc_s), ("w", sc_w))):
                    f = s_fac[:, 1 + k:2 + k]
                    ve.wait_ge(XA.sem, XA.at(name + "e", r))
                    step(name + "rc", ve.reciprocal(f, s_sum[:, 1 + k:2 + k]))
                    step(name + "fa", ve.tensor_tensor(f.unsqueeze(1), f.unsqueeze(1), growv[:, 1 + k:2 + k, bass.ds(r, 1)], ALU.mult))
                    ve.tensor_scalar(buf, buf, f, None, ALU.mult).then_inc(XD.sem, 1)
                for q in range(2):
                    ve.wait_ge(XP.sem, XP.at(f"ts{q}", r))
                    ve.tensor_copy(big[:, q, 0:512], ps[:, q, :]).then_inc(XD.sem, 1)
                ve.wait_ge(XP.sem, XP.at("pv1", r))
                src = ps[:, 7, 0:128].rearrange("p (b g h j t) -> p b g h j t", b=2, g=2, h=2, j=4)
                for g in range(2):
                    for h in range(2):
                        dst = big[64 * h:64 * h + 64, OR + 4 * g:OR + 4 * g + 4, bass.ds(SEQ + r * 8, 8)]
                        op = ve.tensor_copy(dst.rearrange("p j (b t) -> p b j t", b=2), src[64 * h:64 * h + 64, :, g, h, :, :])
                op.then_inc(XD.sem, 1)

            with ve.Fori(0, 4) as r:
                pair(r)

        def NSA_POOL(po, stores, hist_store):
            po.wait_ge(freed[0], SB["out1"])
            po.wait_ge(freed[1], SB["out1"])
            po.dma_start(A["o_kv"], big[:, KVR:KVR + 12, :]).then_inc(kv_store, 16)
            for b in range(NB):
                po.dma_start(A["o_win_k"][b, :, :, W - NT:W], big[:, KW:KW + 2, SEQ + b * NT:SEQ + b * NT + NT]).then_inc(kv_store, 16)
            po.wait_ge(ND.sem, ND.at("F"))
            for b in range(NB):
                po.dma_start(A["o_win_v"][b, W - NT:W, :], fresh_v[b * NT:b * NT + NT, 1, :]).then_inc(kv_store, 16)
            po.wait_ge(kv_store, 16 * (1 + 2 * NB))
            po.wait_ge(TA.sem, TA.at("ov", 7))
            po.wait_ge(tab_in, 16)
            po.memset(qb, 0.0).then_inc(smp_zero, 1)
            po.memset(pj, 0.0).then_inc(smp_zero, 1)
            po.wait_ge(smp_zero, 2)
            po.sem_inc(smp_zero, 1)

            def pair(r):
                prev = not (isinstance(r, int) and r == 0)
                if prev:
                    po.wait_ge(XP.sem, XP.at("pv1", r - 1))
                    po.wait_ge(win_out, 128 * r)
                for g in range(2):
                    for h in range(2):
                        src = big[64 * h:64 * h + 64, 4 * g:4 * g + 4, bass.ds(SEQ + r * 8, 8)].rearrange("p j (b t) -> p b j t", b=2)
                        c0 = g * 32 + h * 16
                        op = po.tensor_copy(qb[64 * h:64 * h + 64, :, g, c0:c0 + 16].rearrange("p b (j t) -> p b j t", j=4), src)
                op.then_inc(XQ, 1)
                for b in range(2):
                    load_pages(po, "cmp_v", 2 + b, r, b)
                for b in range(2):
                    po.dma_start(win_k[:, b, :, :], A["win_k"][bass.ds(r * 2 + b, 1), :, :, :].rearrange("a p g n -> (a p) g n")).then_inc(win_in, 16)
                    for q in range(2):
                        po.dma_start(big[:, 12 + 2 * b + q, 0:512].rearrange("p (t n) -> p t n", t=2),
                                     A["win_v"][bass.ds(r * 2 + b, 1), 2 * q:2 * q + 2, :, :].rearrange("a t p n -> p (a t) n")).then_inc(win_in, 16)
                for b in range(2):
                    po.wait_ge(XP.sem, XP.at(f"cv{b}", r))
                    po.sem_inc(turn_v, 1)
                    load_pages(po, "slc_v", 2 + b, r, b)
                po.wait_ge(win_in, 96 * (r + 1))
                po.sem_inc(turn_v, 1)
                for b in range(2):
                    po.dma_start(A["o_win_k"][bass.ds(r * 2 + b, 1), :, :, 0:W - NT].rearrange("a p g n -> (a p) g n"),
                                 win_k[:, b, :, NT:W]).then_inc(win_out, 16)
                    ov = A["o_win_v"][bass.ds(r * 2 + b, 1), :, :]
                    wv = big[:, 12 + 2 * b:14 + 2 * b, 0:512]
                    po.dma_start(ov[:, 0:124, :].rearrange("a p n -> (a p) n"), wv[NT:128, 0, 0:256]).then_inc(win_out, 16)
                    po.dma_start(ov[:, 124:252, :].rearrange("a p n -> (a p) n"), wv[:, 0, 256:512]).then_inc(win_out, 16)
                    po.dma_start(ov[:, 252:508, :].rearrange("a (t p) n -> p (a t) n", t=2),
                                 wv[:, 1, :].rearrange("p (t n) -> p t n", t=2)).then_inc(win_out, 16)

            pair(0)
            with po.Fori(1, 4) as r:
                pair(r)
            po.wait_ge(win_out, 128 * 4)
            po.wait_ge(XQ, 4)
            return stores
        block = ctx.enter_context(nc.Block())

        @block.sync
        def _(sp):
            sp.dma_start(x[:, :, :], A["xT"]).then_inc(x_in, 16)

            def piece(n, s, src, size):
                if not (isinstance(n, int) and n < 4):
                    sp.wait_ge(pieces, n - 3)
                sp.dma_start(ring[:, s, 0:size], src).then_inc(w_in[s], 16)

            def stream(name, first=False):
                w = A["w_" + name]
                count = dict((g[0], g[1]) for g in GEMMS)[name]
                if name.startswith("down"):
                    with sp.Fori(0, 2) as i:
                        for q in range(12):
                            m, part = q // 3, q % 3
                            size = (8, 8, 6)[part] * 128
                            piece(PB[name] + i * 12 + q, q % 4,
                                  w[bass.ds(i * 4 + m, 1), :, part * 1024:part * 1024 + size].rearrange("m p n -> (m p) n"), size)
                    return
                start = 0
                if first:
                    for s in range(4):
                        piece(s, s, w[s], 1024)
                    start = 1
                with sp.Fori(start, count // 4) as i:
                    for s in range(4):
                        piece(PB[name] + i * 4 + s, s, w[bass.ds(i * 4 + s, 1), :, :].rearrange("m p n -> (m p) n"), 1024)

            stream("in0", True)
            for name in ("out0", "up0", "down0"):
                stream(name)
            NSA_SP(sp, stream)
            for name in ("up1", "down1"):
                stream(name)

        @block.tensor
        def _(pe):
            def stripe(psum_set, slot, ks, rhs, start, stop):
                for k in range(ks):
                    for h in range(2):
                        mm = pe.matmul(ps[:, 2 * psum_set + h, 0:HT], ring[:, slot, k * 128:(k + 1) * 128],
                                       rhs(k)[:, h * HT:(h + 1) * HT], start=start and k == 0, stop=stop and k == ks - 1)
                return mm

            def product(name, rhs, first=False):
                count = dict((g[0], g[1]) for g in GEMMS)[name]
                if name.startswith("down"):
                    with pe.Fori(0, 2) as i:
                        for q in range(12):
                            m, part = q // 3, q % 3
                            pe.wait_ge(w_in[q % 4], 16 * (PB[name] // 4 + i * 3 + q // 4 + 1))
                            if part == 0:
                                pe.wait_ge(freed[m % 2], SB[name] + i * 2 + m // 2)
                            stripe(m % 2, q % 4, (8, 8, 6)[part], lambda k: rhs(part * 8 + k),
                                   part == 0, part == 2).then_inc(pieces, 1)
                    return

                def four(i, peeled):
                    for s in range(4):
                        pe.wait_ge(w_in[s], 16 * (PB[name] // 4 + 1 + i))
                        if not peeled or s >= 2:
                            pe.wait_ge(freed[s % 2], SB[name] + i * 2 + s // 2)
                        stripe(s % 2, s, KC, rhs, True, True).then_inc(pieces, 1)

                if first:
                    four(0, True)
                with pe.Fori(1 if first else 0, count // 4) as i:
                    four(i, False)

            def norm_sums(r):
                pe.wait_ge(ln_sum, 8 * (r + 1))
                for h in range(2):
                    mm = pe.matmul(ps[:, 4 + h, 0:HT], K["mean_d"], ln_row(r, 0)[:, h * HT:(h + 1) * HT], start=True, stop=True)
                mm.then_inc(ln_mean, 1)
                for m in range(KC):
                    pe.wait_ge(ln_sq, 8 * r + m + 1)
                    for h in range(2):
                        mm = pe.matmul(ps[:, 6 + h, 0:HT], K["mean_d"], big[:, m, h * HT:(h + 1) * HT],
                                       start=m == 0, stop=m == KC - 1)
                mm.then_inc(ln_var, 1)

            pe.wait_ge(x_in, 16)
            product("in0", lambda k: x[:, k, :], True)

            pe.wait_ge(early_in, 16)
            pe.wait_ge(freed[0], 14)
            pe.wait_ge(freed[1], 14)
            for n in range(8):
                if n >= 2:
                    pe.wait_ge(RD.sem, RD.at("sin", n - 2))
                for h in range(2):
                    mm = pe.matmul(ps[:, 4 + 2 * (n % 2) + h, 0:HT], K["swap"], big[:, n, h * HT:(h + 1) * HT],
                                   start=True, stop=True)
                mm.then_inc(rope_pe, 1)

            pe.wait_ge(consts_in, 32)
            pe.wait_ge(RD.sem, RD.at("add", 7))
            for c in range(4):
                tok = slice(c * 128, c * 128 + 128)
                if c:
                    pe.wait_ge(RV.sem, RV.at("kn", c - 1))
                for h in range(RH):
                    mm = pe.transpose(ps[:, 4, h * 128:(h + 1) * 128], big[:, KZ + h, tok], K["ident"])
                mm.then_inc(RP.sem, 1)
                if c:
                    pe.wait_ge(RA.sem, RA.at("vn", c - 1))
                for h in range(RH):
                    mm = pe.transpose(ps[:, 5, h * 128:(h + 1) * 128], big[:, VZ + h, tok], K["ident"])
                mm.then_inc(RP.sem, 1)
                if c:
                    pe.wait_ge(RV.sem, RV.at("st", c - 1))
                for h in range(RH):
                    mm = pe.matmul(ps[:, 6, h * 128:(h + 1) * 128], big[:, KZ + h, tok], big[:, QZ + h, tok],
                                   start=True, stop=True)
                mm.then_inc(RP.sem, 1)
                pe.wait_ge(RV.sem, RV.at("qd", c))
                pe.wait_ge(RA.sem, RA.at("vn", c))
                if c:
                    pe.wait_ge(RA.sem, RA.at("o", c - 1))
                    pe.wait_ge(RV.sem, RV.at("state", c - 1))
                for h in range(RH):
                    hs = slice(h * 128, h * 128 + 128)
                    mm = pe.matmul(ps[:, 7, hs], v_nat[:, hs], s_dec[:, hs], start=True, stop=c == 0)
                    if c:
                        mm = pe.matmul(ps[:, 7, hs], state[:, hs], q_dec[:, hs], start=False, stop=True)
                mm.then_inc(RP.sem, 1)
                for h in range(RH):
                    hs = slice(h * 128, h * 128 + 128)
                    mm = pe.matmul(ps[:, 0, hs], k_nat[:, hs], v_nat[:, hs], start=True, stop=True)
                mm.then_inc(RP.sem, 1)

            tok = slice(SEQ, T)
            pe.wait_ge(RV.sem, RV.at("state", 3))
            pe.wait_ge(RA.sem, RA.at("o", 3))
            for h in range(RH):
                mm = pe.transpose(ps[0:32, 4, h * 128:(h + 1) * 128], big[:, KZ + h, tok], K["ident"])
            mm.then_inc(SP_.sem, 1)
            for h in range(RH):
                mm = pe.transpose(ps[0:32, 5, h * 128:(h + 1) * 128], big[:, VZ + h, tok], K["ident"])
            mm.then_inc(SP_.sem, 1)
            for h in range(RH):
                mm = pe.matmul(ps[0:32, 6, h * 32:(h + 1) * 32], big[:, KZ + h, tok], big[:, QZ + h, tok],
                               start=True, stop=True)
            mm.then_inc(SP_.sem, 1)
            pe.wait_ge(ret_in, 16)
            pe.wait_ge(SV.sem, SV.at("qd"))
            pe.wait_ge(SA.sem, SA.at("vn"))
            for h in range(RH):
                hs = slice(h * 128, h * 128 + 128)
                pe.matmul(ps[:, 7, h * 32:(h + 1) * 32], v_nat[0:32, hs], s_dec[0:32, h * 32:h * 32 + 32],
                          start=True, stop=True, skip_group_check=True)
                for b in range(NB):
                    cs = slice(h * 32 + b * NT, h * 32 + b * NT + NT)
                    mm = pe.matmul(ps[:, 7, cs], ret_states[:, b, h, :], q_dec[:, cs], start=False, stop=True,
                                   skip_group_check=True)
            mm.then_inc(SP_.sem, 1)
            for h in range(RH):
                pe.wait_ge(SV.sem, SV.at("vb") + h)
                for u in range(2):
                    n = 2 * h + u
                    if n >= 2:
                        pe.wait_ge(st_s, n - 1)
                    mm = pe.matmul(ps[:, n % 2, :], k_nat[0:32, h * 128:(h + 1) * 128], v_blk[0:32, u * 512:(u + 1) * 512],
                                   start=True, stop=True).then_inc(kv_s, 1)

            pe.wait_ge(SA.sem, SA.at("o"))
            for h in range(RH):
                s = 4
                if h:
                    pe.wait_ge(GV.sem, GV.at("cen", h - 1))
                for u in range(2):
                    mm = pe.matmul(ps[:, s + u, 0:HT], K["mean_h"], big[:, QZ + h, u * HT:(u + 1) * HT], start=True, stop=True)
                mm.then_inc(GP.sem, 1)
                pe.wait_ge(GA.sem, GA.at("sq", h))
                for u in range(2):
                    mm = pe.matmul(ps[:, s + 2 + u, 0:HT], K["mean_h"], gn_sq[:, u * HT:(u + 1) * HT], start=True, stop=True)
                mm.then_inc(GP.sem, 1)

            pe.wait_ge(yb_done, RH)
            pe.wait_ge(ya.sem, ya.at("ys", 3))
            product("out0", lambda k: big[:, HZ + k, :] if k < 4 else big[:, QZ + k - 4, :])
            norm_sums(0)
            for layer in range(2):
                pe.wait_ge(ln_x, 8 * (2 * layer + 1))
                product(f"up{layer}", lambda k: x[:, k, :])
                pe.wait_ge(freed[1], SB[f"down{layer}"])
                product(f"down{layer}", lambda k: big[:, k, :])
                norm_sums(2 * layer + 1)
                if layer == 0:
                    pe.wait_ge(ln_x, 16)
                    product("in1", lambda k: x[:, k, :])
                    NSA_PE(pe, product)
                    norm_sums(2)

        @block.scalar
        def _(act):
            act.dma_start(keep_all, A["keep"]).then_inc(consts_in, 16)
            act.dma_start(vec_all, A["vecs"]).then_inc(consts_in, 16)
            act.dma_start(early_all, A["early"]).then_inc(early_in, 16)
            act.dma_start(ret_states, A["state_ret"]).then_inc(ret_in, 16)
            act.dma_start(sconv_hist, A["state_sconv"]).then_inc(hist_in, 16)
            act.dma_start(wg, A["w_gate"]).then_inc(nsa_in, 16)
            act.dma_start(w1, A["w1"]).then_inc(nsa_in, 16)
            act.dma_start(w2, A["w2"]).then_inc(nsa_in, 16)

            def take_even(name, i, s, scale=1.0):
                act.wait_ge(pieces, PB[name] + i * 4 + (s + 1))
                act.activation(half2(big[:, bass.ds(i * 4 + s, 1), :]), pset(0), ACT.Copy, scale=scale).then_inc(freed[0], 1)

            def half2(v):
                return v.rearrange("p a (h t) -> p (a h) t", h=2)

            with act.Fori(0, 7) as i:
                take_even("in0", i, 0)
                take_even("in0", i, 2)
            for c in range(4):
                tok = slice(c * 128, c * 128 + 128)
                act.wait_ge(RP.sem, RP.at("vT", c))
                if c:
                    act.wait_ge(RP.sem, RP.at("kv", c - 1))
                act.activation(v_nat[:, :], ps[:, 5, :], ACT.Copy).then_inc(RA.sem, 1)
                act.wait_ge(RP.sem, RP.at("o", c))
                act.activation(big[:, QZ:QZ + 4, tok], ps[:, 7, :].rearrange("p (h n) -> p h n", h=4), ACT.Copy).then_inc(RA.sem, 1)
            act.wait_ge(SP_.sem, SP_.at("vT"))
            act.wait_ge(RP.sem, RP.at("kv", 3))
            act.activation(v_nat[0:32, :], ps[0:32, 5, :], ACT.Copy).then_inc(SA.sem, 1)
            act.wait_ge(SP_.sem, SP_.at("o"))
            act.activation(big[:, QZ:QZ + 4, SEQ:T], ps[:, 7, 0:128].rearrange("p (h n) -> p h n", h=4), ACT.Copy).then_inc(SA.sem, 1)
            act.wait_ge(freed[1], 14)
            act.wait_ge(RP.sem, RP.at("kv", 3))
            act.activation(big[:, GZ:GZ + 4, :], big[:, GZ:GZ + 4, :], ACT.Silu).then_inc(gn_gate, 1)
            act.wait_ge(pool_set, 1)
            for h in range(RH):
                act.wait_ge(GV.sem, GV.at("cen", h))
                if h:
                    act.wait_ge(GP.sem, GP.at("var", h - 1))
                act.activation(gn_sq[:, :], big[:, QZ + h, :], ACT.Square).then_inc(GA.sem, 1)
                act.wait_ge(GP.sem, GP.at("var", h))
                if h:
                    act.wait_ge(GV.sem, GV.at("nrm", h - 1))
                act.activation(half(gn_sd[:, :]), ps[:, 6:8, 0:HT], ACT.Sqrt, bias=eps[:, 0:1]).then_inc(GA.sem, 1)

            def norm(r):
                for m in range(KC):
                    act.wait_ge(ln_cen, 8 * r + m + 1)
                    act.activation(big[:, m, :], y[:, m, :], ACT.Square).then_inc(ln_sq, 1)
                act.wait_ge(ln_var, r + 1)
                act.activation(half(ln_row(r, 1)), ps[:, 6:8, 0:HT], ACT.Sqrt, bias=eps[:, 0:1]).then_inc(ln_std, 1)
                for m in range(KC):
                    act.wait_ge(ln_nrm, 8 * r + m + 1)
                    act.activation(x[:, m, :], y[:, m, :], ACT.Identity, scale=K["ln_g"][:, 8 * r + m:8 * r + m + 1],
                                   bias=K["ln_b"][:, 8 * r + m:8 * r + m + 1]).then_inc(ln_x, 1)

            def ffn(layer):
                name = f"up{layer}"
                base = layer * FC

                def row(jb, u, peeled):
                    j = jb * 2 + u
                    act.wait_ge(pieces, PB[name] + jb * 4 + (2 * u + 1))
                    if not peeled:
                        act.wait_ge(fd.sem, fd.at("c2", j + base - 2))
                        act.wait_ge(fp.sem, fp.at("out", j + base - 2))
                    act.activation(ffn_a[:, u, 2:2 + HT], ps[:, 0, 0:HT], ACT.Copy)
                    act.activation(ffn_a[:, u, 2 + HT:SO], ps[:, 1, 0:SEQ - HT], ACT.Copy)
                    act.activation(ffn_a[:, u, SO:CW].rearrange("p (b w) -> p b w", b=NB)[:, :, 2:6],
                                   ps[:, 1, SEQ - HT:HT].rearrange("p (b w) -> p b w", b=NB), ACT.Copy).then_inc(freed[0], 1)

                def gelu(jb, u, peeled):
                    j = jb * 2 + u
                    act.wait_ge(fd.sem, fd.at("c2", j + base))
                    if not peeled:
                        act.wait_ge(freed[1], SB[name] + j - 1)
                    act.activation(ffn_g[:, u, 0:SEQ], ffn_c[:, u, 0:SEQ], ACT.Gelu_apprx_tanh)
                    act.activation(ffn_g[:, u, SEQ:T].rearrange("p (b w) -> p b w", b=NB),
                                   conv_sample(ffn_c[:, u, :]),
                                   ACT.Gelu_apprx_tanh).then_inc(fa.sem, 1)

                row(0, 0, True)
                gelu(0, 0, True)
                row(0, 1, True)
                gelu(0, 1, True)
                with act.Fori(1, FC // 2) as jb:
                    row(jb, 0, False)
                    gelu(jb, 0, False)
                    row(jb, 1, False)
                    gelu(jb, 1, False)

            norm(0)
            ffn(0)
            norm(1)
            NSA_ACT(act, take_even)
            norm(2)
            ffn(1)
            norm(3)
            act.wait_ge(ln_x, 32)
            act.dma_start(A["o_x"], x[:, :, :]).then_inc(out_done, 16)
            act.wait_ge(out_done, 16)

        @block.vector
        def _(ve):
            def take_odd(name, i, s, scale=None):
                ve.wait_ge(pieces, PB[name] + i * 4 + (s + 1))
                dst = big[:, bass.ds(i * 4 + s, 1), :].rearrange("p a (h t) -> p (a h) t", h=2)
                if scale is None:
                    ve.tensor_copy(dst, pset(1)).then_inc(freed[1], 1)
                else:
                    ve.tensor_scalar(dst, pset(1), scale, None, ALU.mult).then_inc(freed[1], 1)

            with ve.Fori(0, 7) as i:
                take_odd("in0", i, 1)
                take_odd("in0", i, 3)
            ve.wait_ge(early_in, 16)
            ve.wait_ge(freed[0], 14)
            for n in range(8):
                ve.wait_ge(rope_pe, n + 1)
                if n:
                    ve.wait_ge(RD.sem, RD.at("add", n - 1))
                ve.tensor_tensor(half(rope_t), ps[:, 4 + 2 * (n % 2):6 + 2 * (n % 2), 0:HT], half(K["rope_sin"]),
                                 ALU.mult).then_inc(RD.sem, 1)
                ve.tensor_tensor(big[:, n, :], big[:, n, :], K["rope_cos"], ALU.mult).then_inc(RD.sem, 1)
                ve.wait_ge(RD.sem, RD.at("cos", n))
                ve.tensor_tensor(big[:, n, :], big[:, n, :], rope_t, ALU.add).then_inc(RD.sem, 1)
            ve.wait_ge(RD.sem, RD.at("add", 7))
            gam = np.exp(128 * np.log1p(-np.exp2(-5.0 - np.arange(RH))))
            gam4 = np.exp(NT * np.log1p(-np.exp2(-5.0 - np.arange(RH))))

            def by_head(v, n=128):
                return v.rearrange("p (h n) -> p h n", h=RH)

            for c in range(4):
                tok = slice(c * 128, c * 128 + 128)
                ve.wait_ge(RP.sem, RP.at("kT", c))
                if c:
                    ve.wait_ge(RP.sem, RP.at("kv", c - 1))
                ve.tensor_tensor(by_head(k_nat), by_head(ps[:, 4, :]),
                                 K["kdec"].unsqueeze(2).to_broadcast([128, RH, 128]), ALU.mult).then_inc(RV.sem, 1)
                ve.wait_ge(RP.sem, RP.at("sc", c))
                ve.tensor_tensor(s_dec, ps[:, 6, :], K["decay"], ALU.mult).then_inc(RV.sem, 1)
                ve.tensor_tensor(by_head(q_dec), big[:, QZ:QZ + 4, tok], by_head(K["qdec"]), ALU.mult).then_inc(RV.sem, 1)
                ve.wait_ge(RP.sem, RP.at("kv", c))
                if c == 0:
                    ve.tensor_copy(state, ps[:, 0, :]).then_inc(RV.sem, 1)
                else:
                    ve.wait_ge(RV.sem, RV.at("state", c - 1))
                    for h in range(RH):
                        hs = slice(h * 128, h * 128 + 128)
                        op = ve.scalar_tensor_tensor(out=state[:, hs], in0=state[:, hs], scalar=float(gam[h]),
                                                     in1=ps[:, 0, hs], op0=ALU.mult, op1=ALU.add)
                    op.then_inc(RV.sem, 1)
            ve.wait_ge(SP_.sem, SP_.at("kT"))
            ve.tensor_tensor(k_nat[0:32, :].rearrange("p (h n) -> p h n", h=RH), ps[0:32, 4, :].rearrange("p (h n) -> p h n", h=RH),
                             K["kdec_s"][0:32, :].unsqueeze(2).to_broadcast([32, RH, 128]), ALU.mult).then_inc(SV.sem, 1)
            ve.wait_ge(SP_.sem, SP_.at("sc"))
            ve.tensor_tensor(s_dec[0:32, 0:128], ps[0:32, 6, 0:128], K["decay_s"][0:32, :], ALU.mult).then_inc(SV.sem, 1)
            ve.tensor_tensor(q_dec[:, 0:128].rearrange("p (h n) -> p h n", h=RH), big[:, QZ:QZ + 4, SEQ:T],
                             K["qdec_s"].rearrange("p (h n) -> p h n", h=RH), ALU.mult).then_inc(SV.sem, 1)
            ve.wait_ge(SA.sem, SA.at("vn"))
            for h in range(RH):
                if h:
                    ve.wait_ge(kv_s, 2 * h)
                ve.tensor_tensor(v_blk[0:32, :].rearrange("p (b e) -> p b e", b=NB),
                                 v_nat[0:32, h * 128:(h + 1) * 128].unsqueeze(1).to_broadcast([32, NB, 128]),
                                 K["seq_of"][0:32, :].unsqueeze(2).to_broadcast([32, NB, 128]), ALU.mult).then_inc(SV.sem, 1)
                for u in range(2):
                    ve.wait_ge(kv_s, 2 * h + u + 1)
                    ve.wait_ge(SP_.sem, SP_.at("o"))
                    st = ret_states[:, 4 * u:4 * u + 4, h, :]
                    ve.scalar_tensor_tensor(out=st, in0=st, scalar=float(gam4[h]),
                                            in1=ps[:, (2 * h + u) % 2, :].rearrange("p (b e) -> p b e", b=4),
                                            op0=ALU.mult, op1=ALU.add).then_inc(st_s, 1)
            for h in range(RH):
                o = big[:, QZ + h, :]
                ve.wait_ge(GP.sem, GP.at("mean", h))
                ve.tensor_tensor(half(o), half(o), ps[:, 4:6, 0:HT], ALU.subtract).then_inc(GV.sem, 1)
                ve.wait_ge(GA.sem, GA.at("std", h))
                ve.reciprocal(gn_sd, gn_sd).then_inc(GV.sem, 1)
                ve.wait_ge(GV.sem, GV.at("rs", h))
                ve.tensor_tensor(o, o, gn_sd, ALU.mult).then_inc(GV.sem, 1)
                ve.wait_ge(GV.sem, GV.at("nrm", h))
                ve.wait_ge(consts_in, 32)
                ve.tensor_scalar(o, o, K["gn_g"][:, h:h + 1], None, ALU.mult).then_inc(GV.sem, 1)
                ve.wait_ge(GV.sem, GV.at("gn", h))
                ve.wait_ge(gn_gate, 1)
                ve.tensor_tensor(o, o, big[:, GZ + h, :], ALU.mult).then_inc(GV.sem, 1)
                ve.wait_ge(GV.sem, GV.at("mul", h))
                ve.sem_inc(yb_done, 1)

            def take_residual(name, m):
                pp = 3 if name.startswith("down") else 1
                ve.wait_ge(pieces, PB[name] + pp * (m + 1))
                ve.scalar_tensor_tensor(out=half(y[:, m, :]), in0=half(x[:, m, :]), scalar=float(ALPHA), in1=pset(m % 2),
                                        op0=ALU.mult, op1=ALU.add).then_inc(freed[m % 2], 1)

            def norm(r, name):
                for m in range(KC):
                    take_residual(name, m)
                ve.wait_ge(ln_mean, r + 1)
                for m in range(KC):
                    ve.tensor_tensor(half(y[:, m, :]), half(y[:, m, :]), ps[:, 4:6, 0:HT], ALU.subtract).then_inc(ln_cen, 1)
                ve.wait_ge(ln_std, r + 1)
                ve.reciprocal(ln_row(r, 1), ln_row(r, 1)).then_inc(ln_rs, 1)
                ve.wait_ge(ln_rs, r + 1)
                ve.wait_ge(ln_sq, 8 * r + 8)
                for m in range(KC):
                    ve.tensor_tensor(y[:, m, :], y[:, m, :], ln_row(r, 1), ALU.mult).then_inc(ln_nrm, 1)

            def ffn(layer):
                name = f"up{layer}"
                base = layer * FC
                cw = K["fconv"].rearrange("p (l c w) -> p l c w", l=2, c=FC)[:, layer, :, :]

                def row(jb, u, peeled):
                    j = jb * 2 + u
                    a, c = ffn_a[:, u, :], ffn_c[:, u, 0:CO]
                    w = cw[:, bass.ds(j, 1), :].rearrange("p a w -> p (a w)")
                    ve.wait_ge(freed[0], SB[name] + j + 1)
                    ve.wait_ge(fp.sem, fp.at("in", j + base))
                    if not peeled:
                        ve.wait_ge(fa.sem, j + base - 1)
                    ve.tensor_scalar(c, a[:, 0:CO], w[:, 0:1], w[:, 3:4], ALU.mult, ALU.add).then_inc(fd.sem, 1)
                    for q in (1, 2):
                        ve.wait_ge(fd.sem, fd.at(f"c{q - 1}", j + base))
                        ve.scalar_tensor_tensor(out=c, in0=a[:, q:q + CO], scalar=w[:, q:q + 1], in1=c,
                                                op0=ALU.mult, op1=ALU.add).then_inc(fd.sem, 1)
                    ve.wait_ge(pieces, PB[name] + jb * 4 + (2 * u + 2))
                    ve.wait_ge(fa.sem, j + base + 1)
                    ve.tensor_tensor(big[:, bass.ds(j, 1), :].rearrange("p a (h t) -> p (a h) t", h=2),
                                     half(ffn_g[:, u, :]), pset(1), ALU.mult).then_inc(freed[1], 1)

                row(0, 0, True)
                row(0, 1, True)
                with ve.Fori(1, FC // 2) as jb:
                    row(jb, 0, False)
                    row(jb, 1, False)

            norm(0, "out0")
            ffn(0)
            norm(1, "down0")
            NSA_DVE(ve, take_odd)
            norm(2, "out1")
            ffn(1)
            norm(3, "down1")

        @block.gpsimd
        def _(po):
            po.memset(eps, EPS).then_inc(pool_set, 1)
            po.memset(conv_u, 0.0).then_inc(zero_u, 1)
            po.wait_ge(zero_u, 1)
            po.wait_ge(hist_in, 16)
            po.wait_ge(consts_in, 32)
            sw = K["sconv"].rearrange("p (c w) -> p c w", c=4)
            us = conv_u[:, SO:CW].rearrange("p (b w) -> p b w", b=NB)
            for c in range(4):
                C_, H_, B_ = big[:, CZ + c, :], big[:, HZ + c, :], big[:, BZ + c, :]

                def sample(v):
                    return v[:, SEQ:T].rearrange("p (b w) -> p b w", b=NB)
                if c:
                    po.wait_ge(ya.sem, ya.at("ys", c - 1))
                po.tensor_copy(us[:, :, 0:2], sconv_hist[:, c, :, :]).then_inc(ya.sem, 1)
                po.wait_ge(freed[0], 14)
                po.wait_ge(freed[1], 14)
                po.tensor_tensor(conv_u[:, 2:SO], C_[:, 0:SEQ], H_[:, 0:SEQ], ALU.mult).then_inc(ya.sem, 1)
                po.tensor_tensor(us[:, :, 2:6], sample(C_), sample(H_), ALU.mult).then_inc(ya.sem, 1)
                po.wait_ge(ya.sem, ya.at("us", c))
                po.tensor_scalar(conv_c[:, 0:CO], conv_u[:, 0:CO], sw[:, c, 0:1], sw[:, c, 3:4], ALU.mult, ALU.add).then_inc(ya.sem, 1)
                for q in (1, 2):
                    po.tensor_scalar(conv_d, conv_u[:, q:q + CO], sw[:, c, q:q + 1], None, ALU.mult).then_inc(ya.sem, 1)
                    po.wait_ge(ya.sem, ya.at(f"t{q}", c))
                    po.tensor_tensor(conv_c[:, 0:CO], conv_c[:, 0:CO], conv_d, ALU.add).then_inc(ya.sem, 1)
                    po.wait_ge(ya.sem, ya.at(f"s{q}", c))
                po.tensor_copy(sconv_out[:, c, 0:2], conv_u[:, SEQ:SEQ + 2])
                po.tensor_copy(sconv_out[:, c, 2:18].rearrange("p (b w) -> p b w", b=NB), us[:, :, 4:6]).then_inc(ya.sem, 1)
                po.tensor_tensor(H_[:, 0:SEQ], conv_c[:, 0:SEQ], B_[:, 0:SEQ], ALU.mult).then_inc(ya.sem, 1)
                po.tensor_tensor(sample(H_), conv_sample(conv_c), sample(B_), ALU.mult).then_inc(ya.sem, 1)
            po.wait_ge(ya.sem, ya.at("ys", 3))
            po.dma_start(A["o_sconv"], sconv_out).then_inc(hist_store, 16)
            po.wait_ge(RV.sem, RV.at("state", 3))
            po.dma_start(A["o_ret_p"], state).then_inc(hist_store, 16)
            po.wait_ge(st_s, 8)
            po.dma_start(A["o_ret_s"], ret_states).then_inc(hist_store, 16)
            stores = 3

            def sums(r, name, stores):
                po.wait_ge(hist_store, 16 * stores)
                if r:
                    po.wait_ge(ln_mean, r)
                po.wait_ge(pieces, PB[name] + 1)
                po.memset(ln_row(r, 0), 0.0).then_inc(ln_zero, 1)
                po.wait_ge(ln_zero, r + 1)
                for m in range(KC):
                    po.wait_ge(freed[m % 2], SB[name] + m // 2 + 1)
                    if m:
                        po.wait_ge(ln_sum, 8 * r + m)
                    po.tensor_tensor(ln_row(r, 0), ln_row(r, 0), y[:, m, :], ALU.add).then_inc(ln_sum, 1)

            def ffn(layer, stores):
                name = f"up{layer}"
                base = layer * FC
                po.wait_ge(hist_store, 16 * stores)
                po.memset(ffn_a[:, 0, 0:2], 0.0).then_inc(ffn_zero, 1)
                po.memset(ffn_a[:, 1, 0:2], 0.0).then_inc(ffn_zero, 1)
                po.dma_start(ffn_hist, A["state_ffn"][layer]).then_inc(hist_load, 16)
                po.wait_ge(ffn_zero, 2 * layer + 2)
                po.wait_ge(hist_load, 16 * (layer + 1))

                def row(jb, u, peeled):
                    j = jb * 2 + u
                    s = ffn_a[:, u, SO:CW].rearrange("p (b w) -> p b w", b=NB)
                    if not peeled:
                        po.wait_ge(fd.sem, fd.at("c2", j + base - 2))
                        po.wait_ge(fp.sem, fp.at("out", j + base - 2))
                    po.tensor_copy(s[:, :, 0:2], ffn_hist[:, bass.ds(j, 1), :, :].rearrange("p a b w -> p (a b) w")).then_inc(fp.sem, 1)
                    po.wait_ge(freed[0], SB[name] + j + 1)
                    fo = ffn_out[:, bass.ds(j, 1), :]
                    po.tensor_copy(fo[:, :, 0:2].rearrange("p a w -> p (a w)"), ffn_a[:, u, SEQ:SEQ + 2])
                    po.tensor_copy(fo[:, :, 2:18].rearrange("p a (b w) -> p (a b) w", b=NB), s[:, :, 4:6]).then_inc(fp.sem, 1)

                row(0, 0, True)
                row(0, 1, True)
                with po.Fori(1, FC // 2) as jb:
                    row(jb, 0, False)
                    row(jb, 1, False)
                po.wait_ge(fp.sem, fp.at("out", base + FC - 1))
                po.dma_start(A["o_ffn"][layer], ffn_out).then_inc(hist_store, 16)
                return stores + 1

            sums(0, "out0", stores)
            stores = ffn(0, stores)
            sums(1, "down0", stores)
            stores = NSA_POOL(po, stores, hist_store)
            sums(2, "out1", stores)
            stores = ffn(1, stores)
            sums(3, "down1", stores)
            po.wait_ge(hist_store, 16 * stores)


OUTS = {
    "o_x": (128, KC, T), "o_sconv": (128, 4, 18), "o_ret_p": (128, RH * 128), "o_ret_s": (128, NB, RH, 128),
    "o_ffn": (2, 128, FC, 18),
    "o_kv": (128, 12, T), "o_win_k": (NB, 128, 2, W), "o_win_v": (NB, W, 256),
}


def pieces_of(w):
    k, n = w.shape
    return np.ascontiguousarray(w.reshape(k // 128, 128, n // 128, 128).transpose(2, 1, 0, 3)).reshape(n // 128, 128, k)


def by_part(v):
    f = v.shape[-1]
    u = v.reshape(v.shape[:-1] + (f // 128, 128))
    return np.moveaxis(u, -1, 0)


def kernel(**inputs):
    import concourse.bacc as bacc
    from concourse.bass_utils import run_bass_kernel_spmd

    I = {k: np.asarray(v) for k, v in inputs.items()}
    A = {}
    xs = np.concatenate([I["x_prompt"][0], I["x_sample"].reshape(NS, D)])
    A["xT"] = xs.T.reshape(KC, 128, T).transpose(1, 0, 2)
    we = I["w_in_even"][0]
    h, b, c, q, k, v, g = (we[:, 512 * n:512 * n + 512] for n in range(7))
    A["w_in0"] = pieces_of(np.concatenate([q, k, v, g, c, h, b], 1))
    A["w_out0"] = pieces_of(I["w_out_even"][0])
    for l in range(2):
        up = I["ffn_w_up"][l].reshape(D, 2, FC, 128).transpose(0, 2, 1, 3).reshape(D, 2 * DFF)
        A[f"w_up{l}"] = pieces_of(up)
        A[f"w_down{l}"] = pieces_of(I["ffn_w_down"][l])
    wo = I["w_in_odd"][0]

    def heads(w, axis):
        s = w.shape
        if axis == 1:
            return w.reshape(s[0], 2, 2, 4, -1).transpose(0, 1, 3, 2, 4).reshape(s)
        return w.reshape(2, 2, 4, -1, s[1]).transpose(0, 2, 1, 3, 4).reshape(s)

    A["w_in1"] = pieces_of(np.concatenate([heads(wo[:, 0:1024], 1), wo[:, 1024:2560]], 1))
    gates = wo[:, 2560:2608].reshape(D, 3, 2, 2, 4).transpose(0, 1, 2, 4, 3).reshape(D, 48)
    A["w_gate"] = gates.reshape(KC, 128, 48).transpose(1, 0, 2)
    A["w_out1"] = pieces_of(heads(I["w_out_odd"][0], 0))
    A["w1"] = I["cmp_w1"][0].reshape(2, 16, 128, 128).transpose(2, 0, 1, 3).reshape(128, 2, 2048)
    A["w2"] = I["cmp_w2"][0].transpose(1, 0, 2)
    A["state_ret"] = I["state_ret"][0].transpose(2, 0, 1, 3)
    A["state_sconv"] = I["state_sconv"][0].reshape(NB, 2, 4, 128).transpose(3, 2, 0, 1)
    A["state_ffn"] = I["state_ffn_conv"].reshape(2, NB, 2, FC, 128).transpose(0, 4, 3, 1, 2)
    A["keep"] = np.concatenate([CONSTS[k] for k in KEEP], 1)
    A["early"] = np.concatenate([CONSTS[k] for k in EARLY], 1)
    sconv = np.concatenate([I["sconv_w"][0], I["sconv_b"]], 0)
    fconv = np.concatenate([I["ffn_conv_w"], I["ffn_conv_b"][:, None]], 1)
    ln_g = np.stack([I["ln_mix_g"][0], I["ln_ffn_g"][0], I["ln_mix_g"][1], I["ln_ffn_g"][1]])
    ln_b = np.stack([I["ln_mix_b"][0], I["ln_ffn_b"][0], I["ln_mix_b"][1], I["ln_ffn_b"][1]])
    vecs = [by_part(sconv).transpose(0, 2, 1), by_part(I["ret_gn_g"][0]), by_part(ln_g), by_part(ln_b),
            by_part(fconv).transpose(0, 1, 3, 2), I["cmp_pe"][0].reshape(2, 16, 128).transpose(2, 0, 1)]
    A["vecs"] = np.concatenate([v.reshape(128, -1) for v in vecs], 1)
    pages_k = I["cache_cmp_k"][0], I["cache_cmp_v"][0]
    for n, p in zip(("cmp_k", "cmp_v"), pages_k):
        A[n] = p.reshape(NPHYS, 8, 8, 2, 4, 64).transpose(0, 3, 5, 2, 4, 1).reshape(NPHYS, 128, 256)
    A["slc_k"] = I["cache_slc_k"][0].reshape(NPHYS, 128, 2, 128).transpose(0, 3, 2, 1).reshape(NPHYS, 128, 256)
    A["slc_v"] = I["cache_slc_v"][0].reshape(NPHYS, 128, 256)
    A["win_k"] = I["cache_win_k"][0].reshape(NB, W, 2, 128).transpose(0, 3, 2, 1)
    A["win_v"] = I["cache_win_v"][0].reshape(NB, 4, 128, 256)
    A["page_table"] = I["page_table"].reshape(1, NB * NPG)

    nc = bacc.Bacc("TRN2", target_bir_lowering=False, num_devices=1)
    arrays, aps = {}, {}
    for name, a in A.items():
        a = np.ascontiguousarray(a)
        arrays["in_" + name] = a
        aps[name] = nc.dram_tensor("in_" + name, a.shape, mybir.dt.from_np(a.dtype), kind="ExternalInput").ap()
    for name, shape in OUTS.items():
        aps[name] = nc.dram_tensor("out_" + name, shape, F32, kind="ExternalOutput").ap()
    build(nc, aps)
    R = run_bass_kernel_spmd(nc, [arrays], core_ids=[0]).results[0]
    R = {n: np.asarray(R["out_" + n]) for n in OUTS}

    yT = R["o_x"].transpose(2, 1, 0).reshape(T, D)

    def conv_states(v, n):
        rows = v.transpose(2, 1, 0).reshape(18, n)
        return rows[0:2][None], rows[2:18].reshape(NB, 2, n)

    sp_, ss = conv_states(R["o_sconv"], 512)
    ret_p = R["o_ret_p"].reshape(128, RH, 128).transpose(1, 0, 2)[None]
    ret_s = R["o_ret_s"].transpose(1, 2, 0, 3)
    ff = [conv_states(R["o_ffn"][l], DFF) for l in range(2)]
    kvT = R["o_kv"].transpose(2, 1, 0).reshape(T, 6, 4, 64)
    p = [kvT[:SEQ, n][None, None] for n in range(6)]
    s = [kvT[SEQ:, n].reshape(1, NB, NT, 4, 64) for n in range(6)]
    wk = R["o_win_k"].transpose(0, 3, 2, 1).reshape(1, NB, W, 4, 64)
    wv = R["o_win_v"].reshape(1, NB, W, 4, 64)
    out = [yT[None, :SEQ], yT[SEQ:].reshape(NB, NT, D), sp_[None], ss[None], ret_p[None], ret_s[None],
           p[0], p[1], p[2], p[3], s[0], s[1], s[2], s[3], p[4], p[5], wk, wv,
           np.stack([ff[0][0], ff[1][0]]), np.stack([ff[0][1], ff[1][1]])]
    return tuple(np.ascontiguousarray(o) for o in out)
```

```python
from contextlib import ExitStack

import numpy as np
import concourse.bass as bass
from concourse import mybir

F32 = mybir.dt.float32
F32R = mybir.dt.float32r
I32 = mybir.dt.int32
ALU = mybir.AluOpType
ACT = mybir.ActivationFunctionType
AX = mybir.AxisListType

MAP = 53080
D = 1024
SEQ, NB, NT = 512, 8, 4
NS = NB * NT
T = SEQ + NS
HT = T // 2
KC = D // 128
DFF = 2816
FC = DFF // 128
RH = 4
PAST, PAGE = 2048, 128
NPG = PAST // PAGE
NPHYS = 160
NC = PAST // 16
NCMP = NC - 1
NCP = SEQ // 16
NSLC = 33
TOPN = 16
W = 512
NEG = -1e30
ALPHA = 4.0 ** 0.25
EPS = 1e-5
CW = 2 + SEQ + NB * (2 + NT)
CO = CW - 2
SO = SEQ + 2

GEMMS = [("in0", 28, 28), ("out0", 8, 8), ("up0", 44, 44), ("down0", 24, 8),
         ("in1", 20, 20), ("out1", 8, 8), ("up1", 44, 44), ("down1", 24, 8)]
PB, SB = {}, {}
_p = _s = 0
for _n, _a, _b in GEMMS:
    PB[_n], SB[_n] = _p, _s // 2
    _p += _a
    _s += _b


class Steps:

    def __init__(self, sem, names):
        self.sem, self.n = sem, len(names)
        self.index = {name: k for k, name in enumerate(names)}

    def at(self, name, r=0):
        return r * self.n + (self.index[name] + 1)


def layout_consts():
    c = {}
    c["ident"] = np.eye(128)
    c["mean_d"] = np.full((128, 128), 1.0 / D)
    c["mean_h"] = np.full((128, 128), 1.0 / 128)
    pos = np.concatenate([np.arange(SEQ), np.tile(PAST + np.arange(NT), NB)]).astype(np.float32)
    inv = (np.float32(10000.0) ** (-np.arange(64, dtype=np.float32) / np.float32(64))).astype(np.float32)
    ang = (pos[None, :] * inv[:, None]).astype(np.float32).astype(np.float64)
    c["rope_cos"] = np.concatenate([np.cos(ang)] * 2)
    c["rope_sin"] = np.concatenate([-np.sin(ang), np.sin(ang)])
    swap = np.zeros((128, 128))
    swap[(np.arange(128) + 64) % 128, np.arange(128)] = 1.0
    c["swap"] = swap
    lg = np.log1p(-np.exp2(-5.0 - np.arange(RH)))
    scale = 128 ** -0.5
    m, n = np.arange(128)[:, None], np.arange(128)[None, :]
    c["decay"] = np.concatenate([np.where(n >= m, np.exp(g * np.maximum(n - m, 0)), 0) * scale for g in lg], 1)
    c["qdec"] = np.concatenate([np.tile(np.exp((np.arange(128) + 1.0) * g) * scale, (128, 1)) for g in lg], 1)
    c["kdec"] = np.stack([np.exp((127.0 - np.arange(128)) * g) for g in lg], 1)
    t = np.arange(NS)
    same = (t[:, None] // NT) == (t[None, :] // NT)
    dt = t[None, :] - t[:, None]
    ds_ = np.concatenate([np.where(same & (dt >= 0), np.exp(g * np.maximum(dt, 0)), 0) * scale for g in lg], 1)
    c["decay_s"] = np.pad(ds_, ((0, 96), (0, 0)))
    c["qdec_s"] = np.concatenate([np.tile(np.exp((t % NT + 1.0) * g) * scale, (128, 1)) for g in lg], 1)
    c["kdec_s"] = np.pad(np.stack([np.exp((NT - 1.0 - t % NT) * g) for g in lg], 1), ((0, 96), (0, 0)))
    c["seq_of"] = np.pad((t[:, None] // NT == np.arange(NB)[None, :]).astype(float), ((0, 96), (0, 0)))
    row = np.arange(128)
    rb, rgp, rg2, rj, rt = row // 64, row // 32 % 2, row // 16 % 2, row // 4 % 4, row % 4
    c["causal"] = np.where(n <= m, 0.0, NEG)
    blk = np.arange(32)[None, :] * 16 + 31
    tok = (np.arange(4)[None, :] * 128 + np.arange(128)[:, None])[:, :, None]
    ok = (blk[None] <= tok) & (np.arange(32) < NCP - 1)[None, None]
    c["cmp_mask"] = np.where(ok, 0.0, NEG).reshape(128, 128)
    c["cmp_valid"] = ok.astype(float).reshape(128, 128)
    sel = np.zeros((128, 3, 128))
    for br in range(3):
        sel[br * 16 + rgp * 8 + rj * 2 + rg2, br, row] = 1.0
    c["head_of_row"] = sel.reshape(128, 384)
    pair, b2, tt = t // 8, t // 4 % 2, t % 4
    c["token_of_row"] = ((b2[None, :] == rb[:, None]) & (tt[None, :] == rt[:, None])).astype(float)
    key = (rb * 4 + rgp * 2 + rg2) * 4 + rt
    c["heads_sum"] = (key[:, None] == key[None, :]).astype(float)
    j = np.arange(NSLC)
    c["bonus"] = np.tile(np.where((j == 0) | (j >= NSLC - 2), 1e4, 0.0), (128, 1))
    c["earlier"] = np.tile((j[None, :] < j[:, None]).astype(float).reshape(1, -1), (128, 1))
    fm = np.zeros((128, 4, NS))
    for r in range(4):
        own = (pair[None, :] == r) & (b2[None, :] == rb[:, None]) & (tt[None, :] <= rt[:, None])
        fm[:, r] = np.where(own, 0.0, NEG)
    c["fresh_mask"] = fm.reshape(128, 128)
    c["win_mask"] = np.where(np.arange(32)[None, :] > rt[:, None], 0.0, NEG)
    return {k: np.ascontiguousarray(v, dtype=np.float32) for k, v in c.items()}


CONSTS = layout_consts()
KEEP = ["ident", "mean_d", "causal", "cmp_mask", "cmp_valid", "head_of_row", "token_of_row", "heads_sum",
        "bonus", "earlier", "fresh_mask", "win_mask"]
EARLY = ["mean_h", "rope_cos", "rope_sin", "swap", "decay", "qdec", "kdec", "decay_s", "qdec_s", "kdec_s", "seq_of"]
VECS = [("sconv", 16), ("gn_g", 4), ("ln_g", 32), ("ln_b", 32), ("fconv", 2 * FC * 4), ("pe", 32)]


def build(nc, A):
    ctx = ExitStack()
    with ctx:
        def sem(name):
            return ctx.enter_context(nc.semaphore(name))

        ptab = ctx.enter_context(nc.sbuf_tensor("ptab", [1, NB * NPG], I32))
        ps = ctx.enter_context(nc.psum_tensor("ps", [128, 8, 512], F32))
        map_at = (nc.sbuf_base + 31) // 32 * 32
        WG = KC * 48
        BIG_AT = 2 * KC * T
        RING_AT = BIG_AT + 28 * T
        SLOTS_AT = RING_AT + 8 * 1024
        GATES_AT = SLOTS_AT + 4 * 4096
        REST_AT = GATES_AT + 2 * WG

        def place(name, start, end, dtype):
            return start, end, nc.alloc_sbuf_tensor_at(name, [128, end - start], dtype, offset=map_at + 4 * start)

        F = [place("big", BIG_AT, RING_AT, F32), place("ring", RING_AT, SLOTS_AT, F32), place("slots", SLOTS_AT, GATES_AT, F32),
             place("gates_w", GATES_AT, GATES_AT + WG, F32), place("rest", REST_AT, MAP, F32)]
        R = [place("x_parts", 0, BIG_AT, F32R), place("big_parts", BIG_AT, RING_AT, F32R),
             place("piece_parts", RING_AT, RING_AT + 4 * 1024, F32R), place("hidden_parts", SLOTS_AT, SLOTS_AT + FC * T, F32R),
             place("gates_w_low", GATES_AT, GATES_AT + WG, F32R), place("gates_w_high", GATES_AT + WG, REST_AT, F32R)]
        top = [REST_AT]

        def span(regions, at, n):
            start, _, t = next(v for v in regions if v[0] <= at and at + n <= v[1])
            return t[:, at - start:at - start + n]

        def alloc(n, base=None):
            b = top if base is None else base
            b[0] += n
            return span(F, b[0] - n, n)

        def as_f32(v):
            return v.bitcast(F32)

        def by_chunk(v, k):
            return v.rearrange("p (k t) -> p k t", k=k)

        xhs, xls = (by_chunk(span(R, k * KC * T, KC * T), KC) for k in range(2))
        big, bigs = (by_chunk(span(v, BIG_AT, 28 * T), 28) for v in (F, R))
        split = span(R, RING_AT, 4 * 1024).rearrange("p (s h n) -> p s h n", s=2, h=2)
        raw_at = RING_AT + 4 * 1024
        raw = [span(F, raw_at + (3 - s) * 1024, 1024) for s in range(4)]
        slots = span(F, SLOTS_AT, 4 * 4096).rearrange("p (s n) -> p s n", s=4)
        wg = span(F, GATES_AT, WG)
        wg_l, wg_h = (by_chunk(span(R, GATES_AT + k * WG, WG), KC) for k in range(2))
        y_at = GATES_AT - KC * T
        y = by_chunk(span(F, y_at, KC * T), KC)
        hid_l = by_chunk(span(R, SLOTS_AT, FC * T), FC)
        assert SLOTS_AT + FC * T <= y_at
        w1 = span(F, BIG_AT + 20 * T, 4096).rearrange("p (v n) -> p v n", v=2)
        w2 = alloc(2 * 64).rearrange("p (v n) -> p v n", v=2)
        keep_w = sum(CONSTS[k].shape[1] for k in KEEP)
        keep_all = alloc(keep_w)
        K = {}
        at = 0
        for k in KEEP:
            n = CONSTS[k].shape[1]
            K[k] = keep_all[:, at:at + n]
            at += n
        vec_w = sum(n for _, n in VECS)
        vec_all = alloc(vec_w)
        at = 0
        for k, n in VECS:
            K[k] = vec_all[:, at:at + n]
            at += n
        eps = alloc(1)
        fresh_v = alloc(512).rearrange("p (v n) -> p v n", v=2)
        grow = alloc(12)

        e = [SLOTS_AT]
        ret_states = alloc(NB * RH * 128, e).rearrange("p (b h e) -> p b h e", b=NB, h=RH)
        early_w = sum(CONSTS[k].shape[1] for k in EARLY)
        early_all = alloc(early_w, e)
        at = 0
        for k in EARLY:
            n = CONSTS[k].shape[1]
            K[k] = early_all[:, at:at + n]
            at += n
        sconv_hist = alloc(4 * 16, e).rearrange("p (c b w) -> p c b w", c=4, b=NB)
        sconv_out = alloc(4 * 18, e).rearrange("p (c w) -> p c w", c=4)
        rope_t = alloc(T, e)
        k_nat, v_nat, s_dec, q_dec, state = (alloc(512, e) for _ in range(5))
        v_blk = alloc(NB * 128, e)
        conv_u, conv_c, conv_d = alloc(CW, e), alloc(CO + 2, e), alloc(CO, e)
        gn_sq, gn_sd = alloc(T, e), alloc(T, e)
        assert e[0] <= GATES_AT
        e = [y_at]
        ffn_a = alloc(2 * CW, e).rearrange("p (u n) -> p u n", u=2)
        ffn_c = alloc(2 * (CO + 2), e).rearrange("p (u n) -> p u n", u=2)
        ffn_g = alloc(2 * T, e).rearrange("p (u n) -> p u n", u=2)
        ffn_hist = alloc(FC * 16, e).rearrange("p (c b w) -> p c b w", c=FC, b=NB)
        ffn_out = alloc(FC * 18, e).rearrange("p (c w) -> p c w", c=FC)
        assert e[0] <= SLOTS_AT + 4 * 4096

        def ln_row(r, k):
            return big[:, (20, 24, 16, 24)[r] + k, :]

        w_hi = sem("w_hi")
        w_lo = sem("w_lo")
        w_in = [sem(f"w_in{s}") for s in range(4)]
        pieces = sem("pieces")
        freed = [sem(f"freed{s}") for s in range(2)]
        consts_in = sem("consts_in")
        early_in = sem("early_in")
        x_in = [sem(f"x_in{k}") for k in range(4)]
        x0_hi, x0_lo = sem("x0_hi"), sem("x0_lo")
        mix_hi, mix_lo = sem("mix_hi"), sem("mix_lo")
        att_hi, att_lo = sem("att_hi"), sem("att_lo")
        wg_hi, wg_lo = sem("wg_hi"), sem("wg_lo")
        hid_hi, hid_lo = sem("hid_hi"), sem("hid_lo")
        ln_hi = sem("ln_hi")
        w1_in = sem("w1_in")
        hist_in = sem("hist_in")
        ln_sum, ln_mean, ln_cen, ln_sq, ln_var, ln_std, ln_rs, ln_nrm, ln_x = (
            sem(n) for n in ("ln_sum", "ln_mean", "ln_cen", "ln_sq", "ln_var", "ln_std", "ln_rs", "ln_nrm", "ln_x"))
        ln_zero = sem("ln_zero")
        nsa_in = sem("nsa_in")
        out_done = sem("out_done")
        pool_set = sem("pool_set")

        def half(v):
            return v.rearrange("p (h t) -> p h t", h=2)

        def half1(v):
            return v.rearrange("p a (h t) -> p (a h) t", h=2)

        def feed(eng, part, name, take, stop=False):
            down = name.startswith("down")
            per = 12 if down else 4
            bodies = dict((g[0], g[1]) for g in GEMMS)[name] // per

            def body(i, last):
                for q in range(per):
                    if not (last and q >= per - 2):
                        part(PB[name] + i * per + (q + 2), (q + 2) % 4, PB[name] // 4 + i * (per // 4) + ((q + 2) // 4 + 1),
                             768 if down and (q + 2) % 3 == 2 else 1024)
                    if take:
                        take(i, q)

            with eng.Fori(0, bodies - stop) as i:
                body(i, False)
            if stop:
                body(bodies - 1, True)

        y_done = sem("y_done")

        def pset(s):
            return ps[:, 2 * s:2 * s + 2, 0:HT]

        rope_pe = sem("rope_pe")
        RD = Steps(sem("rope_dve"), ["sin", "cos", "add"])
        RP = Steps(sem("ret_pe"), ["kT", "vT", "sc", "o", "kv"])
        RV = Steps(sem("ret_dve"), ["kn", "st", "qd", "state"])
        RA = Steps(sem("ret_act"), ["vn", "o"])
        SP_ = Steps(sem("rets_pe"), ["kT", "vT", "sc", "o"])
        SV = Steps(sem("rets_dve"), ["kn", "st", "qd", "vb"])
        SA = Steps(sem("rets_act"), ["vn", "o"])
        kv_s = sem("kv_s")
        st_s = sem("st_s")
        GP = Steps(sem("gn_pe"), ["mean", "var"])
        GV = Steps(sem("gn_dve"), ["cen", "rs", "nrm", "gn", "mul"])
        GA = Steps(sem("gn_act"), ["sq", "std"])
        gn_gate = sem("gn_gate")
        ya = Steps(sem("conv_pool"), ["hist", "up", "us", "t0", "t1", "s1", "t2", "s2", "keep", "yp", "ys"])
        ret_in = sem("ret_in")
        zero_u = sem("zero_u")
        QZ, KZ, VZ, GZ, CZ, HZ, BZ = 0, 4, 8, 12, 16, 20, 24
        MIX_H, MIX_L = KZ, [BZ, BZ + 1, BZ + 2, BZ + 3, CZ, CZ + 1, CZ + 2, CZ + 3]

        def in0_done(row):
            return PB["in0"] + row + 1

        fa = Steps(sem("ffn_act"), ["a", "gelu"])
        fd = Steps(sem("ffn_dve"), ["c0", "c1", "c2"])
        fp = Steps(sem("ffn_pool"), ["in", "out"])
        hist_load = sem("hist_load")
        ffn_zero = sem("ffn_zero")
        hist_store = sem("hist_store")

        def conv_sample(c):
            return c[:, SO:SO + 6 * NB].rearrange("p (b w) -> p b w", b=NB)[:, :, 0:NT]

        KVR = 8
        KS, VS, KW, VW = 12, 14, 16, 18
        cbias = alloc(2)
        ATT_H, ATT_L = 8, 20
        soft = alloc(48)
        e = [RING_AT]
        v_nat_p = alloc(2048, e).rearrange("p (v t n) -> p v t n", v=2, t=4)
        c_p = alloc(2048, e).rearrange("p (v c g n) -> p v c g n", v=2, c=8, g=4)
        gtok = alloc(192, e).rearrange("p (q b h) -> p q b h", q=4, b=3)
        e = [SLOTS_AT + 3 * 4096]
        kcc_p = alloc(64, e).rearrange("p (g n) -> p g n", g=2)
        vcc_p = alloc(256, e)
        q_st = alloc(512, e)
        prob = alloc(2 * 1056, e).rearrange("p (u n) -> p u n", u=2)
        pt_p = alloc(9 * 128, e).rearrange("p (t n) -> p t n", t=9)
        bs_p, hid_p = pt_p[:, 0, :].rearrange("p (g n) -> p g n", g=4), pt_p[:, 1, :].rearrange("p (g n) -> p g n", g=4)
        gate_t = prob[0:48].rearrange("p u n -> p (u n)")[:, 0:T]
        grow_m = pt_p[:, 2, 0:96].rearrange("p (b w t) -> p b w t", b=3, w=4)
        nmax = soft[:, 0:6].rearrange("p (u n) -> p u n", u=2)
        rsum = soft[:, 6:12].rearrange("p (u n) -> p u n", u=2)
        fac = soft[:, 12:18].rearrange("p (u n) -> p u n", u=2)
        growv = grow.rearrange("p (b w) -> p b w", b=3)
        assert e[0] <= SLOTS_AT + 4 * 4096
        e = [RING_AT]
        sc_s = alloc(2048 + NS, e)
        sc_w = alloc(W + NS, e)
        kcc = alloc(512, e).rearrange("p (b g n) -> p b g n", b=2, g=2)
        vcc = alloc(512, e).rearrange("p (b n) -> p b n", b=2)
        qb = alloc(256, e).rearrange("p (b g n) -> p b g n", b=2, g=2)
        pc = alloc(128, e)
        pj = alloc(136, e)
        score, rank_a, rank_b = alloc(NSLC), alloc(NSLC), alloc(NSLC)
        pt_all = alloc(23 * 128, e).rearrange("p (t n) -> p t n", t=23)
        cmpx = sc_s[:, 0:NSLC * NSLC].rearrange("p (m n) -> p m n", m=NSLC)
        assert e[0] <= raw_at + 3 * 1024, e[0] - raw_at
        pt_s = [pt_all[:, t, :] for t in range(16)]
        pt_w = [pt_all[:, 16 + t, :] for t in range(4)]
        pt_c, pt_fs, pt_fw = (pt_all[:, 20 + t, :] for t in range(3))
        def pt4(q):
            return pt_all[:, 4 * q:4 * q + 4, :].rearrange("p t n -> p (t n)")

        win_k = big[:, 8:12, 0:W].rearrange("p (b g) n -> p b g n", b=2)
        bs_s = [big[:, 16, 0:512], big[:, 19, 0:512]]
        hid_s = [big[:, 17, 0:512], big[:, 18, 0:512]]
        s_nm, s_sum, s_fac = soft[:, 20:23], soft[:, 23:26], soft[:, 26:29]

        tab_in = sem("tab_in")
        turn, turn_v, turn_a = sem("turn"), sem("turn_v"), sem("turn_a")
        slot_in = [sem(f"slot_in{s}") for s in range(4)]
        kv_store = sem("kv_store")
        NP = Steps(sem("prep_pe"), ["gate", "gT", "grow", "V0", "V1", "V2", "V3", "F", "bias", "k1", "v1", "k2", "v2"])
        NA = Steps(sem("prep_act"), ["sig", "V0", "V2", "bias", "C", "Bk", "hk", "Bv", "hv"])
        ND = Steps(sem("prep_dve"), ["C", "gtok", "gm", "grow", "V1", "V3", "F", "prek", "prev", "kcc", "vcc"])
        U = range(8)

        def of(names, u):
            return [f"{a}{u}" for a in names.split()] if 0 <= u < 8 else []

        TP = Steps(sem("att_pe"), of("s", 0) + of("s", 1) + sum((of("t", u) + of("s", u + 2) + of("o", u) for u in U), []))
        TA = Steps(sem("att_act"), ["q"] + of("e", 0) + of("e", 1) + sum((of("ta", u) + of("e", u + 2) for u in U), []) + ["ov"])
        TD = Steps(sem("att_dve"), of("dm cm mx my", 0) + of("dm cm mx my", 1) + of("rc fa p", 0)
                   + sum((of("tb", u) + of("rc fa p", u + 1) + of("dm cm mx my", u + 2) for u in U), []))
        XP = Steps(sem("smp_pe"), ["ck0", "ck1", "k20", "k21", "sc", "cv0", "cv1", "J", "v20", "v21", "ss0", "ss1", "ws",
                                   "tc", "ts0", "ts1", "ts2", "ts3", "tw", "pv0", "pv1"])
        XD = Steps(sem("smp_dve"), ["pre0", "pre1", "kc0", "kc1", "cmx", "crc", "cp", "pre2", "pre3", "pj", "im", "sc1", "sc2",
                                    "eq", "tri", "r1", "gt", "r2", "rk", "mk", "cf", "pg", "vc0", "vc1", "sv", "sf", "smx",
                                    "wv", "wf", "wmx", "src", "sfa", "sP", "wrc", "wfa", "wP", "ts0", "ts1", "ov"])
        XA = Steps(sem("smp_act"), ["B0", "h0", "B1", "h1", "ce", "B2", "h2", "B3", "h3", "se", "we", "tc", "ts2", "ts3", "tw"])
        XQ = sem("qb_ready")
        win_in = sem("win_in")
        win_out = sem("win_out")
        smp_zero = sem("smp_zero")

        def load_pages(eng, cache, slot, r, b):
            for g in range(NPG):
                v = eng.value_load(ptab[0:1, bass.ds(r * 32 + (b * NPG + g), 1)], min_val=0, max_val=NPHYS - 1)
                eng.dma_start(slots[:, slot, g * 256:(g + 1) * 256],
                              A[cache][bass.ds(v, 1), :, :].rearrange("a p n -> (a p) n")).then_inc(slot_in[slot], 16)

        def pair_pages(eng, caches, slot, r, last, first, carry):
            for b in range(2):
                if not isinstance(r, int):
                    eng.wait_ge(XP.sem, XP.at(last[b], r - 1))
                    eng.sem_inc(carry, 1)
                load_pages(eng, caches[0], slot + b, r, b)
            for b in range(2):
                eng.wait_ge(XP.sem, XP.at(first[b], r))
                eng.sem_inc(carry, 1)
                load_pages(eng, caches[1], slot + b, r, b)

        def feed_in1(eng, part, take):
            def body(i, scale, last=False):
                for q in range(4):
                    if not (last and q >= 2):
                        part(PB["in1"] + i * 4 + (q + 2), (q + 2) % 4, PB["in1"] // 4 + i + ((q + 2) // 4 + 1), 1024)
                    take(i, q, scale)

            with eng.Fori(0, 2) as i:
                body(i, 0.125)
            with eng.Fori(2, 4) as i:
                body(i, 1.0)
            body(4, 1.0, True)

        def NSA_SP(sp, stream):
            stream("in1")
            sp.dma_start(ptab[:, :], A["page_table"]).then_inc(tab_in, 16)
            sp.wait_ge(tab_in, 16)
            pair_pages(sp, ("cmp_k", "slc_k"), 0, 0, ("ss0", "ss1"), ("ck0", "ck1"), turn)
            with sp.Fori(1, 4) as r:
                pair_pages(sp, ("cmp_k", "slc_k"), 0, r, ("ss0", "ss1"), ("ck0", "ck1"), turn)
            stream("out1")

        def NSA_PE(pe, product):
            pe.wait_ge(wg_lo, 1)
            pe.wait_ge(nsa_in, 32)
            pe.wait_ge(w1_in, 16)
            for k in range(KC):
                for w_part, v_part in ((wg_h, xhs), (wg_h, xls), (wg_l, xhs)):
                    for h in range(2):
                        mm = pe.matmul(ps[0:48, 4 + h, 0:HT], w_part[:, k, :], v_part[:, k, h * HT:(h + 1) * HT],
                                       start=k == 0 and w_part is wg_h and v_part is xhs, stop=k == KC - 1 and w_part is wg_l)
            mm.then_inc(NP.sem, 1)
            pe.wait_ge(NA.sem, NA.at("sig"))
            for t in range(4):
                mm = pe.transpose(ps[:, 6, t * 48:t * 48 + 48], gate_t[:, t * 128:(t + 1) * 128], K["ident"][0:48, 0:48])
            mm.then_inc(NP.sem, 1)
            for b in range(3):
                mm = pe.matmul(ps[:, 7, b * 32:b * 32 + 32], K["head_of_row"][0:48, b * 128:(b + 1) * 128], gate_t[:, SEQ:T],
                               start=True, stop=True)
            mm.then_inc(NP.sem, 1)
            pe.wait_ge(freed[0], SB["out1"])
            pe.wait_ge(freed[1], SB["out1"])
            for t in range(4):
                for v, row in enumerate((VS, VW)):
                    for g in range(2):
                        c = (v * 2 + g) * 128
                        mm = pe.transpose(ps[:, t, c:c + 128], big[:, row + g, t * 128:(t + 1) * 128], K["ident"])
                mm.then_inc(NP.sem, 1)
            for v, row in enumerate((VS, VW)):
                for g in range(2):
                    c = (v * 2 + g) * 128
                    mm = pe.transpose(ps[0:32, 4, c:c + 128], big[:, row + g, SEQ:T], K["ident"])
            mm.then_inc(NP.sem, 1)
            for v in range(2):
                for t in range(16):
                    mm = pe.matmul(ps[:, 5, v:v + 1], w1[:, v, t * 128:(t + 1) * 128], K["pe"][:, v * 16 + t:v * 16 + t + 1],
                                   start=t == 0, stop=t == 15)
            mm.then_inc(NP.sem, 1)
            pe.wait_ge(ND.sem, ND.at("grow"))
            for v in range(2):
                if v == 0:
                    pe.wait_ge(ND.sem, ND.at("C"))
                else:
                    pe.wait_ge(NA.sem, NA.at("C"))
                    pe.wait_ge(ND.sem, ND.at("V1"))
                for part in range(2):
                    bank = (6, 0)[v] + part
                    for c in range(8):
                        mm = pe.matmul(ps[:, bank, 0:128], w1[:, v, (part * 8 + c) * 128:(part * 8 + c + 1) * 128],
                                       c_p[:, v, c, :, :].rearrange("p g n -> p (g n)"), start=c == 0, stop=c == 7)
                mm.then_inc(NP.sem, 1)
            pe.wait_ge(NA.sem, NA.at("hk"))
            hg = hid_p.rearrange("p (g h) n -> p g h n", g=2)
            for g2 in range(2):
                mm = pe.matmul(ps[64 * g2:64 * g2 + 64, 2, 0:62].rearrange("p (g n) -> p g n", g=2), w2[:, 0, :],
                               hg[:, :, g2, 0:31], start=True, stop=True)
            mm.then_inc(NP.sem, 1)
            pe.wait_ge(NA.sem, NA.at("hv"))
            for g in range(4):
                mm = pe.matmul(ps[0:31, 3, g * 64:(g + 1) * 64], hid_p[:, g, 0:31], w2[:, 1, :], start=True, stop=True)
            mm.then_inc(NP.sem, 1)
            pe.wait_ge(ND.sem, ND.at("vcc"))

            for gp in range(2):
                def s(R, u):
                    qt, g2 = u // 2, u % 2
                    p0 = slice(64 * g2, 64 * g2 + 64)
                    q = q_st[p0, qt * 128:qt * 128 + 128]
                    n = (qt + 1) * 128
                    if u == 0:
                        pe.wait_ge(TA.sem, TA.at("q", R))
                    if u >= 2:
                        pe.wait_ge(TA.sem, TA.at(f"e{u - 2}", R))
                    pe.matmul(ps[:, 2 * g2, 0:n], q, big[p0, KS + gp, 0:n], start=True, stop=True)
                    pe.matmul(ps[:, 2 * g2 + 1, 0:n], q, big[p0, KW + gp, 0:n], start=True, stop=True)
                    if u:
                        pe.wait_ge(TD.sem, TD.at(f"cm{u - 1}", R))
                    if u >= 2:
                        pe.wait_ge(TD.sem, TD.at(f"tb{u - 2}", R))
                    pe.matmul(ps[:, 4, g2 * 32:g2 * 32 + 31], q, kcc_p[p0, gp, 0:31], start=True, stop=True).then_inc(TP.sem, 1)

                def t(R, u):
                    qt, g2 = u // 2, u % 2
                    pe.wait_ge(TD.sem, TD.at(f"p{u}", R))
                    for kt in range(qt + 1):
                        pe.transpose(ps[:, 5, kt * 128:(kt + 1) * 128], prob[:, g2, kt * 128:(kt + 1) * 128], K["ident"])
                    for kt in range(qt + 1):
                        pe.transpose(ps[:, 6, kt * 128:(kt + 1) * 128], prob[:, g2, 512 + kt * 128:512 + (kt + 1) * 128], K["ident"])
                    if u < 7:
                        pe.wait_ge(TD.sem, TD.at(f"cm{u + 1}", R))
                    pe.transpose(ps[0:31, 4, 128:256], prob[:, g2, 1024:1055], K["ident"]).then_inc(TP.sem, 1)

                def o(R, u):
                    qt, g2 = u // 2, u % 2
                    out = ps[64 * g2:64 * g2 + 64, 7, qt * 128:(qt + 1) * 128]
                    vc = slice(gp * 128 + g2 * 64, gp * 128 + g2 * 64 + 64)
                    if u == 0 and not (isinstance(R, int) and R == 0):
                        pe.wait_ge(TA.sem, TA.at("ov", R - 1))
                    pe.wait_ge(TA.sem, TA.at(f"ta{u}", R))
                    pe.wait_ge(TD.sem, TD.at(f"tb{u}", R))
                    for kt in range(qt + 1):
                        pe.matmul(out, v_nat_p[:, 0, kt, vc], pt_p[:, kt, :], start=kt == 0, stop=False)
                    for kt in range(qt + 1):
                        pe.matmul(out, v_nat_p[:, 1, kt, vc], pt_p[:, 4 + kt, :], start=False, stop=False)
                    pe.matmul(out, vcc_p[0:31, vc], pt_p[0:31, 8, :], start=False, stop=True).then_inc(TP.sem, 1)

                def round_(R):
                    s(R, 0)
                    s(R, 1)
                    for u in U:
                        t(R, u)
                        if u < 6:
                            s(R, u + 2)
                        o(R, u)

                if gp == 0:
                    round_(0)
                with pe.Fori(1 - gp, 4) as j:
                    round_(j + gp * 4)

            def pair(r):
                prev = not (isinstance(r, int) and r == 0)

                def compress(v, b, part_slots):
                    sl = 2 * v + b
                    pe.wait_ge(slot_in[sl], 256 * (1 + 2 * r))
                    rows = slots[:, sl, :].rearrange("p (pg c g n) -> p pg c g n", pg=NPG, c=8, g=4)
                    for part in range(2):
                        dst = ps[:, 2 * b + part, :].rearrange("p (g pg n) -> p pg g n", g=4, pg=NPG)
                        for c in range(8):
                            mm = pe.matmul(dst, w1[:, v, (part * 8 + c) * 128:(part * 8 + c + 1) * 128], rows[:, :, c, :, :],
                                           start=c == 0, stop=c == 7)
                    mm.then_inc(XP.sem, 1)

                if not prev:
                    pe.wait_ge(smp_zero, 3)
                if prev:
                    pe.wait_ge(XD.sem, XD.at("ov", r - 1))
                    pe.wait_ge(XA.sem, XA.at("tw", r - 1))
                for b in range(2):
                    compress(0, b, None)
                for b in range(2):
                    pe.wait_ge(XA.sem, XA.at(f"h{b}", r))
                    hg = hid_s[b].rearrange("p (g h n) -> p g h n", g=2, h=2)
                    for g2 in range(2):
                        mm = pe.matmul(ps[64 * g2:64 * g2 + 64, 4, b * 256:b * 256 + 254].rearrange("p (g n) -> p g n", g=2),
                                       w2[:, 0, :], hg[:, :, g2, 0:NCMP], start=True, stop=True)
                    mm.then_inc(XP.sem, 1)
                pe.wait_ge(XQ, 1 + r)
                pe.wait_ge(XD.sem, XD.at("kc1", r))
                for b in range(2):
                    for g in range(2):
                        mm = pe.matmul(ps[64 * b:64 * b + 64, 6, 0:NCMP], qb[:, b, g, :], kcc[:, b, g, 0:NCMP], start=g == 0, stop=g == 1)
                mm.then_inc(XP.sem, 1)
                for b in range(2):
                    pe.wait_ge(XD.sem, XD.at(f"pre{b}", r))
                    compress(1, b, None)
                pe.wait_ge(XD.sem, XD.at("cp", r))
                pe.matmul(ps[:, 6, 128:128 + NCMP], K["heads_sum"], pc[:, 0:NCMP], start=True, stop=True).then_inc(XP.sem, 1)
                for b in range(2):
                    pe.wait_ge(XA.sem, XA.at(f"h{2 + b}", r))
                    for g in range(4):
                        mm = pe.matmul(ps[0:NCMP, 5, b * 256 + g * 64:b * 256 + g * 64 + 64], hid_s[b][:, g * 128:g * 128 + NCMP],
                                       w2[:, 1, :], start=True, stop=True)
                    mm.then_inc(XP.sem, 1)
                for b in range(2):
                    pe.wait_ge(slot_in[b], 256 * (2 + 2 * r))
                    if b == 0:
                        pe.wait_ge(XD.sem, XD.at("pre3", r))
                    rows = slots[:, b, :].rearrange("p (pg g n) -> p pg g n", pg=NPG, g=2)
                    p0 = slice(64 * b, 64 * b + 64)
                    for t in range(4):
                        for g in range(2):
                            pe.matmul(ps[p0, t, :].rearrange("p (pg n) -> p pg n", pg=4), qb[:, b, g, :],
                                      rows[:, 4 * t:4 * t + 4, g, :], start=g == 0, stop=g == 1)
                    for g in range(2):
                        mm = pe.matmul(ps[p0, 4, 0:32], qb[:, b, g, :], big[:, KS + g, SEQ:T], start=g == 0, stop=g == 1)
                    mm.then_inc(XP.sem, 1)
                pe.wait_ge(win_in, 96 * (1 + r))
                pe.wait_ge(XD.sem, XD.at("vc1", r))
                for b in range(2):
                    p0 = slice(64 * b, 64 * b + 64)
                    for g in range(2):
                        pe.matmul(ps[p0, 5, :], qb[:, b, g, :], win_k[:, b, g, :], start=g == 0, stop=g == 1)
                    for g in range(2):
                        mm = pe.matmul(ps[p0, 7, 256:288], qb[:, b, g, :], big[:, KW + g, SEQ:T], start=g == 0, stop=g == 1)
                mm.then_inc(XP.sem, 1)
                pe.wait_ge(XD.sem, XD.at("pg", r))
                pe.transpose(ps[0:NCMP, 6, 256:384], pc[:, 0:NCMP], K["ident"]).then_inc(XP.sem, 1)
                pe.wait_ge(XD.sem, XD.at("sP", r))
                for q in range(4):
                    for t in range(4):
                        k0 = (4 * q + t) * 128
                        mm = pe.transpose(ps[:, q, t * 128:(t + 1) * 128], sc_s[:, k0:k0 + 128], K["ident"])
                    if q == 3:
                        pe.wait_ge(XA.sem, XA.at("tc", r))
                        mm = pe.transpose(ps[0:32, 6, 384:512], sc_s[:, 2048:2080], K["ident"])
                    mm.then_inc(XP.sem, 1)
                pe.wait_ge(XD.sem, XD.at("wP", r))
                for t in range(4):
                    pe.transpose(ps[:, 5, t * 128:(t + 1) * 128], sc_w[:, t * 128:(t + 1) * 128], K["ident"])
                pe.transpose(ps[0:32, 4, 128:256], sc_w[:, 512:544], K["ident"]).then_inc(XP.sem, 1)
                pe.wait_ge(XD.sem, XD.at("ts1", r))
                pe.wait_ge(XA.sem, XA.at("tw", r))
                for b in range(2):
                    pe.wait_ge(slot_in[2 + b], 256 * (2 + 2 * r))
                    for g in range(2):
                        out = ps[:, 7, (b * 2 + g) * 32:(b * 2 + g) * 32 + 32]
                        rows = slice(64 * b + 32 * g, 64 * b + 32 * g + 32)
                        vc = slice(g * 128, g * 128 + 128)
                        pe.matmul(out, vcc[0:NCMP, b, vc], pt_c[0:NCMP, rows], start=True, stop=False)
                        for t in range(16):
                            pe.matmul(out, slots[:, 2 + b, t * 256 + g * 128:t * 256 + g * 128 + 128], pt_s[t][:, rows],
                                      start=False, stop=False)
                        pe.matmul(out, fresh_v[0:32, 0, vc], pt_fs[0:32, rows], start=False, stop=False)
                        for t in range(4):
                            wv = big[:, 12 + 2 * b + t // 2, (t % 2) * 256 + g * 128:(t % 2) * 256 + g * 128 + 128]
                            pe.matmul(out, wv, pt_w[t][:, rows], start=False, stop=False)
                        mm = pe.matmul(out, fresh_v[0:32, 1, vc], pt_fw[0:32, rows], start=False, stop=True)
                    mm.then_inc(XP.sem, 1)

            pair(0)
            with pe.Fori(1, 4) as r:
                pair(r)
            pe.wait_ge(XD.sem, XD.at("ov", 3))
            pe.wait_ge(att_lo, 2)
            product("out1", lambda k: (bigs[:, ATT_H + k, :], bigs[:, ATT_L + k, :]))

        def NSA_ACT(act, take, hi):
            feed_in1(act, hi, lambda i, q, scale: take("in1", i, q, scale) if q % 2 == 0 else None)
            act.wait_ge(NP.sem, NP.at("gate"))
            act.activation(gate_t.rearrange("p (h t) -> p h t", h=2), ps[0:48, 4:6, 0:HT], ACT.Sigmoid).then_inc(NA.sem, 1)
            for t in (0, 2):
                act.wait_ge(NP.sem, NP.at(f"V{t}"))
                act.activation(v_nat_p[:, :, t, :], ps[:, t, :].rearrange("p (v n) -> p v n", v=2), ACT.Copy).then_inc(NA.sem, 1)
            act.wait_ge(NP.sem, NP.at("bias"))
            act.activation(cbias, ps[:, 5, 0:2], ACT.Copy).then_inc(NA.sem, 1)
            act.wait_ge(freed[1], SB["out1"])
            for g in range(4):
                for par in range(2):
                    src = big[64 * (g % 2):64 * (g % 2) + 64, KVR + 2 + g // 2, 0:SEQ].rearrange("p (n c r) -> p r c n", c=8, r=2)
                    op = act.activation(c_p[64 * par:64 * par + 64, 1, :, g, :], src[:, par, :, :], ACT.Copy)
            op.then_inc(NA.sem, 1)
            for v in range(2):
                act.wait_ge(NP.sem, NP.at(("k1", "v1")[v]))
                if v == 0:
                    act.wait_ge(NA.sem, NA.at("bias"))
                else:
                    act.wait_ge(ND.sem, ND.at("prek"))
                act.activation(bs_p, ps[:, (7, 1)[v], 0:128].rearrange("p (g n) -> p g n", g=4), ACT.Identity,
                               bias=cbias[:, v:v + 1]).then_inc(NA.sem, 1)
                act.wait_ge(ND.sem, ND.at(("prek", "prev")[v]))
                act.activation(hid_p[:, :, 0:31], hid_p[:, :, 0:31], ACT.Gelu_apprx_tanh).then_inc(NA.sem, 1)

            for gp in range(2):
                def e(R, u):
                    qt, g2 = u // 2, u % 2
                    n = (qt + 1) * 128
                    act.wait_ge(TD.sem, TD.at(f"my{u}", R))
                    if u >= 2:
                        act.wait_ge(TP.sem, TP.at(f"t{u - 2}", R))
                    for k in range(2):
                        act.activation(prob[:, g2, 512 * k:512 * k + n], ps[:, 2 * g2 + k, 0:n], ACT.Exp,
                                       bias=nmax[:, g2, k + 1:k + 2], accum_out=rsum[:, g2, k + 1:k + 2])
                    act.activation(prob[:, g2, 1024:1055], prob[:, g2, 1024:1055], ACT.Exp,
                                   bias=nmax[:, g2, 0:1], accum_out=rsum[:, g2, 0:1]).then_inc(TA.sem, 1)

                def ta(R, u):
                    qt = u // 2
                    act.wait_ge(TP.sem, TP.at(f"t{u}", R))
                    if u:
                        act.wait_ge(TP.sem, TP.at(f"o{u - 1}", R))
                    n = (qt + 1) * 128
                    act.activation(pt_p[:, 0:8, :].rearrange("p (k t) n -> p k (t n)", k=2)[:, :, 0:n], ps[:, 5:7, 0:n],
                                   ACT.Copy).then_inc(TA.sem, 1)

                def round_(R):
                    if not (isinstance(R, int) and R == 0):
                        act.wait_ge(TP.sem, TP.at("o7", R - 1))
                    act.activation(q_st.unsqueeze(1), big[:, bass.ds(R, 1), 0:SEQ], ACT.Copy).then_inc(TA.sem, 1)
                    e(R, 0)
                    e(R, 1)
                    for u in U:
                        ta(R, u)
                        if u < 6:
                            e(R, u + 2)
                    act.wait_ge(TP.sem, TP.at("o7", R))
                    act.sem_inc(turn_a, 1)
                    act.activation(big[:, bass.ds(R, 1), 0:SEQ], ps[:, 7, :].unsqueeze(1), ACT.Copy).then_inc(TA.sem, 1)

                if gp == 0:
                    act.wait_ge(ND.sem, ND.at("vcc"))
                    round_(0)
                with act.Fori(1 - gp, 4) as j:
                    round_(j + gp * 4)

            def pair(r):
                def first(c):
                    b = c % 2
                    act.wait_ge(XP.sem, XP.at(("ck0", "ck1", "cv0", "cv1")[c], r))
                    if c >= 2:
                        act.wait_ge(XD.sem, XD.at(f"pre{c - 2}", r))
                    act.activation(bs_s[b], ps[:, 2 * b + 1, :], ACT.Identity, bias=cbias[:, c // 2:c // 2 + 1]).then_inc(XA.sem, 1)
                    act.wait_ge(XD.sem, XD.at(f"pre{c}", r))
                    h = hid_s[b].rearrange("p (g n) -> p g n", g=4)[:, :, 0:NCMP]
                    act.activation(h, h, ACT.Gelu_apprx_tanh).then_inc(XA.sem, 1)
                first(0)
                first(1)
                act.wait_ge(XD.sem, XD.at("cmx", r))
                act.activation(pc[:, 0:NCMP], ps[:, 6, 0:NCMP], ACT.Exp, bias=s_nm[:, 0:1], accum_out=s_sum[:, 0:1]).then_inc(XA.sem, 1)
                first(2)
                first(3)
                act.wait_ge(XD.sem, XD.at("smx", r))
                act.activation(sc_s, sc_s, ACT.Exp, bias=s_nm[:, 1:2], accum_out=s_sum[:, 1:2]).then_inc(XA.sem, 1)
                act.wait_ge(XD.sem, XD.at("wmx", r))
                act.activation(sc_w, sc_w, ACT.Exp, bias=s_nm[:, 2:3], accum_out=s_sum[:, 2:3]).then_inc(XA.sem, 1)
                act.wait_ge(XP.sem, XP.at("tc", r))
                act.activation(pt_c[0:NCMP, :], ps[0:NCMP, 6, 256:384], ACT.Copy).then_inc(XA.sem, 1)
                act.wait_ge(XP.sem, XP.at("ts2", r))
                act.activation(pt4(2), ps[:, 2, :], ACT.Copy).then_inc(XA.sem, 1)
                act.wait_ge(XP.sem, XP.at("ts3", r))
                act.activation(pt4(3), ps[:, 3, :], ACT.Copy)
                act.activation(pt_fs[0:32, :], ps[0:32, 6, 384:512], ACT.Copy).then_inc(XA.sem, 1)
                act.wait_ge(XP.sem, XP.at("tw", r))
                act.activation(pt4(4), ps[:, 5, :], ACT.Copy)
                act.activation(pt_fw[0:32, :], ps[0:32, 4, 128:256], ACT.Copy).then_inc(XA.sem, 1)

            with act.Fori(0, 4) as r:
                pair(r)
            act.wait_ge(XD.sem, XD.at("ov", 3))
            act.wait_ge(win_out, 128 * 4)
            hi(PB["out1"], 0, PB["out1"] // 4 + 1)
            for u in range(2):
                act.activation(bigs[:, ATT_H + 4 * u:ATT_H + 4 * u + 4, :], big[:, 4 * u:4 * u + 4, :], ACT.Copy).then_inc(att_hi, 1)
            hi(PB["out1"] + 1, 1, PB["out1"] // 4 + 1)

        def NSA_DVE(ve, take, lo):
            feed_in1(ve, lo, lambda i, q, scale: take("in1", i, q, scale) if q % 2 else None)
            ve.wait_ge(freed[0], SB["out1"])
            for g in range(4):
                for par in range(2):
                    src = big[64 * (g % 2):64 * (g % 2) + 64, KVR + g // 2, 0:SEQ].rearrange("p (n c r) -> p r c n", c=8, r=2)
                    op = ve.tensor_copy(c_p[64 * par:64 * par + 64, 0, :, g, :], src[:, par, :, :])
            op.then_inc(ND.sem, 1)
            ve.wait_ge(NP.sem, NP.at("gT"))
            ve.tensor_copy(gtok, ps[:, 6, 0:192].rearrange("p (q b h) -> p q b h", q=4, b=3)).then_inc(ND.sem, 1)
            ve.wait_ge(NP.sem, NP.at("grow"))
            ve.tensor_tensor(grow_m.rearrange("p b w t -> p b (w t)"), ps[:, 7, 0:96].rearrange("p (b t) -> p b t", b=3),
                             K["token_of_row"].unsqueeze(1).to_broadcast([128, 3, 32]), ALU.mult).then_inc(ND.sem, 1)
            ve.wait_ge(ND.sem, ND.at("gm"))
            ve.tensor_reduce(growv, grow_m, AX.X, ALU.add).then_inc(ND.sem, 1)
            for t in (1, 3):
                ve.wait_ge(NP.sem, NP.at(f"V{t}"))
                ve.tensor_copy(v_nat_p[:, :, t, :], ps[:, t, :].rearrange("p (v n) -> p v n", v=2)).then_inc(ND.sem, 1)
            ve.wait_ge(NP.sem, NP.at("F"))
            ve.tensor_copy(fresh_v[0:32, :, :], ps[0:32, 4, :].rearrange("p (v n) -> p v n", v=2)).then_inc(ND.sem, 1)
            for v in range(2):
                if v:
                    ve.wait_ge(NP.sem, NP.at("k2"))
                ve.wait_ge(NA.sem, NA.at(("Bk", "Bv")[v]))
                ve.tensor_tensor(hid_p[:, :, 0:31], ps[:, (6, 0)[v], 0:128].rearrange("p (g n) -> p g n", g=4)[:, :, 0:31],
                                 bs_p[:, :, 1:32], ALU.add).then_inc(ND.sem, 1)
            ve.wait_ge(NP.sem, NP.at("k2"))
            ve.tensor_copy(kcc_p[:, :, 0:31], ps[:, 2, 0:62].rearrange("p (g n) -> p g n", g=2)).then_inc(ND.sem, 1)
            ve.wait_ge(NP.sem, NP.at("v2"))
            ve.tensor_copy(vcc_p[0:31, :], ps[0:31, 3, 0:256]).then_inc(ND.sem, 1)

            for gp in range(2):
                def a(R, u):
                    qt, g2 = u // 2, u % 2
                    n = (qt + 1) * 128
                    ve.wait_ge(TP.sem, TP.at(f"s{u}", R))
                    d = ps[:, 2 * g2:2 * g2 + 2, qt * 128:n]
                    ve.tensor_tensor(d, d, K["causal"].unsqueeze(1).to_broadcast([128, 2, 128]), ALU.add).then_inc(TD.sem, 1)
                    if u >= 2:
                        ve.wait_ge(TP.sem, TP.at(f"t{u - 2}", R))
                    ve.tensor_tensor(prob[:, g2, 1024:1055], ps[:, 4, g2 * 32:g2 * 32 + 31], K["cmp_mask"][:, qt * 32:qt * 32 + 31],
                                     ALU.add).then_inc(TD.sem, 1)
                    ve.wait_ge(TD.sem, TD.at(f"dm{u}", R))
                    ve.tensor_reduce(nmax[:, g2, 1:3], ps[:, 2 * g2:2 * g2 + 2, 0:n], AX.X, ALU.max, negate=True).then_inc(TD.sem, 1)
                    ve.wait_ge(TD.sem, TD.at(f"cm{u}", R))
                    ve.tensor_reduce(nmax[:, g2, 0:1], prob[:, g2, 1024:1055], AX.X, ALU.max, negate=True).then_inc(TD.sem, 1)

                def b(R, u):
                    qt, g2 = u // 2, u % 2
                    n = (qt + 1) * 128
                    j = R - gp * 4
                    ve.wait_ge(TA.sem, TA.at(f"e{u}", R))
                    ve.reciprocal(fac[:, g2, :], rsum[:, g2, :]).then_inc(TD.sem, 1)
                    ve.wait_ge(TD.sem, TD.at(f"rc{u}", R))
                    ve.tensor_tensor(fac[:, g2, :].unsqueeze(2), fac[:, g2, :].unsqueeze(2),
                                     gtok[:, qt, :, bass.ds(gp * 8 + j * 2 + g2, 1)], ALU.mult).then_inc(TD.sem, 1)
                    ve.wait_ge(TD.sem, TD.at(f"fa{u}", R))
                    for k in range(2):
                        pr = prob[:, g2, 512 * k:512 * k + n]
                        ve.tensor_scalar(pr, pr, fac[:, g2, k + 1:k + 2], None, ALU.mult)
                    pr = prob[:, g2, 1024:1055]
                    ve.scalar_tensor_tensor(out=pr, in0=pr, scalar=fac[:, g2, 0:1], in1=K["cmp_valid"][:, qt * 32:qt * 32 + 31],
                                            op0=ALU.mult, op1=ALU.mult).then_inc(TD.sem, 1)

                def c(R, u):
                    ve.wait_ge(TP.sem, TP.at(f"t{u}", R))
                    if u:
                        ve.wait_ge(TP.sem, TP.at(f"o{u - 1}", R))
                    ve.tensor_copy(pt_p[0:31, 8, :], ps[0:31, 4, 128:256]).then_inc(TD.sem, 1)

                def round_(R):
                    a(R, 0)
                    a(R, 1)
                    b(R, 0)
                    for u in U:
                        c(R, u)
                        if u < 7:
                            b(R, u + 1)
                        if u < 6:
                            a(R, u + 2)

                with ve.Fori(0, 4) as j:
                    round_(j + gp * 4)

            def pair(r):
                def pre(c):
                    b = c % 2
                    ve.wait_ge(XA.sem, XA.at(f"B{c}", r))
                    if c >= 2:
                        ve.wait_ge(XP.sem, XP.at(f"k2{b}", r))
                    ve.tensor_tensor(hid_s[b].rearrange("p (g n) -> p g n", g=4)[:, :, 0:NCMP],
                                     ps[:, 2 * b, :].rearrange("p (g n) -> p g n", g=4)[:, :, 0:NCMP],
                                     bs_s[b].rearrange("p (g n) -> p g n", g=4)[:, :, 1:NC], ALU.add).then_inc(XD.sem, 1)

                def step(name, op):
                    op.then_inc(XD.sem, 1)
                    ve.wait_ge(XD.sem, XD.at(name, r))

                pre(0)
                pre(1)
                for b in range(2):
                    ve.wait_ge(XP.sem, XP.at("k21", r))
                    ve.tensor_copy(kcc[:, b, :, 0:NCMP], ps[:, 4, b * 256:b * 256 + 254].rearrange("p (g n) -> p g n", g=2)).then_inc(XD.sem, 1)
                ve.wait_ge(XP.sem, XP.at("sc", r))
                ve.tensor_reduce(s_nm[:, 0:1], ps[:, 6, 0:NCMP], AX.X, ALU.max, negate=True).then_inc(XD.sem, 1)
                ve.wait_ge(XA.sem, XA.at("ce", r))
                step("crc", ve.reciprocal(s_fac[:, 0:1], s_sum[:, 0:1]))
                ve.tensor_scalar(pc[:, 0:NCMP], pc[:, 0:NCMP], s_fac[:, 0:1], None, ALU.mult).then_inc(XD.sem, 1)
                pre(2)
                pre(3)
                ve.wait_ge(XP.sem, XP.at("J", r))
                step("pj", ve.tensor_copy(pj[:, 1:1 + NCMP], ps[:, 6, 128:128 + NCMP]))
                step("im", ve.tensor_reduce(score, pj[:, 0:132].rearrange("p (m n) -> p m n", n=4), AX.X, ALU.add))
                step("sc1", ve.tensor_tensor(score, score, pj[:, 4:136].rearrange("p (m n) -> p m n", n=4)[:, :, 0], ALU.add))
                step("sc2", ve.tensor_tensor(score, score, K["bonus"], ALU.add))
                other = score.unsqueeze(1).to_broadcast([128, NSLC, NSLC])
                own = score.unsqueeze(2).to_broadcast([128, NSLC, NSLC])
                step("eq", ve.tensor_tensor(cmpx, other, own, ALU.is_equal))
                step("tri", ve.tensor_tensor(cmpx, cmpx, K["earlier"].rearrange("p (m n) -> p m n", m=NSLC), ALU.mult))
                step("r1", ve.tensor_reduce(rank_a, cmpx, AX.X, ALU.add))
                step("gt", ve.tensor_tensor(cmpx, other, own, ALU.is_gt))
                step("r2", ve.tensor_reduce(rank_b, cmpx, AX.X, ALU.add))
                step("rk", ve.tensor_tensor(rank_a, rank_a, rank_b, ALU.add))
                step("mk", ve.tensor_scalar(rank_a, rank_a, TOPN - 0.5, NEG, ALU.is_gt, ALU.mult))
                step("cf", ve.tensor_copy(s_fac[:, 0:1].unsqueeze(1), growv[:, 0:1, bass.ds(r, 1)]))
                ve.tensor_scalar(pc[:, 0:NCMP], pc[:, 0:NCMP], s_fac[:, 0:1], None, ALU.mult).then_inc(XD.sem, 1)
                for b in range(2):
                    ve.wait_ge(XP.sem, XP.at("v21", r))
                    ve.tensor_copy(vcc[0:NCMP, b, :], ps[0:NCMP, 5, b * 256:b * 256 + 256]).then_inc(XD.sem, 1)
                ve.wait_ge(XP.sem, XP.at("ss1", r))
                ve.tensor_tensor(sc_s[:, 0:2048].rearrange("p (m n) -> p m n", n=64),
                                 ps[:, 0:4, :].rearrange("p k (m n) -> p (k m) n", n=64),
                                 rank_a[:, 0:32].unsqueeze(2).to_broadcast([128, 32, 64]), ALU.add).then_inc(XD.sem, 1)
                fm = K["fresh_mask"].rearrange("p (w t) -> p w t", w=4)[:, bass.ds(r, 1), :]
                step("sf", ve.tensor_tensor(sc_s[:, 2048:2080].unsqueeze(1), ps[:, 4, 0:32].unsqueeze(1), fm, ALU.add))
                ve.tensor_reduce(s_nm[:, 1:2], sc_s, AX.X, ALU.max, negate=True).then_inc(XD.sem, 1)
                ve.wait_ge(XP.sem, XP.at("ws", r))
                ve.tensor_tensor(sc_w[:, 0:32], ps[:, 5, 0:32], K["win_mask"], ALU.add)
                ve.tensor_copy(sc_w[:, 32:512], ps[:, 5, 32:512]).then_inc(XD.sem, 1)
                step("wf", ve.tensor_tensor(sc_w[:, 512:544].unsqueeze(1), ps[:, 7, 256:288].unsqueeze(1), fm, ALU.add))
                ve.tensor_reduce(s_nm[:, 2:3], sc_w, AX.X, ALU.max, negate=True).then_inc(XD.sem, 1)
                for k, (name, buf) in enumerate((("s", sc_s), ("w", sc_w))):
                    f = s_fac[:, 1 + k:2 + k]
                    ve.wait_ge(XA.sem, XA.at(name + "e", r))
                    step(name + "rc", ve.reciprocal(f, s_sum[:, 1 + k:2 + k]))
                    step(name + "fa", ve.tensor_tensor(f.unsqueeze(1), f.unsqueeze(1), growv[:, 1 + k:2 + k, bass.ds(r, 1)], ALU.mult))
                    ve.tensor_scalar(buf, buf, f, None, ALU.mult).then_inc(XD.sem, 1)
                for q in range(2):
                    ve.wait_ge(XP.sem, XP.at(f"ts{q}", r))
                    ve.tensor_copy(pt4(q), ps[:, q, :]).then_inc(XD.sem, 1)
                ve.wait_ge(XP.sem, XP.at("pv1", r))
                src = ps[:, 7, 0:128].rearrange("p (b g h j t) -> p b g h j t", b=2, g=2, h=2, j=4)
                for g in range(2):
                    for h in range(2):
                        dst = big[64 * h:64 * h + 64, 4 * g:4 * g + 4, bass.ds(SEQ + r * 8, 8)]
                        op = ve.tensor_copy(dst.rearrange("p j (b t) -> p b j t", b=2), src[64 * h:64 * h + 64, :, g, h, :, :])
                op.then_inc(XD.sem, 1)

            with ve.Fori(0, 4) as r:
                pair(r)
            lo(PB["out1"], 0, None)
            for u in range(2):
                ve.wait_ge(att_hi, u + 1)
                ve.tensor_tensor(bigs[:, ATT_L + 4 * u:ATT_L + 4 * u + 4, :], big[:, 4 * u:4 * u + 4, :],
                                 as_f32(bigs[:, ATT_H + 4 * u:ATT_H + 4 * u + 4, :]), ALU.subtract).then_inc(att_lo, 1)
            lo(PB["out1"] + 1, 1, None)

        def NSA_POOL(po, stores, hist_store):
            po.wait_ge(ln_x, 16)
            po.dma_start(w1, A["w1"]).then_inc(w1_in, 16)
            po.wait_ge(freed[0], SB["out1"])
            po.wait_ge(freed[1], SB["out1"])
            po.dma_start(A["o_kv"], big[:, KVR:KVR + 12, :]).then_inc(kv_store, 16)
            for b in range(NB):
                po.dma_start(A["o_win_k"][b, :, :, W - NT:W], big[:, KW:KW + 2, SEQ + b * NT:SEQ + b * NT + NT]).then_inc(kv_store, 16)
            po.wait_ge(ND.sem, ND.at("F"))
            for b in range(NB):
                po.dma_start(A["o_win_v"][b, W - NT:W, :], fresh_v[b * NT:b * NT + NT, 1, :]).then_inc(kv_store, 16)
            po.wait_ge(kv_store, 16 * (1 + 2 * NB))
            po.wait_ge(TA.sem, TA.at("ov", 7))
            po.wait_ge(tab_in, 16)
            po.memset(qb, 0.0).then_inc(smp_zero, 1)
            po.memset(pj, 0.0).then_inc(smp_zero, 1)
            po.wait_ge(smp_zero, 2)
            po.sem_inc(smp_zero, 1)

            def pair(r):
                prev = not (isinstance(r, int) and r == 0)
                if prev:
                    po.wait_ge(XP.sem, XP.at("pv1", r - 1))
                    po.wait_ge(win_out, 128 * r)
                for g in range(2):
                    for h in range(2):
                        src = big[64 * h:64 * h + 64, 4 * g:4 * g + 4, bass.ds(SEQ + r * 8, 8)].rearrange("p j (b t) -> p b j t", b=2)
                        c0 = g * 32 + h * 16
                        op = po.tensor_copy(qb[64 * h:64 * h + 64, :, g, c0:c0 + 16].rearrange("p b (j t) -> p b j t", j=4), src)
                op.then_inc(XQ, 1)
                for b in range(2):
                    load_pages(po, "cmp_v", 2 + b, r, b)
                for b in range(2):
                    po.dma_start(win_k[:, b, :, :], A["win_k"][bass.ds(r * 2 + b, 1), :, :, :].rearrange("a p g n -> (a p) g n")).then_inc(win_in, 16)
                    for q in range(2):
                        po.dma_start(big[:, 12 + 2 * b + q, 0:512].rearrange("p (t n) -> p t n", t=2),
                                     A["win_v"][bass.ds(r * 2 + b, 1), 2 * q:2 * q + 2, :, :].rearrange("a t p n -> p (a t) n")).then_inc(win_in, 16)
                for b in range(2):
                    po.wait_ge(XP.sem, XP.at(f"cv{b}", r))
                    po.sem_inc(turn_v, 1)
                    load_pages(po, "slc_v", 2 + b, r, b)
                po.wait_ge(win_in, 96 * (r + 1))
                po.sem_inc(turn_v, 1)
                for b in range(2):
                    po.dma_start(A["o_win_k"][bass.ds(r * 2 + b, 1), :, :, 0:W - NT].rearrange("a p g n -> (a p) g n"),
                                 win_k[:, b, :, NT:W]).then_inc(win_out, 16)
                    ov = A["o_win_v"][bass.ds(r * 2 + b, 1), :, :]
                    wv = big[:, 12 + 2 * b:14 + 2 * b, 0:512]
                    po.dma_start(ov[:, 0:124, :].rearrange("a p n -> (a p) n"), wv[NT:128, 0, 0:256]).then_inc(win_out, 16)
                    po.dma_start(ov[:, 124:252, :].rearrange("a p n -> (a p) n"), wv[:, 0, 256:512]).then_inc(win_out, 16)
                    po.dma_start(ov[:, 252:508, :].rearrange("a (t p) n -> p (a t) n", t=2),
                                 wv[:, 1, :].rearrange("p (t n) -> p t n", t=2)).then_inc(win_out, 16)

            pair(0)
            with po.Fori(1, 4) as r:
                pair(r)
            po.wait_ge(win_out, 128 * 4)
            po.wait_ge(XQ, 4)
            return stores
        block = ctx.enter_context(nc.Block())

        @block.sync
        def _(sp):

            def piece(n, s, src, size):
                if not (isinstance(n, int) and n < 4):
                    sp.wait_ge(w_lo, n - 3)
                sp.dma_start(raw[s][:, 0:size], src).then_inc(w_in[s], 16)

            def stream(name, first=False):
                w = A["w_" + name]
                count = dict((g[0], g[1]) for g in GEMMS)[name]
                if name.startswith("down"):
                    with sp.Fori(0, 2) as i:
                        for q in range(12):
                            m, part = q // 3, q % 3
                            size = (8, 8, 6)[part] * 128
                            piece(PB[name] + i * 12 + q, q % 4,
                                  w[bass.ds(i * 4 + m, 1), :, part * 1024:part * 1024 + size].rearrange("m p n -> (m p) n"), size)
                    return
                start = 0
                if first:
                    for s in range(4):
                        piece(s, s, w[s], 1024)
                        if s == 0:
                            for k in range(0, KC, 2):
                                sp.dma_start(big[:, 20 + k:22 + k, :], A["xT"][:, k:k + 2, :]).then_inc(x_in[k // 2], 16)
                    start = 1
                if name == "out1":
                    piece(PB[name], 0, w[0], 1024)
                    sp.wait_ge(XD.sem, XD.at("ov", 3))
                    for s in range(1, 4):
                        piece(PB[name] + s, s, w[s], 1024)
                    start = 1
                with sp.Fori(start, count // 4) as i:
                    for s in range(4):
                        piece(PB[name] + i * 4 + s, s, w[bass.ds(i * 4 + s, 1), :, :].rearrange("m p n -> (m p) n"), 1024)

            stream("in0", True)
            for name in ("out0", "up0", "down0"):
                stream(name)
            NSA_SP(sp, stream)
            for name in ("up1", "down1"):
                stream(name)

        @block.tensor
        def _(pe):
            def stripe(psum_set, slot, ks, rhs, start, stop, ready=None):
                for k in range(ks):
                    if ready:
                        ready(k)
                    for w_part, v_part in ((0, 0), (0, 1), (1, 0)):
                        for h in range(2):
                            mm = pe.matmul(ps[:, 2 * psum_set + h, 0:HT], split[:, slot % 2, w_part, k * 128:(k + 1) * 128],
                                           rhs(k)[v_part][:, h * HT:(h + 1) * HT],
                                           start=start and k == 0 and w_part + v_part == 0,
                                           stop=stop and k == ks - 1 and w_part == 1)
                return mm

            def product(name, rhs, ready=None):
                count = dict((g[0], g[1]) for g in GEMMS)[name]
                if name.startswith("down"):
                    layer = int(name[-1])
                    with pe.Fori(0, 2) as i:
                        for q in range(12):
                            m, part = q // 3, q % 3
                            pe.wait_ge(w_lo, PB[name] + i * 12 + (q + 1))
                            pe.wait_ge(hid_lo, FC * layer + (8, 16, FC)[part])
                            if part == 0:
                                pe.wait_ge(freed[m % 2], SB[name] + i * 2 + m // 2)
                            stripe(m % 2, q % 4, (8, 8, 6)[part], lambda k: rhs(part * 8 + k),
                                   part == 0, part == 2).then_inc(pieces, 1)
                    return

                def four(i, peeled):
                    for s in range(4):
                        pe.wait_ge(w_lo, PB[name] + i * 4 + (s + 1))
                        if not (peeled and name == "in0") or s >= 2:
                            pe.wait_ge(freed[s % 2], SB[name] + i * 2 + s // 2)
                        stripe(s % 2, s, KC, rhs, True, True, ready if peeled and s == 0 else None).then_inc(pieces, 1)

                if ready:
                    four(0, True)
                with pe.Fori(1 if ready else 0, count // 4) as i:
                    four(i, False)

            def norm_sums(r):
                pe.wait_ge(ln_sum, 8 * (r + 1))
                for h in range(2):
                    mm = pe.matmul(ps[:, 4 + h, 0:HT], K["mean_d"], ln_row(r, 0)[:, h * HT:(h + 1) * HT], start=True, stop=True)
                mm.then_inc(ln_mean, 1)
                for m in range(KC):
                    pe.wait_ge(ln_sq, 8 * r + m + 1)
                    for h in range(2):
                        mm = pe.matmul(ps[:, 6 + h, 0:HT], K["mean_d"], big[:, m, h * HT:(h + 1) * HT],
                                       start=m == 0, stop=m == KC - 1)
                mm.then_inc(ln_var, 1)

            def x_parts(k):
                return xhs[:, k, :], xls[:, k, :]

            def normed(r):
                return lambda k: pe.wait_ge(ln_x, 8 * r + k + 1)

            product("in0", x_parts, lambda k: pe.wait_ge(x0_lo, k + 1))

            pe.wait_ge(early_in, 16)
            pe.wait_ge(freed[0], 14)
            pe.wait_ge(freed[1], 14)
            for n in range(8):
                if n >= 2:
                    pe.wait_ge(RD.sem, RD.at("sin", n - 2))
                for h in range(2):
                    mm = pe.matmul(ps[:, 4 + 2 * (n % 2) + h, 0:HT], K["swap"], big[:, n, h * HT:(h + 1) * HT],
                                   start=True, stop=True)
                mm.then_inc(rope_pe, 1)

            pe.wait_ge(consts_in, 32)
            pe.wait_ge(RD.sem, RD.at("add", 7))
            for c in range(4):
                tok = slice(c * 128, c * 128 + 128)
                if c:
                    pe.wait_ge(RV.sem, RV.at("kn", c - 1))
                for h in range(RH):
                    mm = pe.transpose(ps[:, 4, h * 128:(h + 1) * 128], big[:, KZ + h, tok], K["ident"])
                mm.then_inc(RP.sem, 1)
                if c:
                    pe.wait_ge(RA.sem, RA.at("vn", c - 1))
                for h in range(RH):
                    mm = pe.transpose(ps[:, 5, h * 128:(h + 1) * 128], big[:, VZ + h, tok], K["ident"])
                mm.then_inc(RP.sem, 1)
                if c:
                    pe.wait_ge(RV.sem, RV.at("st", c - 1))
                for h in range(RH):
                    mm = pe.matmul(ps[:, 6, h * 128:(h + 1) * 128], big[:, KZ + h, tok], big[:, QZ + h, tok],
                                   start=True, stop=True)
                mm.then_inc(RP.sem, 1)
                pe.wait_ge(RV.sem, RV.at("qd", c))
                pe.wait_ge(RA.sem, RA.at("vn", c))
                if c:
                    pe.wait_ge(RA.sem, RA.at("o", c - 1))
                    pe.wait_ge(RV.sem, RV.at("state", c - 1))
                for h in range(RH):
                    hs = slice(h * 128, h * 128 + 128)
                    mm = pe.matmul(ps[:, 7, hs], v_nat[:, hs], s_dec[:, hs], start=True, stop=c == 0)
                    if c:
                        mm = pe.matmul(ps[:, 7, hs], state[:, hs], q_dec[:, hs], start=False, stop=True)
                mm.then_inc(RP.sem, 1)
                for h in range(RH):
                    hs = slice(h * 128, h * 128 + 128)
                    mm = pe.matmul(ps[:, 0, hs], k_nat[:, hs], v_nat[:, hs], start=True, stop=True)
                mm.then_inc(RP.sem, 1)

            tok = slice(SEQ, T)
            pe.wait_ge(RV.sem, RV.at("state", 3))
            pe.wait_ge(RA.sem, RA.at("o", 3))
            for h in range(RH):
                mm = pe.transpose(ps[0:32, 4, h * 128:(h + 1) * 128], big[:, KZ + h, tok], K["ident"])
            mm.then_inc(SP_.sem, 1)
            for h in range(RH):
                mm = pe.transpose(ps[0:32, 5, h * 128:(h + 1) * 128], big[:, VZ + h, tok], K["ident"])
            mm.then_inc(SP_.sem, 1)
            for h in range(RH):
                mm = pe.matmul(ps[0:32, 6, h * 32:(h + 1) * 32], big[:, KZ + h, tok], big[:, QZ + h, tok],
                               start=True, stop=True)
            mm.then_inc(SP_.sem, 1)
            pe.wait_ge(ret_in, 16)
            pe.wait_ge(SV.sem, SV.at("qd"))
            pe.wait_ge(SA.sem, SA.at("vn"))
            for h in range(RH):
                hs = slice(h * 128, h * 128 + 128)
                pe.matmul(ps[:, 7, h * 32:(h + 1) * 32], v_nat[0:32, hs], s_dec[0:32, h * 32:h * 32 + 32],
                          start=True, stop=True, skip_group_check=True)
                for b in range(NB):
                    cs = slice(h * 32 + b * NT, h * 32 + b * NT + NT)
                    mm = pe.matmul(ps[:, 7, cs], ret_states[:, b, h, :], q_dec[:, cs], start=False, stop=True,
                                   skip_group_check=True)
            mm.then_inc(SP_.sem, 1)
            for h in range(RH):
                pe.wait_ge(SV.sem, SV.at("vb") + h)
                for u in range(2):
                    n = 2 * h + u
                    if n >= 2:
                        pe.wait_ge(st_s, n - 1)
                    mm = pe.matmul(ps[:, n % 2, :], k_nat[0:32, h * 128:(h + 1) * 128], v_blk[0:32, u * 512:(u + 1) * 512],
                                   start=True, stop=True).then_inc(kv_s, 1)

            pe.wait_ge(SA.sem, SA.at("o"))
            for h in range(RH):
                s = 4
                if h:
                    pe.wait_ge(GV.sem, GV.at("cen", h - 1))
                for u in range(2):
                    mm = pe.matmul(ps[:, s + u, 0:HT], K["mean_h"], big[:, QZ + h, u * HT:(u + 1) * HT], start=True, stop=True)
                mm.then_inc(GP.sem, 1)
                pe.wait_ge(GA.sem, GA.at("sq", h))
                for u in range(2):
                    mm = pe.matmul(ps[:, s + 2 + u, 0:HT], K["mean_h"], gn_sq[:, u * HT:(u + 1) * HT], start=True, stop=True)
                mm.then_inc(GP.sem, 1)

            pe.wait_ge(mix_lo, 1 + RH)
            product("out0", lambda k: (bigs[:, MIX_H + k, :], bigs[:, MIX_L[k], :]))
            norm_sums(0)
            for layer in range(2):
                product(f"up{layer}", x_parts, normed(2 * layer))
                product(f"down{layer}", lambda k: (bigs[:, k, :], hid_l[:, k, :]))
                norm_sums(2 * layer + 1)
                if layer == 0:
                    product("in1", x_parts, normed(1))
                    NSA_PE(pe, product)
                    norm_sums(2)

        @block.scalar
        def _(act):
            act.dma_start(keep_all, A["keep"]).then_inc(consts_in, 16)
            act.dma_start(vec_all, A["vecs"]).then_inc(consts_in, 16)
            act.dma_start(early_all, A["early"]).then_inc(early_in, 16)
            act.dma_start(ret_states, A["state_ret"]).then_inc(ret_in, 16)
            act.dma_start(sconv_hist, A["state_sconv"]).then_inc(hist_in, 16)
            act.dma_start(wg, A["w_gate"].rearrange("p k n -> p (k n)")).then_inc(nsa_in, 16)
            act.dma_start(w2, A["w2"]).then_inc(nsa_in, 16)

            def hi(n, s, turn, size=1024):
                act.wait_ge(w_in[s], 16 * turn)
                if not (isinstance(n, int) and (n < 2 or n in (PB["out1"], PB["out1"] + 1))):
                    act.wait_ge(pieces, n - 1)
                act.activation(split[:, s % 2, 0, 0:size], raw[s][:, 0:size], ACT.Copy).then_inc(w_hi, 1)

            def take_even(name, i, s, scale=1.0):
                act.wait_ge(pieces, PB[name] + i * 4 + (s + 1))
                act.activation(half2(big[:, bass.ds(i * 4 + s, 1), :]), pset(0), ACT.Copy, scale=scale).then_inc(freed[0], 1)

            def half2(v):
                return v.rearrange("p a (h t) -> p (a h) t", h=2)

            hi(0, 0, 1)
            for k in range(KC):
                act.wait_ge(x_in[k // 2], 16)
                act.activation(xhs[:, k, :], big[:, 20 + k, :], ACT.Copy).then_inc(x0_hi, 1)
            hi(1, 1, 1)
            feed(act, hi, "in0", lambda i, q: take_even("in0", i, q) if q % 2 == 0 else None)
            act.wait_ge(nsa_in, 32)
            act.activation(wg_h.rearrange("p k n -> p (k n)"), wg, ACT.Copy).then_inc(wg_hi, 1)
            for c in range(4):
                tok = slice(c * 128, c * 128 + 128)
                act.wait_ge(RP.sem, RP.at("vT", c))
                if c:
                    act.wait_ge(RP.sem, RP.at("kv", c - 1))
                act.activation(v_nat[:, :], ps[:, 5, :], ACT.Copy).then_inc(RA.sem, 1)
                act.wait_ge(RP.sem, RP.at("o", c))
                act.activation(big[:, QZ:QZ + 4, tok], ps[:, 7, :].rearrange("p (h n) -> p h n", h=4), ACT.Copy).then_inc(RA.sem, 1)
            act.wait_ge(SP_.sem, SP_.at("vT"))
            act.wait_ge(RP.sem, RP.at("kv", 3))
            act.activation(v_nat[0:32, :], ps[0:32, 5, :], ACT.Copy).then_inc(SA.sem, 1)
            act.wait_ge(SP_.sem, SP_.at("o"))
            act.activation(big[:, QZ:QZ + 4, SEQ:T], ps[:, 7, 0:128].rearrange("p (h n) -> p h n", h=4), ACT.Copy).then_inc(SA.sem, 1)
            act.wait_ge(freed[1], 14)
            act.wait_ge(RP.sem, RP.at("kv", 3))
            act.activation(big[:, GZ:GZ + 4, :], big[:, GZ:GZ + 4, :], ACT.Silu).then_inc(gn_gate, 1)
            act.wait_ge(ya.sem, ya.at("ys", 3))
            act.activation(bigs[:, MIX_H:MIX_H + 4, :], big[:, HZ:HZ + 4, :], ACT.Copy).then_inc(mix_hi, 1)
            act.wait_ge(pool_set, 1)

            def head_hi(h):
                act.wait_ge(GV.sem, GV.at("mul", h))
                act.activation(bigs[:, MIX_H + 4 + h, :], big[:, QZ + h, :], ACT.Copy).then_inc(mix_hi, 1)

            for h in range(RH):
                act.wait_ge(GV.sem, GV.at("cen", h))
                if h:
                    act.wait_ge(GP.sem, GP.at("var", h - 1))
                act.activation(gn_sq[:, :], big[:, QZ + h, :], ACT.Square).then_inc(GA.sem, 1)
                if h:
                    head_hi(h - 1)
                act.wait_ge(GP.sem, GP.at("var", h))
                if h:
                    act.wait_ge(GV.sem, GV.at("nrm", h - 1))
                act.activation(half(gn_sd[:, :]), ps[:, 6:8, 0:HT], ACT.Sqrt, bias=eps[:, 0:1]).then_inc(GA.sem, 1)
            head_hi(RH - 1)

            def norm(r):
                for m in range(KC):
                    act.wait_ge(ln_cen, 8 * r + m + 1)
                    act.activation(big[:, m, :], y[:, m, :], ACT.Square).then_inc(ln_sq, 1)
                act.wait_ge(ln_var, r + 1)
                act.activation(half(ln_row(r, 1)), ps[:, 6:8, 0:HT], ACT.Sqrt, bias=eps[:, 0:1]).then_inc(ln_std, 1)
                for m in range(KC):
                    g, b = (K[v][:, 8 * r + m:8 * r + m + 1] for v in ("ln_g", "ln_b"))
                    act.wait_ge(ln_nrm, 8 * r + m + 1)
                    op = act.activation(big[:, m, :], y[:, m, :], ACT.Identity, scale=g, bias=b)
                    if r < 3:
                        op = act.activation(xhs[:, m, :], y[:, m, :], ACT.Identity, scale=g, bias=b)
                    op.then_inc(ln_hi, 1)

            def ffn(layer):
                name = f"up{layer}"
                base = layer * FC

                def row(jb, u, peeled):
                    j = jb * 2 + u
                    hi(PB[name] + jb * 4 + (2 * u + 2), (2 * u + 2) % 4, PB[name] // 4 + jb + (1 + (u + 1) // 2))
                    if not peeled:
                        act.wait_ge(fd.sem, fd.at("c2", j + base - 2))
                        act.wait_ge(fp.sem, fp.at("out", j + base - 2))
                    act.activation(ffn_a[:, u, 2:2 + HT], ps[:, 0, 0:HT], ACT.Copy)
                    act.activation(ffn_a[:, u, 2 + HT:SO], ps[:, 1, 0:SEQ - HT], ACT.Copy)
                    act.activation(ffn_a[:, u, SO:CW].rearrange("p (b w) -> p b w", b=NB)[:, :, 2:6],
                                   ps[:, 1, SEQ - HT:HT].rearrange("p (b w) -> p b w", b=NB), ACT.Copy).then_inc(freed[0], 1)

                def gelu(jb, u, peeled):
                    j = jb * 2 + u
                    act.wait_ge(fd.sem, fd.at("c2", j + base))
                    if not peeled:
                        act.wait_ge(freed[1], SB[name] + j - 1)
                    act.activation(ffn_g[:, u, 0:SEQ], ffn_c[:, u, 0:SEQ], ACT.Gelu_apprx_tanh)
                    act.activation(ffn_g[:, u, SEQ:T].rearrange("p (b w) -> p b w", b=NB),
                                   conv_sample(ffn_c[:, u, :]),
                                   ACT.Gelu_apprx_tanh).then_inc(fa.sem, 1)
                    hi(PB[name] + jb * 4 + (2 * u + 3), (2 * u + 3) % 4, PB[name] // 4 + jb + (1 + (u + 1) // 2))
                    act.wait_ge(freed[1], SB[name] + j + 1)
                    act.activation(bigs[:, bass.ds(j, 1), :], big[:, 22 + u:23 + u, :], ACT.Copy).then_inc(hid_hi, 1)

                row(0, 0, True)
                gelu(0, 0, True)
                row(0, 1, True)
                gelu(0, 1, True)
                with act.Fori(1, FC // 2) as jb:
                    row(jb, 0, False)
                    gelu(jb, 0, False)
                    row(jb, 1, False)
                    gelu(jb, 1, False)

            feed(act, hi, "out0", None)
            norm(0)
            ffn(0)
            feed(act, hi, "down0", None)
            norm(1)
            NSA_ACT(act, take_even, hi)
            feed(act, hi, "out1", None)
            norm(2)
            ffn(1)
            feed(act, hi, "down1", None, True)
            norm(3)
            act.wait_ge(ln_hi, 32)
            act.dma_start(A["o_x"], big[:, 0:KC, :]).then_inc(out_done, 16)
            act.wait_ge(out_done, 16)

        @block.vector
        def _(ve):
            def lo(n, s, turn, size=1024):
                ve.wait_ge(w_hi, n + 1)
                ve.tensor_tensor(split[:, s % 2, 1, 0:size], raw[s][:, 0:size], as_f32(split[:, s % 2, 0, 0:size]),
                                 ALU.subtract).then_inc(w_lo, 1)

            def take_odd(name, i, s, scale=None):
                ve.wait_ge(pieces, PB[name] + i * 4 + (s + 1))
                dst = big[:, bass.ds(i * 4 + s, 1), :].rearrange("p a (h t) -> p (a h) t", h=2)
                if scale is None:
                    ve.tensor_copy(dst, pset(1)).then_inc(freed[1], 1)
                else:
                    ve.tensor_scalar(dst, pset(1), scale, None, ALU.mult).then_inc(freed[1], 1)

            lo(0, 0, 1)
            for k in range(KC):
                ve.wait_ge(x0_hi, k + 1)
                ve.tensor_tensor(xls[:, k, :], big[:, 20 + k, :], as_f32(xhs[:, k, :]), ALU.subtract).then_inc(x0_lo, 1)
            lo(1, 1, 1)
            feed(ve, lo, "in0", lambda i, q: take_odd("in0", i, q) if q % 2 else None)
            ve.wait_ge(early_in, 16)
            ve.wait_ge(freed[0], 14)
            for n in range(8):
                ve.wait_ge(rope_pe, n + 1)
                if n:
                    ve.wait_ge(RD.sem, RD.at("add", n - 1))
                ve.tensor_tensor(half(rope_t), ps[:, 4 + 2 * (n % 2):6 + 2 * (n % 2), 0:HT], half(K["rope_sin"]),
                                 ALU.mult).then_inc(RD.sem, 1)
                ve.tensor_tensor(big[:, n, :], big[:, n, :], K["rope_cos"], ALU.mult).then_inc(RD.sem, 1)
                ve.wait_ge(RD.sem, RD.at("cos", n))
                ve.tensor_tensor(big[:, n, :], big[:, n, :], rope_t, ALU.add).then_inc(RD.sem, 1)
            ve.wait_ge(RD.sem, RD.at("add", 7))
            gam = np.exp(128 * np.log1p(-np.exp2(-5.0 - np.arange(RH))))
            gam4 = np.exp(NT * np.log1p(-np.exp2(-5.0 - np.arange(RH))))

            def by_head(v, n=128):
                return v.rearrange("p (h n) -> p h n", h=RH)

            for c in range(4):
                tok = slice(c * 128, c * 128 + 128)
                ve.wait_ge(RP.sem, RP.at("kT", c))
                if c:
                    ve.wait_ge(RP.sem, RP.at("kv", c - 1))
                ve.tensor_tensor(by_head(k_nat), by_head(ps[:, 4, :]),
                                 K["kdec"].unsqueeze(2).to_broadcast([128, RH, 128]), ALU.mult).then_inc(RV.sem, 1)
                ve.wait_ge(RP.sem, RP.at("sc", c))
                ve.tensor_tensor(s_dec, ps[:, 6, :], K["decay"], ALU.mult).then_inc(RV.sem, 1)
                ve.tensor_tensor(by_head(q_dec), big[:, QZ:QZ + 4, tok], by_head(K["qdec"]), ALU.mult).then_inc(RV.sem, 1)
                ve.wait_ge(RP.sem, RP.at("kv", c))
                if c == 0:
                    ve.tensor_copy(state, ps[:, 0, :]).then_inc(RV.sem, 1)
                else:
                    ve.wait_ge(RV.sem, RV.at("state", c - 1))
                    for h in range(RH):
                        hs = slice(h * 128, h * 128 + 128)
                        op = ve.scalar_tensor_tensor(out=state[:, hs], in0=state[:, hs], scalar=float(gam[h]),
                                                     in1=ps[:, 0, hs], op0=ALU.mult, op1=ALU.add)
                    op.then_inc(RV.sem, 1)
            ve.wait_ge(SP_.sem, SP_.at("kT"))
            ve.tensor_tensor(k_nat[0:32, :].rearrange("p (h n) -> p h n", h=RH), ps[0:32, 4, :].rearrange("p (h n) -> p h n", h=RH),
                             K["kdec_s"][0:32, :].unsqueeze(2).to_broadcast([32, RH, 128]), ALU.mult).then_inc(SV.sem, 1)
            ve.wait_ge(SP_.sem, SP_.at("sc"))
            ve.tensor_tensor(s_dec[0:32, 0:128], ps[0:32, 6, 0:128], K["decay_s"][0:32, :], ALU.mult).then_inc(SV.sem, 1)
            ve.tensor_tensor(q_dec[:, 0:128].rearrange("p (h n) -> p h n", h=RH), big[:, QZ:QZ + 4, SEQ:T],
                             K["qdec_s"].rearrange("p (h n) -> p h n", h=RH), ALU.mult).then_inc(SV.sem, 1)
            ve.wait_ge(SA.sem, SA.at("vn"))
            for h in range(RH):
                if h:
                    ve.wait_ge(kv_s, 2 * h)
                ve.tensor_tensor(v_blk[0:32, :].rearrange("p (b e) -> p b e", b=NB),
                                 v_nat[0:32, h * 128:(h + 1) * 128].unsqueeze(1).to_broadcast([32, NB, 128]),
                                 K["seq_of"][0:32, :].unsqueeze(2).to_broadcast([32, NB, 128]), ALU.mult).then_inc(SV.sem, 1)
                for u in range(2):
                    ve.wait_ge(kv_s, 2 * h + u + 1)
                    ve.wait_ge(SP_.sem, SP_.at("o"))
                    st = ret_states[:, 4 * u:4 * u + 4, h, :]
                    ve.scalar_tensor_tensor(out=st, in0=st, scalar=float(gam4[h]),
                                            in1=ps[:, (2 * h + u) % 2, :].rearrange("p (b e) -> p b e", b=4),
                                            op0=ALU.mult, op1=ALU.add).then_inc(st_s, 1)
            ve.wait_ge(mix_hi, 1)
            ve.tensor_tensor(bigs[:, MIX_L[0]:MIX_L[3] + 1, :], big[:, HZ:HZ + 4, :], as_f32(bigs[:, MIX_H:MIX_H + 4, :]),
                             ALU.subtract).then_inc(mix_lo, 1)
            ve.wait_ge(wg_hi, 1)
            ve.tensor_tensor(wg_l.rearrange("p k n -> p (k n)"), wg, as_f32(wg_h.rearrange("p k n -> p (k n)")), ALU.subtract).then_inc(wg_lo, 1)

            def head_lo(h):
                ve.wait_ge(mix_hi, 2 + h)
                ve.tensor_tensor(bigs[:, MIX_L[4 + h], :], big[:, QZ + h, :], as_f32(bigs[:, MIX_H + 4 + h, :]),
                                 ALU.subtract).then_inc(mix_lo, 1)

            for h in range(RH):
                o = big[:, QZ + h, :]
                ve.wait_ge(GP.sem, GP.at("mean", h))
                ve.tensor_tensor(half(o), half(o), ps[:, 4:6, 0:HT], ALU.subtract).then_inc(GV.sem, 1)
                if h:
                    head_lo(h - 1)
                ve.wait_ge(GA.sem, GA.at("std", h))
                ve.reciprocal(gn_sd, gn_sd).then_inc(GV.sem, 1)
                ve.wait_ge(GV.sem, GV.at("rs", h))
                ve.tensor_tensor(o, o, gn_sd, ALU.mult).then_inc(GV.sem, 1)
                ve.wait_ge(GV.sem, GV.at("nrm", h))
                ve.wait_ge(consts_in, 32)
                ve.tensor_scalar(o, o, K["gn_g"][:, h:h + 1], None, ALU.mult).then_inc(GV.sem, 1)
                ve.wait_ge(GV.sem, GV.at("gn", h))
                ve.wait_ge(gn_gate, 1)
                ve.tensor_tensor(o, o, big[:, GZ + h, :], ALU.mult).then_inc(GV.sem, 1)
            head_lo(RH - 1)

            def residual(name, stop=False):
                pp = 3 if name.startswith("down") else 1

                def take(i, q):
                    if q % pp != pp - 1:
                        return
                    m = q // pp
                    ve.wait_ge(pieces, PB[name] + i * 4 * pp + (q + 1))
                    row, rh, rl = (v[:, bass.ds(i * 4 + m, 1), :] for v in (y, xhs, xls))
                    ve.scalar_tensor_tensor(out=half1(row), in0=half1(as_f32(rh)), scalar=float(ALPHA), in1=pset(m % 2),
                                            op0=ALU.mult, op1=ALU.add).then_inc(freed[m % 2], 1)
                    ve.wait_ge(freed[m % 2], SB[name] + i * 2 + (m // 2 + 1))
                    ve.scalar_tensor_tensor(out=row, in0=as_f32(rl), scalar=float(ALPHA), in1=row,
                                            op0=ALU.mult, op1=ALU.add).then_inc(y_done, 1)

                feed(ve, lo, name, take, stop)

            def norm(r, name):
                residual(name, r == 3)
                ve.wait_ge(ln_mean, r + 1)
                for m in range(KC):
                    ve.tensor_tensor(half(y[:, m, :]), half(y[:, m, :]), ps[:, 4:6, 0:HT], ALU.subtract).then_inc(ln_cen, 1)
                ve.wait_ge(ln_std, r + 1)
                ve.reciprocal(ln_row(r, 1), ln_row(r, 1)).then_inc(ln_rs, 1)
                ve.wait_ge(ln_rs, r + 1)
                ve.wait_ge(ln_sq, 8 * r + 8)
                for m in range(KC + 1):
                    if m < KC:
                        ve.tensor_tensor(y[:, m, :], y[:, m, :], ln_row(r, 1), ALU.mult).then_inc(ln_nrm, 1)
                    if m and r < 3:
                        ve.wait_ge(ln_hi, 8 * r + m)
                        ve.tensor_tensor(xls[:, m - 1, :], big[:, m - 1, :], as_f32(xhs[:, m - 1, :]), ALU.subtract).then_inc(ln_x, 1)

            def ffn(layer):
                name = f"up{layer}"
                base = layer * FC
                cw = K["fconv"].rearrange("p (l c w) -> p l c w", l=2, c=FC)[:, layer, :, :]

                def row(jb, u, peeled):
                    j = jb * 2 + u
                    a, c = ffn_a[:, u, :], ffn_c[:, u, 0:CO]
                    w = cw[:, bass.ds(j, 1), :].rearrange("p a w -> p (a w)")
                    lo(PB[name] + jb * 4 + (2 * u + 2), (2 * u + 2) % 4, None)
                    ve.wait_ge(freed[0], SB[name] + j + 1)
                    ve.wait_ge(fp.sem, fp.at("in", j + base))
                    if not peeled:
                        ve.wait_ge(fa.sem, j + base - 1)
                    ve.tensor_scalar(c, a[:, 0:CO], w[:, 0:1], w[:, 3:4], ALU.mult, ALU.add).then_inc(fd.sem, 1)
                    for q in (1, 2):
                        ve.wait_ge(fd.sem, fd.at(f"c{q - 1}", j + base))
                        ve.scalar_tensor_tensor(out=c, in0=a[:, q:q + CO], scalar=w[:, q:q + 1], in1=c,
                                                op0=ALU.mult, op1=ALU.add).then_inc(fd.sem, 1)
                    lo(PB[name] + jb * 4 + (2 * u + 3), (2 * u + 3) % 4, None)
                    ve.wait_ge(pieces, PB[name] + jb * 4 + (2 * u + 2))
                    ve.wait_ge(fa.sem, j + base + 1)
                    h = big[:, 22 + u, :]
                    ve.tensor_tensor(half(h), half(ffn_g[:, u, :]), pset(1), ALU.mult).then_inc(freed[1], 1)
                    ve.wait_ge(hid_hi, j + base + 1)
                    ve.tensor_tensor(hid_l[:, bass.ds(j, 1), :], h.unsqueeze(1), as_f32(bigs[:, bass.ds(j, 1), :]),
                                     ALU.subtract).then_inc(hid_lo, 1)

                row(0, 0, True)
                row(0, 1, True)
                with ve.Fori(1, FC // 2) as jb:
                    row(jb, 0, False)
                    row(jb, 1, False)

            norm(0, "out0")
            ffn(0)
            ve.wait_ge(hist_store, 16 * 4)
            norm(1, "down0")
            NSA_DVE(ve, take_odd, lo)
            norm(2, "out1")
            ffn(1)
            ve.wait_ge(hist_store, 16 * 5)
            norm(3, "down1")

        @block.gpsimd
        def _(po):
            po.memset(eps, EPS).then_inc(pool_set, 1)
            po.memset(conv_u, 0.0).then_inc(zero_u, 1)
            po.wait_ge(zero_u, 1)
            po.wait_ge(hist_in, 16)
            po.wait_ge(consts_in, 32)
            sw = K["sconv"].rearrange("p (c w) -> p c w", c=4)
            us = conv_u[:, SO:CW].rearrange("p (b w) -> p b w", b=NB)
            for c in range(4):
                C_, H_, B_ = big[:, CZ + c, :], big[:, HZ + c, :], big[:, BZ + c, :]

                def sample(v):
                    return v[:, SEQ:T].rearrange("p (b w) -> p b w", b=NB)
                if c:
                    po.wait_ge(ya.sem, ya.at("ys", c - 1))
                po.tensor_copy(us[:, :, 0:2], sconv_hist[:, c, :, :]).then_inc(ya.sem, 1)
                po.wait_ge(freed[0], 14)
                po.wait_ge(freed[1], 14)
                po.tensor_tensor(conv_u[:, 2:SO], C_[:, 0:SEQ], H_[:, 0:SEQ], ALU.mult).then_inc(ya.sem, 1)
                po.tensor_tensor(us[:, :, 2:6], sample(C_), sample(H_), ALU.mult).then_inc(ya.sem, 1)
                po.wait_ge(ya.sem, ya.at("us", c))
                po.tensor_scalar(conv_c[:, 0:CO], conv_u[:, 0:CO], sw[:, c, 0:1], sw[:, c, 3:4], ALU.mult, ALU.add).then_inc(ya.sem, 1)
                for q in (1, 2):
                    po.tensor_scalar(conv_d, conv_u[:, q:q + CO], sw[:, c, q:q + 1], None, ALU.mult).then_inc(ya.sem, 1)
                    po.wait_ge(ya.sem, ya.at(f"t{q}", c))
                    po.tensor_tensor(conv_c[:, 0:CO], conv_c[:, 0:CO], conv_d, ALU.add).then_inc(ya.sem, 1)
                    po.wait_ge(ya.sem, ya.at(f"s{q}", c))
                po.tensor_copy(sconv_out[:, c, 0:2], conv_u[:, SEQ:SEQ + 2])
                po.tensor_copy(sconv_out[:, c, 2:18].rearrange("p (b w) -> p b w", b=NB), us[:, :, 4:6]).then_inc(ya.sem, 1)
                po.tensor_tensor(H_[:, 0:SEQ], conv_c[:, 0:SEQ], B_[:, 0:SEQ], ALU.mult).then_inc(ya.sem, 1)
                po.tensor_tensor(sample(H_), conv_sample(conv_c), sample(B_), ALU.mult).then_inc(ya.sem, 1)
            po.wait_ge(ya.sem, ya.at("ys", 3))
            po.dma_start(A["o_sconv"], sconv_out).then_inc(hist_store, 16)
            po.wait_ge(RV.sem, RV.at("state", 3))
            po.dma_start(A["o_ret_p"], state).then_inc(hist_store, 16)
            po.wait_ge(st_s, 8)
            po.dma_start(A["o_ret_s"], ret_states).then_inc(hist_store, 16)
            stores = 3

            def sums(r, name, stores):
                po.wait_ge(hist_store, 16 * stores)
                if r:
                    po.wait_ge(ln_mean, r)
                po.wait_ge(pieces, PB[name] + 1)
                po.memset(ln_row(r, 0), 0.0).then_inc(ln_zero, 1)
                po.wait_ge(ln_zero, r + 1)
                for m in range(KC):
                    po.wait_ge(y_done, 8 * r + m + 1)
                    if m:
                        po.wait_ge(ln_sum, 8 * r + m)
                    po.tensor_tensor(ln_row(r, 0), ln_row(r, 0), y[:, m, :], ALU.add).then_inc(ln_sum, 1)

            def ffn(layer, stores):
                name = f"up{layer}"
                base = layer * FC
                po.wait_ge(hist_store, 16 * stores)
                po.wait_ge(ln_x, 8 * (2 * layer + 1))
                po.memset(ffn_a[:, 0, 0:2], 0.0).then_inc(ffn_zero, 1)
                po.memset(ffn_a[:, 1, 0:2], 0.0).then_inc(ffn_zero, 1)
                po.dma_start(ffn_hist, A["state_ffn"][layer]).then_inc(hist_load, 16)
                po.wait_ge(ffn_zero, 2 * layer + 2)
                po.wait_ge(hist_load, 16 * (layer + 1))

                def row(jb, u, peeled):
                    j = jb * 2 + u
                    s = ffn_a[:, u, SO:CW].rearrange("p (b w) -> p b w", b=NB)
                    if not peeled:
                        po.wait_ge(fd.sem, fd.at("c2", j + base - 2))
                        po.wait_ge(fp.sem, fp.at("out", j + base - 2))
                    po.tensor_copy(s[:, :, 0:2], ffn_hist[:, bass.ds(j, 1), :, :].rearrange("p a b w -> p (a b) w")).then_inc(fp.sem, 1)
                    po.wait_ge(freed[0], SB[name] + j + 1)
                    fo = ffn_out[:, bass.ds(j, 1), :]
                    po.tensor_copy(fo[:, :, 0:2].rearrange("p a w -> p (a w)"), ffn_a[:, u, SEQ:SEQ + 2])
                    po.tensor_copy(fo[:, :, 2:18].rearrange("p a (b w) -> p (a b) w", b=NB), s[:, :, 4:6]).then_inc(fp.sem, 1)

                row(0, 0, True)
                row(0, 1, True)
                with po.Fori(1, FC // 2) as jb:
                    row(jb, 0, False)
                    row(jb, 1, False)
                po.wait_ge(fp.sem, fp.at("out", base + FC - 1))
                po.dma_start(A["o_ffn"][layer], ffn_out).then_inc(hist_store, 16)
                return stores + 1

            sums(0, "out0", stores)
            stores = ffn(0, stores)
            sums(1, "down0", stores)
            stores = NSA_POOL(po, stores, hist_store)
            sums(2, "out1", stores)
            stores = ffn(1, stores)
            sums(3, "down1", stores)
            po.wait_ge(hist_store, 16 * stores)


OUTS = {
    "o_x": (128, KC, T), "o_sconv": (128, 4, 18), "o_ret_p": (128, RH * 128), "o_ret_s": (128, NB, RH, 128),
    "o_ffn": (2, 128, FC, 18),
    "o_kv": (128, 12, T), "o_win_k": (NB, 128, 2, W), "o_win_v": (NB, W, 256),
}


def pieces_of(w):
    k, n = w.shape
    return np.ascontiguousarray(w.reshape(k // 128, 128, n // 128, 128).transpose(2, 1, 0, 3)).reshape(n // 128, 128, k)


def by_part(v):
    f = v.shape[-1]
    u = v.reshape(v.shape[:-1] + (f // 128, 128))
    return np.moveaxis(u, -1, 0)


def kernel(**inputs):
    import concourse.bacc as bacc
    from concourse.bass_utils import run_bass_kernel_spmd

    I = {k: np.asarray(v) for k, v in inputs.items()}
    A = {}
    xs = np.concatenate([I["x_prompt"][0], I["x_sample"].reshape(NS, D)])
    A["xT"] = xs.T.reshape(KC, 128, T).transpose(1, 0, 2)
    we = I["w_in_even"][0]
    h, b, c, q, k, v, g = (we[:, 512 * n:512 * n + 512] for n in range(7))
    A["w_in0"] = pieces_of(np.concatenate([q, k, v, g, c, h, b], 1))
    A["w_out0"] = pieces_of(I["w_out_even"][0])
    for l in range(2):
        up = I["ffn_w_up"][l].reshape(D, 2, FC, 128).transpose(0, 2, 1, 3).reshape(D, 2 * DFF)
        A[f"w_up{l}"] = pieces_of(up)
        A[f"w_down{l}"] = pieces_of(I["ffn_w_down"][l])
    wo = I["w_in_odd"][0]

    def heads(w, axis):
        s = w.shape
        if axis == 1:
            return w.reshape(s[0], 2, 2, 4, -1).transpose(0, 1, 3, 2, 4).reshape(s)
        return w.reshape(2, 2, 4, -1, s[1]).transpose(0, 2, 1, 3, 4).reshape(s)

    A["w_in1"] = pieces_of(np.concatenate([heads(wo[:, 0:1024], 1), wo[:, 1024:2560]], 1))
    gates = wo[:, 2560:2608].reshape(D, 3, 2, 2, 4).transpose(0, 1, 2, 4, 3).reshape(D, 48)
    A["w_gate"] = gates.reshape(KC, 128, 48).transpose(1, 0, 2)
    A["w_out1"] = pieces_of(heads(I["w_out_odd"][0], 0))
    A["w1"] = I["cmp_w1"][0].reshape(2, 16, 128, 128).transpose(2, 0, 1, 3).reshape(128, 2, 2048)
    A["w2"] = I["cmp_w2"][0].transpose(1, 0, 2)
    A["state_ret"] = I["state_ret"][0].transpose(2, 0, 1, 3)
    A["state_sconv"] = I["state_sconv"][0].reshape(NB, 2, 4, 128).transpose(3, 2, 0, 1)
    A["state_ffn"] = I["state_ffn_conv"].reshape(2, NB, 2, FC, 128).transpose(0, 4, 3, 1, 2)
    A["keep"] = np.concatenate([CONSTS[k] for k in KEEP], 1)
    A["early"] = np.concatenate([CONSTS[k] for k in EARLY], 1)
    sconv = np.concatenate([I["sconv_w"][0], I["sconv_b"]], 0)
    fconv = np.concatenate([I["ffn_conv_w"], I["ffn_conv_b"][:, None]], 1)
    ln_g = np.stack([I["ln_mix_g"][0], I["ln_ffn_g"][0], I["ln_mix_g"][1], I["ln_ffn_g"][1]])
    ln_b = np.stack([I["ln_mix_b"][0], I["ln_ffn_b"][0], I["ln_mix_b"][1], I["ln_ffn_b"][1]])
    vecs = [by_part(sconv).transpose(0, 2, 1), by_part(I["ret_gn_g"][0]), by_part(ln_g), by_part(ln_b),
            by_part(fconv).transpose(0, 1, 3, 2), I["cmp_pe"][0].reshape(2, 16, 128).transpose(2, 0, 1)]
    A["vecs"] = np.concatenate([v.reshape(128, -1) for v in vecs], 1)
    pages_k = I["cache_cmp_k"][0], I["cache_cmp_v"][0]
    for n, p in zip(("cmp_k", "cmp_v"), pages_k):
        A[n] = p.reshape(NPHYS, 8, 8, 2, 4, 64).transpose(0, 3, 5, 2, 4, 1).reshape(NPHYS, 128, 256)
    A["slc_k"] = I["cache_slc_k"][0].reshape(NPHYS, 128, 2, 128).transpose(0, 3, 2, 1).reshape(NPHYS, 128, 256)
    A["slc_v"] = I["cache_slc_v"][0].reshape(NPHYS, 128, 256)
    A["win_k"] = I["cache_win_k"][0].reshape(NB, W, 2, 128).transpose(0, 3, 2, 1)
    A["win_v"] = I["cache_win_v"][0].reshape(NB, 4, 128, 256)
    A["page_table"] = I["page_table"].reshape(1, NB * NPG)

    nc = bacc.Bacc("TRN2", target_bir_lowering=False, num_devices=1)
    arrays, aps = {}, {}
    for name, a in A.items():
        a = np.ascontiguousarray(a)
        arrays["in_" + name] = a
        aps[name] = nc.dram_tensor("in_" + name, a.shape, mybir.dt.from_np(a.dtype), kind="ExternalInput").ap()
    for name, shape in OUTS.items():
        aps[name] = nc.dram_tensor("out_" + name, shape, F32, kind="ExternalOutput").ap()
    build(nc, aps)
    R = run_bass_kernel_spmd(nc, [arrays], core_ids=[0]).results[0]
    R = {n: np.asarray(R["out_" + n]) for n in OUTS}

    yT = R["o_x"].transpose(2, 1, 0).reshape(T, D)

    def conv_states(v, n):
        rows = v.transpose(2, 1, 0).reshape(18, n)
        return rows[0:2][None], rows[2:18].reshape(NB, 2, n)

    sp_, ss = conv_states(R["o_sconv"], 512)
    ret_p = R["o_ret_p"].reshape(128, RH, 128).transpose(1, 0, 2)[None]
    ret_s = R["o_ret_s"].transpose(1, 2, 0, 3)
    ff = [conv_states(R["o_ffn"][l], DFF) for l in range(2)]
    kvT = R["o_kv"].transpose(2, 1, 0).reshape(T, 6, 4, 64)
    p = [kvT[:SEQ, n][None, None] for n in range(6)]
    s = [kvT[SEQ:, n].reshape(1, NB, NT, 4, 64) for n in range(6)]
    wk = R["o_win_k"].transpose(0, 3, 2, 1).reshape(1, NB, W, 4, 64)
    wv = R["o_win_v"].reshape(1, NB, W, 4, 64)
    out = [yT[None, :SEQ], yT[SEQ:].reshape(NB, NT, D), sp_[None], ss[None], ret_p[None], ret_s[None],
           p[0], p[1], p[2], p[3], s[0], s[1], s[2], s[3], p[4], p[5], wk, wv,
           np.stack([ff[0][0], ff[1][0]]), np.stack([ff[0][1], ff[1][1]])]
    return tuple(np.ascontiguousarray(o) for o in out)
```

```python
from contextlib import ExitStack

import numpy as np
import concourse.bass as bass
from concourse import mybir

F32 = mybir.dt.float32
F32R = mybir.dt.float32r
I32 = mybir.dt.int32
ALU = mybir.AluOpType
ACT = mybir.ActivationFunctionType
AX = mybir.AxisListType

MAP = 53080
D = 1024
SEQ, NB, NT = 512, 8, 4
NS = NB * NT
T = SEQ + NS
HT = T // 2
KC = D // 128
DFF = 2816
FC = DFF // 128
RH = 4
PAST, PAGE = 2048, 128
NPG = PAST // PAGE
NPHYS = 160
NC = PAST // 16
NCMP = NC - 1
NCP = SEQ // 16
NSLC = 33
TOPN = 16
W = 512
NEG = -1e30
ALPHA = 4.0 ** 0.25
EPS = 1e-5
CW = 2 + SEQ + NB * (2 + NT)
CO = CW - 2
SO = SEQ + 2

GEMMS = [("in0", 28, 28), ("out0", 8, 8), ("up0", 44, 44), ("down0", 24, 8),
         ("in1", 20, 20), ("out1", 8, 8), ("up1", 44, 44), ("down1", 24, 8)]
PB, SB = {}, {}
_p = _s = 0
for _n, _a, _b in GEMMS:
    PB[_n], SB[_n] = _p, _s // 2
    _p += _a
    _s += _b


class Steps:

    def __init__(self, sem, names):
        self.sem, self.n = sem, len(names)
        self.index = {name: k for k, name in enumerate(names)}

    def at(self, name, r=0):
        return r * self.n + (self.index[name] + 1)


def layout_consts():
    c = {}
    c["ident"] = np.eye(128)
    c["mean_d"] = np.full((128, 128), 1.0 / D)
    c["mean_h"] = np.full((128, 128), 1.0 / 128)
    pos = np.concatenate([np.arange(SEQ), np.tile(PAST + np.arange(NT), NB)]).astype(np.float32)
    inv = (np.float32(10000.0) ** (-np.arange(64, dtype=np.float32) / np.float32(64))).astype(np.float32)
    ang = (pos[None, :] * inv[:, None]).astype(np.float32).astype(np.float64)
    c["rope_cos"] = np.concatenate([np.cos(ang)] * 2)
    c["rope_sin"] = np.concatenate([-np.sin(ang), np.sin(ang)])
    swap = np.zeros((128, 128))
    swap[(np.arange(128) + 64) % 128, np.arange(128)] = 1.0
    c["swap"] = swap
    lg = np.log1p(-np.exp2(-5.0 - np.arange(RH)))
    scale = 128 ** -0.5
    m, n = np.arange(128)[:, None], np.arange(128)[None, :]
    c["decay"] = np.concatenate([np.where(n >= m, np.exp(g * np.maximum(n - m, 0)), 0) * scale for g in lg], 1)
    c["qdec"] = np.concatenate([np.tile(np.exp((np.arange(128) + 1.0) * g) * scale, (128, 1)) for g in lg], 1)
    c["kdec"] = np.stack([np.exp((127.0 - np.arange(128)) * g) for g in lg], 1)
    t = np.arange(NS)
    same = (t[:, None] // NT) == (t[None, :] // NT)
    dt = t[None, :] - t[:, None]
    ds_ = np.concatenate([np.where(same & (dt >= 0), np.exp(g * np.maximum(dt, 0)), 0) * scale for g in lg], 1)
    c["decay_s"] = np.pad(ds_, ((0, 96), (0, 0)))
    c["qdec_s"] = np.concatenate([np.tile(np.exp((t % NT + 1.0) * g) * scale, (128, 1)) for g in lg], 1)
    c["kdec_s"] = np.pad(np.stack([np.exp((NT - 1.0 - t % NT) * g) for g in lg], 1), ((0, 96), (0, 0)))
    c["seq_of"] = np.pad((t[:, None] // NT == np.arange(NB)[None, :]).astype(float), ((0, 96), (0, 0)))
    row = np.arange(128)
    rb, rgp, rg2, rj, rt = row // 64, row // 32 % 2, row // 16 % 2, row // 4 % 4, row % 4
    c["causal"] = np.where(n <= m, 0.0, NEG)
    blk = np.arange(32)[None, :] * 16 + 31
    tok = (np.arange(4)[None, :] * 128 + np.arange(128)[:, None])[:, :, None]
    ok = (blk[None] <= tok) & (np.arange(32) < NCP - 1)[None, None]
    c["cmp_mask"] = np.where(ok, 0.0, NEG).reshape(128, 128)
    c["cmp_valid"] = ok.astype(float).reshape(128, 128)
    sel = np.zeros((128, 3, 128))
    for br in range(3):
        sel[br * 16 + rgp * 8 + rj * 2 + rg2, br, row] = 1.0
    c["head_of_row"] = sel.reshape(128, 384)
    pair, b2, tt = t // 8, t // 4 % 2, t % 4
    c["token_of_row"] = ((b2[None, :] == rb[:, None]) & (tt[None, :] == rt[:, None])).astype(float)
    key = (rb * 4 + rgp * 2 + rg2) * 4 + rt
    c["heads_sum"] = (key[:, None] == key[None, :]).astype(float)
    j = np.arange(NSLC)
    c["bonus"] = np.tile(np.where((j == 0) | (j >= NSLC - 2), 1e4, 0.0), (128, 1))
    c["earlier"] = np.tile((j[None, :] < j[:, None]).astype(float).reshape(1, -1), (128, 1))
    fm = np.zeros((128, 4, NS))
    for r in range(4):
        own = (pair[None, :] == r) & (b2[None, :] == rb[:, None]) & (tt[None, :] <= rt[:, None])
        fm[:, r] = np.where(own, 0.0, NEG)
    c["fresh_mask"] = fm.reshape(128, 128)
    c["win_mask"] = np.where(np.arange(32)[None, :] > rt[:, None], 0.0, NEG)
    return {k: np.ascontiguousarray(v, dtype=np.float32) for k, v in c.items()}


CONSTS = layout_consts()
KEEP = ["ident", "mean_d", "causal", "cmp_mask", "cmp_valid", "head_of_row", "token_of_row", "heads_sum",
        "bonus", "earlier", "fresh_mask", "win_mask"]
EARLY = ["mean_h", "rope_cos", "rope_sin", "swap", "decay", "qdec", "kdec", "decay_s", "qdec_s", "kdec_s", "seq_of"]
VECS = [("sconv", 16), ("gn_g", 4), ("ln_g", 32), ("ln_b", 32), ("fconv", 2 * FC * 4), ("pe", 32)]


def build(nc, A):
    ctx = ExitStack()
    with ctx:
        def sem(name):
            return ctx.enter_context(nc.semaphore(name))

        ptab = ctx.enter_context(nc.sbuf_tensor("ptab", [1, NB * NPG], I32))
        ps = ctx.enter_context(nc.psum_tensor("ps", [128, 8, 512], F32))
        map_at = (nc.sbuf_base + 31) // 32 * 32
        WG = KC * 48
        BIG_AT = 2 * KC * T
        RING_AT = BIG_AT + 28 * T
        SLOTS_AT = RING_AT + 8 * 1024
        GATES_AT = SLOTS_AT + 4 * 4096
        REST_AT = GATES_AT + 2 * WG

        def place(name, start, end, dtype):
            return start, end, nc.alloc_sbuf_tensor_at(name, [128, end - start], dtype, offset=map_at + 4 * start)

        F = [place("big", BIG_AT, RING_AT, F32), place("ring", RING_AT, SLOTS_AT, F32), place("slots", SLOTS_AT, GATES_AT, F32),
             place("gates_w", GATES_AT, GATES_AT + WG, F32), place("rest", REST_AT, MAP, F32)]
        R = [place("x_parts", 0, BIG_AT, F32R), place("big_parts", BIG_AT, RING_AT, F32R),
             place("piece_parts", RING_AT, RING_AT + 4 * 1024, F32R), place("hidden_parts", SLOTS_AT, SLOTS_AT + FC * T, F32R),
             place("gates_w_low", GATES_AT, GATES_AT + WG, F32R), place("gates_w_high", GATES_AT + WG, REST_AT, F32R)]
        top = [REST_AT]

        def span(regions, at, n):
            start, _, t = next(v for v in regions if v[0] <= at and at + n <= v[1])
            return t[:, at - start:at - start + n]

        def alloc(n, base=None):
            b = top if base is None else base
            b[0] += n
            return span(F, b[0] - n, n)

        def as_f32(v):
            return v.bitcast(F32)

        def by_chunk(v, k):
            return v.rearrange("p (k t) -> p k t", k=k)

        xhs, xls = (by_chunk(span(R, k * KC * T, KC * T), KC) for k in range(2))
        big, bigs = (by_chunk(span(v, BIG_AT, 28 * T), 28) for v in (F, R))
        split = span(R, RING_AT, 4 * 1024).rearrange("p (s h n) -> p s h n", s=2, h=2)
        raw_at = RING_AT + 4 * 1024
        raw = [span(F, raw_at + (3 - s) * 1024, 1024) for s in range(4)]
        slots = span(F, SLOTS_AT, 4 * 4096).rearrange("p (s n) -> p s n", s=4)
        wg = span(F, GATES_AT, WG)
        wg_l, wg_h = (by_chunk(span(R, GATES_AT + k * WG, WG), KC) for k in range(2))
        y_at = GATES_AT - KC * T
        y = by_chunk(span(F, y_at, KC * T), KC)
        hid_l = by_chunk(span(R, SLOTS_AT, FC * T), FC)
        assert SLOTS_AT + FC * T <= y_at
        w1 = span(F, BIG_AT + 20 * T, 4096).rearrange("p (v n) -> p v n", v=2)
        w2 = alloc(2 * 64).rearrange("p (v n) -> p v n", v=2)
        keep_w = sum(CONSTS[k].shape[1] for k in KEEP)
        keep_all = alloc(keep_w)
        K = {}
        at = 0
        for k in KEEP:
            n = CONSTS[k].shape[1]
            K[k] = keep_all[:, at:at + n]
            at += n
        vec_w = sum(n for _, n in VECS)
        vec_all = alloc(vec_w)
        at = 0
        for k, n in VECS:
            K[k] = vec_all[:, at:at + n]
            at += n
        eps = alloc(1)
        fresh_v = alloc(512).rearrange("p (v n) -> p v n", v=2)
        grow = alloc(12)

        e = [SLOTS_AT]
        ret_states = alloc(NB * RH * 128, e).rearrange("p (b h e) -> p b h e", b=NB, h=RH)
        early_w = sum(CONSTS[k].shape[1] for k in EARLY)
        early_all = alloc(early_w, e)
        at = 0
        for k in EARLY:
            n = CONSTS[k].shape[1]
            K[k] = early_all[:, at:at + n]
            at += n
        sconv_hist = alloc(4 * 16, e).rearrange("p (c b w) -> p c b w", c=4, b=NB)
        sconv_out = alloc(4 * 18, e).rearrange("p (c w) -> p c w", c=4)
        rope_t = alloc(T, e)
        k_nat, v_nat, s_dec, q_dec, state = (alloc(512, e) for _ in range(5))
        v_blk = alloc(NB * 128, e)
        conv_u, conv_c, conv_d = alloc(CW, e), alloc(CO + 2, e), alloc(CO, e)
        gn_sq, gn_sd = ([alloc(T, e) for _ in range(2)] for _ in range(2))
        assert e[0] <= GATES_AT
        e = [y_at]
        ffn_a = alloc(2 * CW, e).rearrange("p (u n) -> p u n", u=2)
        ffn_c = alloc(2 * (CO + 2), e).rearrange("p (u n) -> p u n", u=2)
        ffn_g = alloc(2 * T, e).rearrange("p (u n) -> p u n", u=2)
        ffn_hist = alloc(FC * 16, e).rearrange("p (c b w) -> p c b w", c=FC, b=NB)
        ffn_out = alloc(FC * 18, e).rearrange("p (c w) -> p c w", c=FC)
        assert e[0] <= SLOTS_AT + 4 * 4096

        def ln_row(r, k):
            return big[:, (20, 24, 16, 24)[r] + k, :]

        w_hi = sem("w_hi")
        w_lo = sem("w_lo")
        w_in = [sem(f"w_in{s}") for s in range(4)]
        pieces = sem("pieces")
        freed = [sem(f"freed{s}") for s in range(2)]
        consts_in = sem("consts_in")
        early_in = sem("early_in")
        x_in = [sem(f"x_in{k}") for k in range(4)]
        x0_hi, x0_lo = sem("x0_hi"), sem("x0_lo")
        mix_hi, mix_lo = sem("mix_hi"), sem("mix_lo")
        att_hi, att_lo = sem("att_hi"), sem("att_lo")
        wg_hi, wg_lo = sem("wg_hi"), sem("wg_lo")
        hid_hi, hid_lo = sem("hid_hi"), sem("hid_lo")
        ln_hi = sem("ln_hi")
        w1_in = sem("w1_in")
        hist_in = sem("hist_in")
        ln_sum, ln_mean, ln_cen, ln_sq, ln_var, ln_std, ln_rs, ln_nrm, ln_x = (
            sem(n) for n in ("ln_sum", "ln_mean", "ln_cen", "ln_sq", "ln_var", "ln_std", "ln_rs", "ln_nrm", "ln_x"))
        ln_zero = sem("ln_zero")
        nsa_in = sem("nsa_in")
        out_done = sem("out_done")
        pool_set = sem("pool_set")

        def half(v):
            return v.rearrange("p (h t) -> p h t", h=2)

        def half1(v):
            return v.rearrange("p a (h t) -> p (a h) t", h=2)

        def feed(eng, part, name, take, stop=False):
            down = name.startswith("down")
            per = 12 if down else 4
            bodies = dict((g[0], g[1]) for g in GEMMS)[name] // per

            def body(i, last):
                for q in range(per):
                    if not (last and q >= per - 2):
                        part(PB[name] + i * per + (q + 2), (q + 2) % 4, PB[name] // 4 + i * (per // 4) + ((q + 2) // 4 + 1),
                             768 if down and (q + 2) % 3 == 2 else 1024)
                    if take:
                        take(i, q)

            with eng.Fori(0, bodies - stop) as i:
                body(i, False)
            if stop:
                body(bodies - 1, True)

        y_done = sem("y_done")

        def pset(s):
            return ps[:, 2 * s:2 * s + 2, 0:HT]

        rope_pe = sem("rope_pe")
        RD = Steps(sem("rope_dve"), ["sin", "cos", "add"])
        RP = Steps(sem("ret_pe"), ["kT", "vT", "sc", "o", "kv"])
        RV = Steps(sem("ret_dve"), ["kn", "st", "qd", "state"])
        RA = Steps(sem("ret_act"), ["vn", "o"])
        SP_ = Steps(sem("rets_pe"), ["kT", "vT", "sc", "o"])
        SV = Steps(sem("rets_dve"), ["kn", "st", "qd", "vb"])
        SA = Steps(sem("rets_act"), ["vn", "o"])
        kv_s = sem("kv_s")
        st_s = sem("st_s")
        GN = {k: sem(f"gn_{k}") for k in ("mean", "var", "sq", "std", "cen", "rs", "nrm", "mul")}
        gn_gate = sem("gn_gate")
        ya = Steps(sem("conv_pool"), ["hist", "up", "us", "t0", "t1", "s1", "t2", "s2", "keep", "yp", "ys"])
        ret_in = sem("ret_in")
        zero_u = sem("zero_u")
        QZ, KZ, VZ, GZ, CZ, HZ, BZ = 0, 4, 8, 12, 16, 20, 24
        MIX_H, MIX_L = KZ, [BZ, BZ + 1, BZ + 2, BZ + 3, CZ, CZ + 1, CZ + 2, CZ + 3]

        def in0_done(row):
            return PB["in0"] + row + 1

        fa = Steps(sem("ffn_act"), ["a", "gelu"])
        fd = Steps(sem("ffn_dve"), ["c0", "c1", "c2"])
        fp = Steps(sem("ffn_pool"), ["in", "out"])
        hist_load = sem("hist_load")
        ffn_zero = sem("ffn_zero")
        hist_store = sem("hist_store")

        def conv_sample(c):
            return c[:, SO:SO + 6 * NB].rearrange("p (b w) -> p b w", b=NB)[:, :, 0:NT]

        KVR = 8
        KS, VS, KW, VW = 12, 14, 16, 18
        cbias = alloc(2)
        ATT_H, ATT_L = 8, 20
        soft = alloc(48)
        e = [RING_AT]
        v_nat_p = alloc(2048, e).rearrange("p (v t n) -> p v t n", v=2, t=4)
        c_p = alloc(2048, e).rearrange("p (v c g n) -> p v c g n", v=2, c=8, g=4)
        gtok = alloc(192, e).rearrange("p (q b h) -> p q b h", q=4, b=3)
        e = [SLOTS_AT + 3 * 4096]
        kcc_p = alloc(64, e).rearrange("p (g n) -> p g n", g=2)
        vcc_p = alloc(256, e)
        q_st = [alloc(512, e), span(F, SLOTS_AT + 2 * 4096, 512)]
        prob = alloc(2 * 1056, e).rearrange("p (u n) -> p u n", u=2)
        pt_p = alloc(9 * 128, e).rearrange("p (t n) -> p t n", t=9)
        bs_p, hid_p = pt_p[:, 0, :].rearrange("p (g n) -> p g n", g=4), pt_p[:, 1, :].rearrange("p (g n) -> p g n", g=4)
        gate_t = prob[0:48].rearrange("p u n -> p (u n)")[:, 0:T]
        grow_m = pt_p[:, 2, 0:96].rearrange("p (b w t) -> p b w t", b=3, w=4)
        nmax = soft[:, 0:6].rearrange("p (u n) -> p u n", u=2)
        rsum = soft[:, 6:12].rearrange("p (u n) -> p u n", u=2)
        fac = soft[:, 12:18].rearrange("p (u n) -> p u n", u=2)
        growv = grow.rearrange("p (b w) -> p b w", b=3)
        assert e[0] <= SLOTS_AT + 4 * 4096
        e = [RING_AT]
        sc_s = alloc(2048 + NS, e)
        sc_w = alloc(W + NS, e)
        kcc = alloc(512, e).rearrange("p (b g n) -> p b g n", b=2, g=2)
        vcc = alloc(512, e).rearrange("p (b n) -> p b n", b=2)
        qb = alloc(256, e).rearrange("p (b g n) -> p b g n", b=2, g=2)
        pc = alloc(128, e)
        pj = alloc(136, e)
        score, rank_a, rank_b = alloc(NSLC), alloc(NSLC), alloc(NSLC)
        pt_all = alloc(23 * 128, e).rearrange("p (t n) -> p t n", t=23)
        cmpx = sc_s[:, 0:NSLC * NSLC].rearrange("p (m n) -> p m n", m=NSLC)
        assert e[0] <= raw_at + 3 * 1024, e[0] - raw_at
        pt_s = [pt_all[:, t, :] for t in range(16)]
        pt_w = [pt_all[:, 16 + t, :] for t in range(4)]
        pt_c, pt_fs, pt_fw = (pt_all[:, 20 + t, :] for t in range(3))
        def pt4(q):
            return pt_all[:, 4 * q:4 * q + 4, :].rearrange("p t n -> p (t n)")

        win_k = big[:, 8:12, 0:W].rearrange("p (b g) n -> p b g n", b=2)
        bs_s = [big[:, 16, 0:512], big[:, 19, 0:512]]
        hid_s = [big[:, 17, 0:512], big[:, 18, 0:512]]
        s_nm, s_sum, s_fac = soft[:, 20:23], soft[:, 23:26], soft[:, 26:29]

        tab_in = sem("tab_in")
        turn, turn_v, turn_a = sem("turn"), sem("turn_v"), sem("turn_a")
        slot_in = [sem(f"slot_in{s}") for s in range(4)]
        kv_store = sem("kv_store")
        NP = Steps(sem("prep_pe"), ["gate", "gT", "grow", "V0", "V1", "V2", "V3", "F", "bias", "k1", "v1", "k2", "v2"])
        NA = Steps(sem("prep_act"), ["sig", "V0", "V2", "bias", "C", "Bk", "hk", "Bv", "hv"])
        ND = Steps(sem("prep_dve"), ["C", "gtok", "gm", "grow", "V1", "V3", "F", "prek", "prev", "kcc", "vcc"])
        U = range(8)
        QT = (3,3,0,0,2,2,1,1)

        class Units:
            def __init__(self, names):
                self.sem = {k: sem(f"unit_{k}") for k in names.split()}

            def done(self, eng, name, R, u):
                eng.wait_ge(self.sem[name], R * 8 + (u + (2 if name == "o" else 1)))

        UN = Units("s t o e ta dm cm mx my rc fa p tb")
        q_in, out_free = sem("q_in"), sem("out_free")

        XP = Steps(sem("smp_pe"), ["ck0", "ck1", "k20", "k21", "sc", "cv0", "cv1", "J", "v20", "v21", "ss0", "ss1", "ws",
                                   "tc", "ts0", "ts1", "ts2", "ts3", "tw", "pv0", "pv1", "po"])
        XD = Steps(sem("smp_dve"), ["pre0", "pre1", "kc0", "kc1", "cmx", "crc", "cp", "pre2", "pre3", "pj", "im", "sc1", "sc2",
                                    "eq", "tri", "r1", "gt", "r2", "rk", "mk", "cf", "pg", "vc0", "vc1", "sv", "sf", "smx",
                                    "wv", "wf", "wmx", "src", "sfa", "sP", "wrc", "wfa", "wP", "ts0", "ts1", "pv", "ov"])
        XA = Steps(sem("smp_act"), ["B0", "h0", "B1", "h1", "ce", "B2", "h2", "B3", "h3", "se", "we", "tc", "ts2", "ts3", "tw"])
        XQ = sem("qb_ready")
        win_in = sem("win_in")
        win_out = sem("win_out")
        smp_zero = sem("smp_zero")

        def load_pages(eng, cache, slot, r, b):
            for g in range(NPG):
                v = eng.value_load(ptab[0:1, bass.ds(r * 32 + (b * NPG + g), 1)], min_val=0, max_val=NPHYS - 1)
                eng.dma_start(slots[:, slot, g * 256:(g + 1) * 256],
                              A[cache][bass.ds(v, 1), :, :].rearrange("a p n -> (a p) n")).then_inc(slot_in[slot], 16)

        def pair_pages(eng, caches, slot, r, last, first, carry):
            for b in range(2):
                if not isinstance(r, int):
                    eng.wait_ge(XP.sem, XP.at(last[b], r - 1))
                    eng.sem_inc(carry, 1)
                load_pages(eng, caches[0], slot + b, r, b)
            for b in range(2):
                eng.wait_ge(XP.sem, XP.at(first[b], r))
                eng.sem_inc(carry, 1)
                load_pages(eng, caches[1], slot + b, r, b)

        def feed_in1(eng, part, take):
            def body(i, scale, last=False):
                for q in range(4):
                    if not (last and q >= 2):
                        part(PB["in1"] + i * 4 + (q + 2), (q + 2) % 4, PB["in1"] // 4 + i + ((q + 2) // 4 + 1), 1024)
                    take(i, q, scale)

            with eng.Fori(0, 2) as i:
                body(i, 0.125)
            with eng.Fori(2, 4) as i:
                body(i, 1.0)
            body(4, 1.0, True)

        def NSA_SP(sp, stream):
            stream("in1")
            sp.dma_start(ptab[:, :], A["page_table"]).then_inc(tab_in, 16)
            sp.wait_ge(tab_in, 16)
            pair_pages(sp, ("cmp_k", "slc_k"), 0, 0, ("ss0", "ss1"), ("ck0", "ck1"), turn)
            with sp.Fori(1, 4) as r:
                pair_pages(sp, ("cmp_k", "slc_k"), 0, r, ("ss0", "ss1"), ("ck0", "ck1"), turn)
            stream("out1")

        def NSA_PE(pe, product):
            pe.wait_ge(wg_lo, 1)
            pe.wait_ge(nsa_in, 32)
            pe.wait_ge(w1_in, 16)
            for k in range(KC):
                for w_part, v_part in ((wg_h, xhs), (wg_h, xls), (wg_l, xhs)):
                    for h in range(2):
                        mm = pe.matmul(ps[0:48, 4 + h, 0:HT], w_part[:, k, :], v_part[:, k, h * HT:(h + 1) * HT],
                                       start=k == 0 and w_part is wg_h and v_part is xhs, stop=k == KC - 1 and w_part is wg_l)
            mm.then_inc(NP.sem, 1)
            pe.wait_ge(NA.sem, NA.at("sig"))
            for t in range(4):
                mm = pe.transpose(ps[:, 6, t * 48:t * 48 + 48], gate_t[:, t * 128:(t + 1) * 128], K["ident"][0:48, 0:48])
            mm.then_inc(NP.sem, 1)
            for b in range(3):
                mm = pe.matmul(ps[:, 7, b * 32:b * 32 + 32], K["head_of_row"][0:48, b * 128:(b + 1) * 128], gate_t[:, SEQ:T],
                               start=True, stop=True)
            mm.then_inc(NP.sem, 1)
            pe.wait_ge(freed[0], SB["out1"])
            pe.wait_ge(freed[1], SB["out1"])
            for t in range(4):
                for v, row in enumerate((VS, VW)):
                    for g in range(2):
                        c = (v * 2 + g) * 128
                        mm = pe.transpose(ps[:, t, c:c + 128], big[:, row + g, t * 128:(t + 1) * 128], K["ident"])
                mm.then_inc(NP.sem, 1)
            for v, row in enumerate((VS, VW)):
                for g in range(2):
                    c = (v * 2 + g) * 128
                    mm = pe.transpose(ps[0:32, 4, c:c + 128], big[:, row + g, SEQ:T], K["ident"])
            mm.then_inc(NP.sem, 1)
            for v in range(2):
                for t in range(16):
                    mm = pe.matmul(ps[:, 5, v:v + 1], w1[:, v, t * 128:(t + 1) * 128], K["pe"][:, v * 16 + t:v * 16 + t + 1],
                                   start=t == 0, stop=t == 15)
            mm.then_inc(NP.sem, 1)
            pe.wait_ge(ND.sem, ND.at("grow"))
            for v in range(2):
                if v == 0:
                    pe.wait_ge(ND.sem, ND.at("C"))
                else:
                    pe.wait_ge(NA.sem, NA.at("C"))
                    pe.wait_ge(ND.sem, ND.at("V1"))
                for part in range(2):
                    bank = (6, 0)[v] + part
                    for c in range(8):
                        mm = pe.matmul(ps[:, bank, 0:128], w1[:, v, (part * 8 + c) * 128:(part * 8 + c + 1) * 128],
                                       c_p[:, v, c, :, :].rearrange("p g n -> p (g n)"), start=c == 0, stop=c == 7)
                mm.then_inc(NP.sem, 1)
            pe.wait_ge(NA.sem, NA.at("hk"))
            hg = hid_p.rearrange("p (g h) n -> p g h n", g=2)
            for g2 in range(2):
                mm = pe.matmul(ps[64 * g2:64 * g2 + 64, 2, 0:62].rearrange("p (g n) -> p g n", g=2), w2[:, 0, :],
                               hg[:, :, g2, 0:31], start=True, stop=True)
            mm.then_inc(NP.sem, 1)
            pe.wait_ge(NA.sem, NA.at("hv"))
            for g in range(4):
                mm = pe.matmul(ps[0:31, 3, g * 64:(g + 1) * 64], hid_p[:, g, 0:31], w2[:, 1, :], start=True, stop=True)
            mm.then_inc(NP.sem, 1)
            pe.wait_ge(ND.sem, ND.at("vcc"))

            def s(R, u, gp):
                qt, g2 = QT[u % 8], u % 2
                p0 = slice(64 * g2, 64 * g2 + 64)
                q = q_st[gp][p0, qt * 128:qt * 128 + 128]
                n = (qt + 1) * 128
                first = isinstance(R, int) and R == 0
                if u % 8 == 0:
                    pe.wait_ge(q_in, R + (1 + u // 8))
                if not first or u >= 2:
                    UN.done(pe, "e", R, u - 2)
                pe.matmul(ps[:, 2 * g2, 0:n], q, big[p0, KS + gp, 0:n], start=True, stop=True)
                pe.matmul(ps[:, 2 * g2 + 1, 0:n], q, big[p0, KW + gp, 0:n], start=True, stop=True)
                if not first or u:
                    UN.done(pe, "cm", R, u - 1)
                if not first or u >= 2:
                    UN.done(pe, "tb", R, u - 2)
                pe.matmul(ps[:, 4, g2 * 32:g2 * 32 + 31], q, kcc_p[p0, gp, 0:31],
                          start=True, stop=True).then_inc(UN.sem["s"], 1)

            def t(R, u, last):
                qt, g2 = QT[u], u % 2
                UN.done(pe, "p", R, u)
                for kt in range(qt + 1):
                    pe.transpose(ps[:, 5, kt * 128:(kt + 1) * 128], prob[:, g2, kt * 128:(kt + 1) * 128], K["ident"])
                for kt in range(qt + 1):
                    pe.transpose(ps[:, 6, kt * 128:(kt + 1) * 128], prob[:, g2, 512 + kt * 128:512 + (kt + 1) * 128], K["ident"])
                if not (last and u == 7):
                    UN.done(pe, "cm", R, u + 1)
                pe.transpose(ps[0:31, 4, 128:256], prob[:, g2, 1024:1055], K["ident"]).then_inc(UN.sem["t"], 1)

            def o(R, u, gp):
                qt, g2 = QT[u], u % 2
                out = ps[64 * g2:64 * g2 + 64, 7, qt * 128:(qt + 1) * 128]
                vc = slice(gp * 128 + g2 * 64, gp * 128 + g2 * 64 + 64)
                if u == 0:
                    pe.wait_ge(out_free, R + 1)
                UN.done(pe, "ta", R, u)
                UN.done(pe, "tb", R, u)
                for kt in range(qt + 1):
                    pe.matmul(out, v_nat_p[:, 0, kt, vc], pt_p[:, kt, :], start=kt == 0, stop=False)
                for kt in range(qt + 1):
                    pe.matmul(out, v_nat_p[:, 1, kt, vc], pt_p[:, 4 + kt, :], start=False, stop=False)
                pe.matmul(out, vcc_p[0:31, vc], pt_p[0:31, 8, :], start=False, stop=True).then_inc(UN.sem["o"], 1)

            def two_rounds(i, last):
                for gp in range(2):
                    end = last and gp == 1
                    for u in U:
                        t(i * 2 + gp, u, end)
                        if u < 6:
                            s(i * 2 + gp, u + 2, gp)
                        elif not end:
                            s(i * 2 + gp, u + 2, 1 - gp)
                        o(i * 2 + gp, u, gp)

            pe.sem_inc(UN.sem["o"], 1)
            s(0, 0, 0)
            s(0, 1, 0)
            with pe.Fori(0, 3) as i:
                two_rounds(i, False)
            two_rounds(3, True)

            def pair(r):
                prev = not (isinstance(r, int) and r == 0)

                def compress(v, b, part_slots):
                    sl = 2 * v + b
                    pe.wait_ge(slot_in[sl], 256 * (1 + 2 * r))
                    rows = slots[:, sl, :].rearrange("p (pg c g n) -> p pg c g n", pg=NPG, c=8, g=4)
                    for part in range(2):
                        dst = ps[:, 2 * b + part, :].rearrange("p (g pg n) -> p pg g n", g=4, pg=NPG)
                        for c in range(8):
                            mm = pe.matmul(dst, w1[:, v, (part * 8 + c) * 128:(part * 8 + c + 1) * 128], rows[:, :, c, :, :],
                                           start=c == 0, stop=c == 7)
                    mm.then_inc(XP.sem, 1)

                if not prev:
                    pe.wait_ge(smp_zero, 3)
                for b in range(2):
                    compress(0, b, None)
                for b in range(2):
                    pe.wait_ge(XA.sem, XA.at(f"h{b}", r))
                    hg = hid_s[b].rearrange("p (g h n) -> p g h n", g=2, h=2)
                    for g2 in range(2):
                        mm = pe.matmul(ps[64 * g2:64 * g2 + 64, 4, b * 256:b * 256 + 254].rearrange("p (g n) -> p g n", g=2),
                                       w2[:, 0, :], hg[:, :, g2, 0:NCMP], start=True, stop=True)
                    mm.then_inc(XP.sem, 1)
                pe.wait_ge(XQ, 1 + r)
                pe.wait_ge(XD.sem, XD.at("kc1", r))
                for b in range(2):
                    for g in range(2):
                        mm = pe.matmul(ps[64 * b:64 * b + 64, 6, 0:NCMP], qb[:, b, g, :], kcc[:, b, g, 0:NCMP], start=g == 0, stop=g == 1)
                mm.then_inc(XP.sem, 1)
                for b in range(2):
                    pe.wait_ge(XD.sem, XD.at(f"pre{b}", r))
                    compress(1, b, None)
                pe.wait_ge(XD.sem, XD.at("cp", r))
                pe.matmul(ps[:, 6, 128:128 + NCMP], K["heads_sum"], pc[:, 0:NCMP], start=True, stop=True).then_inc(XP.sem, 1)
                for b in range(2):
                    pe.wait_ge(XA.sem, XA.at(f"h{2 + b}", r))
                    for g in range(4):
                        mm = pe.matmul(ps[0:NCMP, 5, b * 256 + g * 64:b * 256 + g * 64 + 64], hid_s[b][:, g * 128:g * 128 + NCMP],
                                       w2[:, 1, :], start=True, stop=True)
                    mm.then_inc(XP.sem, 1)
                for b in range(2):
                    pe.wait_ge(slot_in[b], 256 * (2 + 2 * r))
                    if b == 0:
                        pe.wait_ge(XD.sem, XD.at("pre3", r))
                    rows = slots[:, b, :].rearrange("p (pg g n) -> p pg g n", pg=NPG, g=2)
                    p0 = slice(64 * b, 64 * b + 64)
                    for t in range(4):
                        for g in range(2):
                            pe.matmul(ps[p0, t, :].rearrange("p (pg n) -> p pg n", pg=4), qb[:, b, g, :],
                                      rows[:, 4 * t:4 * t + 4, g, :], start=g == 0, stop=g == 1)
                    for g in range(2):
                        mm = pe.matmul(ps[p0, 4, 0:32], qb[:, b, g, :], big[:, KS + g, SEQ:T], start=g == 0, stop=g == 1)
                    mm.then_inc(XP.sem, 1)
                pe.wait_ge(win_in, 96 * (1 + r))
                if prev:
                    pe.wait_ge(XD.sem, XD.at("ov", r - 1))
                pe.wait_ge(XD.sem, XD.at("vc1", r))
                for b in range(2):
                    p0 = slice(64 * b, 64 * b + 64)
                    for g in range(2):
                        pe.matmul(ps[p0, 5, :], qb[:, b, g, :], win_k[:, b, g, :], start=g == 0, stop=g == 1)
                    for g in range(2):
                        mm = pe.matmul(ps[p0, 7, 256:288], qb[:, b, g, :], big[:, KW + g, SEQ:T], start=g == 0, stop=g == 1)
                mm.then_inc(XP.sem, 1)
                pe.wait_ge(XD.sem, XD.at("pg", r))
                pe.transpose(ps[0:NCMP, 6, 256:384], pc[:, 0:NCMP], K["ident"]).then_inc(XP.sem, 1)
                pe.wait_ge(XD.sem, XD.at("sP", r))
                for q in range(4):
                    for t in range(4):
                        k0 = (4 * q + t) * 128
                        mm = pe.transpose(ps[:, q, t * 128:(t + 1) * 128], sc_s[:, k0:k0 + 128], K["ident"])
                    if q == 3:
                        pe.wait_ge(XA.sem, XA.at("tc", r))
                        mm = pe.transpose(ps[0:32, 6, 384:512], sc_s[:, 2048:2080], K["ident"])
                    mm.then_inc(XP.sem, 1)
                pe.wait_ge(XD.sem, XD.at("wP", r))
                for t in range(4):
                    pe.transpose(ps[:, 5, t * 128:(t + 1) * 128], sc_w[:, t * 128:(t + 1) * 128], K["ident"])
                pe.transpose(ps[0:32, 4, 128:256], sc_w[:, 512:544], K["ident"]).then_inc(XP.sem, 1)
                pe.wait_ge(XD.sem, XD.at("ts1", r))
                pe.wait_ge(XA.sem, XA.at("tw", r))
                for b in range(2):
                    pe.wait_ge(slot_in[2 + b], 256 * (2 + 2 * r))
                    out, mine = ps[64 * b:64 * b + 64, 7, 0:256], slice(64 * b, 64 * b + 64)
                    pe.matmul(out, pt_c[0:NCMP, mine], vcc[0:NCMP, b, :], start=True, stop=False)
                    for t in range(16):
                        pe.matmul(out, pt_s[t][:, mine], slots[:, 2 + b, t * 256:(t + 1) * 256], start=False, stop=False)
                    pe.matmul(out, pt_fs[0:32, mine], fresh_v[0:32, 0, :], start=False, stop=False)
                    for t in range(4):
                        wv = big[:, 12 + 2 * b + t // 2, (t % 2) * 256:(t % 2) * 256 + 256]
                        pe.matmul(out, pt_w[t][:, mine], wv, start=False, stop=False)
                    pe.matmul(out, pt_fw[0:32, mine], fresh_v[0:32, 1, :], start=False, stop=True).then_inc(XP.sem, 1)
                pe.wait_ge(XD.sem, XD.at("pv", r))
                for g in range(2):
                    mm = pe.transpose(ps[:, 7, 256 + g * 128:384 + g * 128], sc_w[:, g * 128:(g + 1) * 128], K["ident"])
                mm.then_inc(XP.sem, 1)

            pair(0)
            with pe.Fori(1, 4) as r:
                pair(r)
            pe.wait_ge(XD.sem, XD.at("ov", 3))
            product("out1", lambda k: (bigs[:, ATT_H + k, :], bigs[:, ATT_L + k, :]), lambda k: pe.wait_ge(att_lo, 1 + k // 4))

        def NSA_ACT(act, take, hi):
            feed_in1(act, hi, lambda i, q, scale: take("in1", i, q, scale) if q % 2 == 0 else None)
            act.wait_ge(NP.sem, NP.at("gate"))
            act.activation(gate_t.rearrange("p (h t) -> p h t", h=2), ps[0:48, 4:6, 0:HT], ACT.Sigmoid).then_inc(NA.sem, 1)
            for t in (0, 2):
                act.wait_ge(NP.sem, NP.at(f"V{t}"))
                act.activation(v_nat_p[:, :, t, :], ps[:, t, :].rearrange("p (v n) -> p v n", v=2), ACT.Copy).then_inc(NA.sem, 1)
            act.wait_ge(NP.sem, NP.at("bias"))
            act.activation(cbias, ps[:, 5, 0:2], ACT.Copy).then_inc(NA.sem, 1)
            act.wait_ge(freed[1], SB["out1"])
            for g in range(4):
                for par in range(2):
                    src = big[64 * (g % 2):64 * (g % 2) + 64, KVR + 2 + g // 2, 0:SEQ].rearrange("p (n c r) -> p r c n", c=8, r=2)
                    op = act.activation(c_p[64 * par:64 * par + 64, 1, :, g, :], src[:, par, :, :], ACT.Copy)
            op.then_inc(NA.sem, 1)
            for v in range(2):
                act.wait_ge(NP.sem, NP.at(("k1", "v1")[v]))
                if v == 0:
                    act.wait_ge(NA.sem, NA.at("bias"))
                else:
                    act.wait_ge(ND.sem, ND.at("prek"))
                act.activation(bs_p, ps[:, (7, 1)[v], 0:128].rearrange("p (g n) -> p g n", g=4), ACT.Identity,
                               bias=cbias[:, v:v + 1]).then_inc(NA.sem, 1)
                act.wait_ge(ND.sem, ND.at(("prek", "prev")[v]))
                act.activation(hid_p[:, :, 0:31], hid_p[:, :, 0:31], ACT.Gelu_apprx_tanh).then_inc(NA.sem, 1)

            def q_copy(row, gp):
                act.activation(q_st[gp].unsqueeze(1), big[:, bass.ds(row, 1), 0:SEQ], ACT.Copy).then_inc(q_in, 1)

            def e(R, u):
                qt, g2 = QT[u % 8], u % 2
                n = (qt + 1) * 128
                UN.done(act, "my", R, u)
                if not (isinstance(R, int) and R == 0 and u < 2):
                    UN.done(act, "t", R, u - 2)
                for k in range(2):
                    act.activation(prob[:, g2, 512 * k:512 * k + n], ps[:, 2 * g2 + k, 0:n], ACT.Exp,
                                   bias=nmax[:, g2, k + 1:k + 2], accum_out=rsum[:, g2, k + 1:k + 2])
                act.activation(prob[:, g2, 1024:1055], prob[:, g2, 1024:1055], ACT.Exp,
                               bias=nmax[:, g2, 0:1], accum_out=rsum[:, g2, 0:1]).then_inc(UN.sem["e"], 1)

            def ta(R, u):
                UN.done(act, "t", R, u)
                UN.done(act, "o", R, u - 1)
                n = (QT[u] + 1) * 128
                act.activation(pt_p[:, 0:8, :].rearrange("p (k t) n -> p k (t n)", k=2)[:, :, 0:n], ps[:, 5:7, 0:n],
                               ACT.Copy).then_inc(UN.sem["ta"], 1)

            def round_(i, gp, last):
                R = i * 2 + gp
                if gp == 0:
                    q_copy(i + 4, 1)
                elif not last:
                    q_copy(i + 1, 0)
                for u in U:
                    ta(R, u)
                    if not last or u < 6:
                        e(R, u + 2)
                UN.done(act, "o", R, 7)
                act.sem_inc(turn_a, 1)
                act.activation(big[:, bass.ds(i + 4 * gp, 1), 0:SEQ], ps[:, 7, :].unsqueeze(1), ACT.Copy).then_inc(out_free, 1)

            act.wait_ge(ND.sem, ND.at("vcc"))
            q_copy(0, 0)
            act.sem_inc(out_free, 1)
            e(0, 0)
            e(0, 1)
            with act.Fori(0, 3) as i:
                round_(i, 0, False)
                round_(i, 1, False)
            round_(3, 0, False)
            round_(3, 1, True)

            def pair(r):
                def first(c):
                    b = c % 2
                    act.wait_ge(XP.sem, XP.at(("ck0", "ck1", "cv0", "cv1")[c], r))
                    if c >= 2:
                        act.wait_ge(XD.sem, XD.at(f"pre{c - 2}", r))
                    act.activation(bs_s[b], ps[:, 2 * b + 1, :], ACT.Identity, bias=cbias[:, c // 2:c // 2 + 1]).then_inc(XA.sem, 1)
                    act.wait_ge(XD.sem, XD.at(f"pre{c}", r))
                    h = hid_s[b].rearrange("p (g n) -> p g n", g=4)[:, :, 0:NCMP]
                    act.activation(h, h, ACT.Gelu_apprx_tanh).then_inc(XA.sem, 1)
                first(0)
                first(1)
                act.wait_ge(XD.sem, XD.at("cmx", r))
                act.activation(pc[:, 0:NCMP], ps[:, 6, 0:NCMP], ACT.Exp, bias=s_nm[:, 0:1], accum_out=s_sum[:, 0:1]).then_inc(XA.sem, 1)
                first(2)
                first(3)
                act.wait_ge(XD.sem, XD.at("smx", r))
                act.activation(sc_s, sc_s, ACT.Exp, bias=s_nm[:, 1:2], accum_out=s_sum[:, 1:2]).then_inc(XA.sem, 1)
                act.wait_ge(XD.sem, XD.at("wmx", r))
                act.activation(sc_w, sc_w, ACT.Exp, bias=s_nm[:, 2:3], accum_out=s_sum[:, 2:3]).then_inc(XA.sem, 1)
                act.wait_ge(XP.sem, XP.at("tc", r))
                act.activation(pt_c[0:NCMP, :], ps[0:NCMP, 6, 256:384], ACT.Copy).then_inc(XA.sem, 1)
                act.wait_ge(XP.sem, XP.at("ts2", r))
                act.activation(pt4(2), ps[:, 2, :], ACT.Copy).then_inc(XA.sem, 1)
                act.wait_ge(XP.sem, XP.at("ts3", r))
                act.activation(pt4(3), ps[:, 3, :], ACT.Copy)
                act.activation(pt_fs[0:32, :], ps[0:32, 6, 384:512], ACT.Copy).then_inc(XA.sem, 1)
                act.wait_ge(XP.sem, XP.at("tw", r))
                act.activation(pt4(4), ps[:, 5, :], ACT.Copy)
                act.activation(pt_fw[0:32, :], ps[0:32, 4, 128:256], ACT.Copy).then_inc(XA.sem, 1)

            with act.Fori(0, 4) as r:
                pair(r)
            act.wait_ge(XD.sem, XD.at("ov", 3))
            act.wait_ge(win_out, 128 * 4)
            hi(PB["out1"], 0, PB["out1"] // 4 + 1)
            for u in range(2):
                act.activation(bigs[:, ATT_H + 4 * u:ATT_H + 4 * u + 4, :], big[:, 4 * u:4 * u + 4, :], ACT.Copy).then_inc(att_hi, 1)
            hi(PB["out1"] + 1, 1, PB["out1"] // 4 + 1)

        def NSA_DVE(ve, take, lo):
            feed_in1(ve, lo, lambda i, q, scale: take("in1", i, q, scale) if q % 2 else None)
            ve.wait_ge(freed[0], SB["out1"])
            for g in range(4):
                for par in range(2):
                    src = big[64 * (g % 2):64 * (g % 2) + 64, KVR + g // 2, 0:SEQ].rearrange("p (n c r) -> p r c n", c=8, r=2)
                    op = ve.tensor_copy(c_p[64 * par:64 * par + 64, 0, :, g, :], src[:, par, :, :])
            op.then_inc(ND.sem, 1)
            ve.wait_ge(NP.sem, NP.at("gT"))
            ve.tensor_copy(gtok, ps[:, 6, 0:192].rearrange("p (q b h) -> p q b h", q=4, b=3)).then_inc(ND.sem, 1)
            ve.wait_ge(NP.sem, NP.at("grow"))
            ve.tensor_tensor(grow_m.rearrange("p b w t -> p b (w t)"), ps[:, 7, 0:96].rearrange("p (b t) -> p b t", b=3),
                             K["token_of_row"].unsqueeze(1).to_broadcast([128, 3, 32]), ALU.mult).then_inc(ND.sem, 1)
            ve.wait_ge(ND.sem, ND.at("gm"))
            ve.tensor_reduce(growv, grow_m, AX.X, ALU.add).then_inc(ND.sem, 1)
            for t in (1, 3):
                ve.wait_ge(NP.sem, NP.at(f"V{t}"))
                ve.tensor_copy(v_nat_p[:, :, t, :], ps[:, t, :].rearrange("p (v n) -> p v n", v=2)).then_inc(ND.sem, 1)
            ve.wait_ge(NP.sem, NP.at("F"))
            ve.tensor_copy(fresh_v[0:32, :, :], ps[0:32, 4, :].rearrange("p (v n) -> p v n", v=2)).then_inc(ND.sem, 1)
            for v in range(2):
                if v:
                    ve.wait_ge(NP.sem, NP.at("k2"))
                ve.wait_ge(NA.sem, NA.at(("Bk", "Bv")[v]))
                ve.tensor_tensor(hid_p[:, :, 0:31], ps[:, (6, 0)[v], 0:128].rearrange("p (g n) -> p g n", g=4)[:, :, 0:31],
                                 bs_p[:, :, 1:32], ALU.add).then_inc(ND.sem, 1)
            ve.wait_ge(NP.sem, NP.at("k2"))
            ve.tensor_copy(kcc_p[:, :, 0:31], ps[:, 2, 0:62].rearrange("p (g n) -> p g n", g=2)).then_inc(ND.sem, 1)
            ve.wait_ge(NP.sem, NP.at("v2"))
            ve.tensor_copy(vcc_p[0:31, :], ps[0:31, 3, 0:256]).then_inc(ND.sem, 1)

            def a(R, u):
                qt, g2 = QT[u % 8], u % 2
                n = (qt + 1) * 128
                UN.done(ve, "s", R, u)
                d = ps[:, 2 * g2:2 * g2 + 2, qt * 128:n]
                ve.tensor_tensor(d, d, K["causal"].unsqueeze(1).to_broadcast([128, 2, 128]), ALU.add).then_inc(UN.sem["dm"], 1)
                if not (isinstance(R, int) and R == 0 and u < 2):
                    UN.done(ve, "t", R, u - 2)
                ve.tensor_tensor(prob[:, g2, 1024:1055], ps[:, 4, g2 * 32:g2 * 32 + 31], K["cmp_mask"][:, qt * 32:qt * 32 + 31],
                                 ALU.add).then_inc(UN.sem["cm"], 1)
                UN.done(ve, "dm", R, u)
                ve.tensor_reduce(nmax[:, g2, 1:3], ps[:, 2 * g2:2 * g2 + 2, 0:n], AX.X, ALU.max, negate=True).then_inc(UN.sem["mx"], 1)
                UN.done(ve, "cm", R, u)
                ve.tensor_reduce(nmax[:, g2, 0:1], prob[:, g2, 1024:1055], AX.X, ALU.max, negate=True).then_inc(UN.sem["my"], 1)

            def b(i, gp, u):
                R = i * 2 + gp
                qt, g2 = QT[u % 8], u % 2
                n = (qt + 1) * 128
                col = 8 * gp + g2 if u < 8 else (8, 2)[gp]
                UN.done(ve, "e", R, u)
                ve.reciprocal(fac[:, g2, :], rsum[:, g2, :]).then_inc(UN.sem["rc"], 1)
                UN.done(ve, "rc", R, u)
                ve.tensor_tensor(fac[:, g2, :].unsqueeze(2), fac[:, g2, :].unsqueeze(2),
                                 gtok[:, qt, :, bass.ds(i * 2 + col, 1)], ALU.mult).then_inc(UN.sem["fa"], 1)
                UN.done(ve, "fa", R, u)
                for k in range(2):
                    pr = prob[:, g2, 512 * k:512 * k + n]
                    ve.tensor_scalar(pr, pr, fac[:, g2, k + 1:k + 2], None, ALU.mult)
                pr = prob[:, g2, 1024:1055]
                ve.scalar_tensor_tensor(out=pr, in0=pr, scalar=fac[:, g2, 0:1], in1=K["cmp_valid"][:, qt * 32:qt * 32 + 31],
                                        op0=ALU.mult, op1=ALU.mult).then_inc(UN.sem["p"], 1)

            def c(R, u):
                UN.done(ve, "t", R, u)
                UN.done(ve, "o", R, u - 1)
                ve.tensor_copy(pt_p[0:31, 8, :], ps[0:31, 4, 128:256]).then_inc(UN.sem["tb"], 1)

            def round_(i, gp, last):
                R = i * 2 + gp
                for u in U:
                    c(R, u)
                    if not last or u < 7:
                        b(i, gp, u + 1)
                    if not last or u < 6:
                        a(R, u + 2)

            a(0, 0)
            a(0, 1)
            b(0, 0, 0)
            with ve.Fori(0, 3) as i:
                round_(i, 0, False)
                round_(i, 1, False)
            round_(3, 0, False)
            round_(3, 1, True)

            def pair(r):
                def pre(c):
                    b = c % 2
                    ve.wait_ge(XA.sem, XA.at(f"B{c}", r))
                    if c >= 2:
                        ve.wait_ge(XP.sem, XP.at(f"k2{b}", r))
                    ve.tensor_tensor(hid_s[b].rearrange("p (g n) -> p g n", g=4)[:, :, 0:NCMP],
                                     ps[:, 2 * b, :].rearrange("p (g n) -> p g n", g=4)[:, :, 0:NCMP],
                                     bs_s[b].rearrange("p (g n) -> p g n", g=4)[:, :, 1:NC], ALU.add).then_inc(XD.sem, 1)

                def step(name, op):
                    op.then_inc(XD.sem, 1)
                    ve.wait_ge(XD.sem, XD.at(name, r))

                pre(0)
                pre(1)
                for b in range(2):
                    ve.wait_ge(XP.sem, XP.at("k21", r))
                    ve.tensor_copy(kcc[:, b, :, 0:NCMP], ps[:, 4, b * 256:b * 256 + 254].rearrange("p (g n) -> p g n", g=2)).then_inc(XD.sem, 1)
                ve.wait_ge(XP.sem, XP.at("sc", r))
                ve.tensor_reduce(s_nm[:, 0:1], ps[:, 6, 0:NCMP], AX.X, ALU.max, negate=True).then_inc(XD.sem, 1)
                ve.wait_ge(XA.sem, XA.at("ce", r))
                step("crc", ve.reciprocal(s_fac[:, 0:1], s_sum[:, 0:1]))
                ve.tensor_scalar(pc[:, 0:NCMP], pc[:, 0:NCMP], s_fac[:, 0:1], None, ALU.mult).then_inc(XD.sem, 1)
                pre(2)
                pre(3)
                ve.wait_ge(XP.sem, XP.at("J", r))
                step("pj", ve.tensor_copy(pj[:, 1:1 + NCMP], ps[:, 6, 128:128 + NCMP]))
                step("im", ve.tensor_reduce(score, pj[:, 0:132].rearrange("p (m n) -> p m n", n=4), AX.X, ALU.add))
                step("sc1", ve.tensor_tensor(score, score, pj[:, 4:136].rearrange("p (m n) -> p m n", n=4)[:, :, 0], ALU.add))
                step("sc2", ve.tensor_tensor(score, score, K["bonus"], ALU.add))
                other = score.unsqueeze(1).to_broadcast([128, NSLC, NSLC])
                own = score.unsqueeze(2).to_broadcast([128, NSLC, NSLC])
                step("eq", ve.tensor_tensor(cmpx, other, own, ALU.is_equal))
                step("tri", ve.tensor_tensor(cmpx, cmpx, K["earlier"].rearrange("p (m n) -> p m n", m=NSLC), ALU.mult))
                step("r1", ve.tensor_reduce(rank_a, cmpx, AX.X, ALU.add))
                step("gt", ve.tensor_tensor(cmpx, other, own, ALU.is_gt))
                step("r2", ve.tensor_reduce(rank_b, cmpx, AX.X, ALU.add))
                step("rk", ve.tensor_tensor(rank_a, rank_a, rank_b, ALU.add))
                step("mk", ve.tensor_scalar(rank_a, rank_a, TOPN - 0.5, NEG, ALU.is_gt, ALU.mult))
                step("cf", ve.tensor_copy(s_fac[:, 0:1].unsqueeze(1), growv[:, 0:1, bass.ds(r, 1)]))
                ve.tensor_scalar(pc[:, 0:NCMP], pc[:, 0:NCMP], s_fac[:, 0:1], None, ALU.mult).then_inc(XD.sem, 1)
                for b in range(2):
                    ve.wait_ge(XP.sem, XP.at("v21", r))
                    ve.tensor_copy(vcc[0:NCMP, b, :], ps[0:NCMP, 5, b * 256:b * 256 + 256]).then_inc(XD.sem, 1)
                ve.wait_ge(XP.sem, XP.at("ss1", r))
                ve.tensor_tensor(sc_s[:, 0:2048].rearrange("p (m n) -> p m n", n=64),
                                 ps[:, 0:4, :].rearrange("p k (m n) -> p (k m) n", n=64),
                                 rank_a[:, 0:32].unsqueeze(2).to_broadcast([128, 32, 64]), ALU.add).then_inc(XD.sem, 1)
                fm = K["fresh_mask"].rearrange("p (w t) -> p w t", w=4)[:, bass.ds(r, 1), :]
                step("sf", ve.tensor_tensor(sc_s[:, 2048:2080].unsqueeze(1), ps[:, 4, 0:32].unsqueeze(1), fm, ALU.add))
                ve.tensor_reduce(s_nm[:, 1:2], sc_s, AX.X, ALU.max, negate=True).then_inc(XD.sem, 1)
                ve.wait_ge(XP.sem, XP.at("ws", r))
                ve.tensor_tensor(sc_w[:, 0:32], ps[:, 5, 0:32], K["win_mask"], ALU.add)
                ve.tensor_copy(sc_w[:, 32:512], ps[:, 5, 32:512]).then_inc(XD.sem, 1)
                step("wf", ve.tensor_tensor(sc_w[:, 512:544].unsqueeze(1), ps[:, 7, 256:288].unsqueeze(1), fm, ALU.add))
                ve.tensor_reduce(s_nm[:, 2:3], sc_w, AX.X, ALU.max, negate=True).then_inc(XD.sem, 1)
                for k, (name, buf) in enumerate((("s", sc_s), ("w", sc_w))):
                    f = s_fac[:, 1 + k:2 + k]
                    ve.wait_ge(XA.sem, XA.at(name + "e", r))
                    step(name + "rc", ve.reciprocal(f, s_sum[:, 1 + k:2 + k]))
                    step(name + "fa", ve.tensor_tensor(f.unsqueeze(1), f.unsqueeze(1), growv[:, 1 + k:2 + k, bass.ds(r, 1)], ALU.mult))
                    ve.tensor_scalar(buf, buf, f, None, ALU.mult).then_inc(XD.sem, 1)
                for q in range(2):
                    ve.wait_ge(XP.sem, XP.at(f"ts{q}", r))
                    ve.tensor_copy(pt4(q), ps[:, q, :]).then_inc(XD.sem, 1)
                ve.wait_ge(XP.sem, XP.at("pv1", r))
                ve.tensor_copy(sc_w[:, 0:256], ps[:, 7, 0:256]).then_inc(XD.sem, 1)
                ve.wait_ge(XP.sem, XP.at("po", r))
                src = ps[:, 7, 256:512].rearrange("p (G b g h j t) -> p G b g h j t", G=2, b=2, g=2, h=2, j=4)
                for g in range(2):
                    for h in range(2):
                        dst = big[64 * h:64 * h + 64, 4 * g:4 * g + 4, bass.ds(SEQ + r * 8, 8)]
                        op = ve.tensor_copy(dst.rearrange("p j (b t) -> p b j t", b=2), src[64 * h:64 * h + 64, g, :, g, h, :, :])
                op.then_inc(XD.sem, 1)

            with ve.Fori(0, 4) as r:
                pair(r)
            lo(PB["out1"], 0, None)
            for u in range(2):
                ve.wait_ge(att_hi, u + 1)
                ve.tensor_tensor(bigs[:, ATT_L + 4 * u:ATT_L + 4 * u + 4, :], big[:, 4 * u:4 * u + 4, :],
                                 as_f32(bigs[:, ATT_H + 4 * u:ATT_H + 4 * u + 4, :]), ALU.subtract).then_inc(att_lo, 1)
            lo(PB["out1"] + 1, 1, None)

        def NSA_POOL(po, stores, hist_store):
            po.wait_ge(ln_x, 16)
            po.dma_start(w1, A["w1"]).then_inc(w1_in, 16)
            po.wait_ge(freed[0], SB["out1"])
            po.wait_ge(freed[1], SB["out1"])
            po.dma_start(A["o_kv"], big[:, KVR:KVR + 12, :]).then_inc(kv_store, 16)
            for b in range(NB):
                po.dma_start(A["o_win_k"][b, :, :, W - NT:W], big[:, KW:KW + 2, SEQ + b * NT:SEQ + b * NT + NT]).then_inc(kv_store, 16)
            po.wait_ge(ND.sem, ND.at("F"))
            for b in range(NB):
                po.dma_start(A["o_win_v"][b, W - NT:W, :], fresh_v[b * NT:b * NT + NT, 1, :]).then_inc(kv_store, 16)
            po.wait_ge(kv_store, 16 * (1 + 2 * NB))
            po.wait_ge(out_free, 9)
            po.wait_ge(tab_in, 16)
            po.memset(qb, 0.0).then_inc(smp_zero, 1)
            po.memset(pj, 0.0).then_inc(smp_zero, 1)
            po.wait_ge(smp_zero, 2)
            po.sem_inc(smp_zero, 1)

            def pair(r):
                prev = not (isinstance(r, int) and r == 0)
                if prev:
                    po.wait_ge(XP.sem, XP.at("pv1", r - 1))
                    po.wait_ge(win_out, 128 * r)
                for g in range(2):
                    for h in range(2):
                        src = big[64 * h:64 * h + 64, 4 * g:4 * g + 4, bass.ds(SEQ + r * 8, 8)].rearrange("p j (b t) -> p b j t", b=2)
                        c0 = g * 32 + h * 16
                        op = po.tensor_copy(qb[64 * h:64 * h + 64, :, g, c0:c0 + 16].rearrange("p b (j t) -> p b j t", j=4), src)
                op.then_inc(XQ, 1)
                for b in range(2):
                    load_pages(po, "cmp_v", 2 + b, r, b)
                for b in range(2):
                    po.dma_start(win_k[:, b, :, :], A["win_k"][bass.ds(r * 2 + b, 1), :, :, :].rearrange("a p g n -> (a p) g n")).then_inc(win_in, 16)
                    for q in range(2):
                        po.dma_start(big[:, 12 + 2 * b + q, 0:512].rearrange("p (t n) -> p t n", t=2),
                                     A["win_v"][bass.ds(r * 2 + b, 1), 2 * q:2 * q + 2, :, :].rearrange("a t p n -> p (a t) n")).then_inc(win_in, 16)
                for b in range(2):
                    po.wait_ge(XP.sem, XP.at(f"cv{b}", r))
                    po.sem_inc(turn_v, 1)
                    load_pages(po, "slc_v", 2 + b, r, b)
                po.wait_ge(win_in, 96 * (r + 1))
                po.sem_inc(turn_v, 1)
                for b in range(2):
                    po.dma_start(A["o_win_k"][bass.ds(r * 2 + b, 1), :, :, 0:W - NT].rearrange("a p g n -> (a p) g n"),
                                 win_k[:, b, :, NT:W]).then_inc(win_out, 16)
                    ov = A["o_win_v"][bass.ds(r * 2 + b, 1), :, :]
                    wv = big[:, 12 + 2 * b:14 + 2 * b, 0:512]
                    po.dma_start(ov[:, 0:124, :].rearrange("a p n -> (a p) n"), wv[NT:128, 0, 0:256]).then_inc(win_out, 16)
                    po.dma_start(ov[:, 124:252, :].rearrange("a p n -> (a p) n"), wv[:, 0, 256:512]).then_inc(win_out, 16)
                    po.dma_start(ov[:, 252:508, :].rearrange("a (t p) n -> p (a t) n", t=2),
                                 wv[:, 1, :].rearrange("p (t n) -> p t n", t=2)).then_inc(win_out, 16)

            pair(0)
            with po.Fori(1, 4) as r:
                pair(r)
            po.wait_ge(win_out, 128 * 4)
            po.wait_ge(XQ, 4)
            return stores
        block = ctx.enter_context(nc.Block())

        @block.sync
        def _(sp):

            def piece(n, s, src, size):
                if not (isinstance(n, int) and n < 4):
                    sp.wait_ge(w_lo, n - 3)
                sp.dma_start(raw[s][:, 0:size], src).then_inc(w_in[s], 16)

            def stream(name, first=False):
                w = A["w_" + name]
                count = dict((g[0], g[1]) for g in GEMMS)[name]
                if name.startswith("down"):
                    with sp.Fori(0, 2) as i:
                        for q in range(12):
                            m, part = q // 3, q % 3
                            size = (8, 8, 6)[part] * 128
                            piece(PB[name] + i * 12 + q, q % 4,
                                  w[bass.ds(i * 4 + m, 1), :, part * 1024:part * 1024 + size].rearrange("m p n -> (m p) n"), size)
                    return
                start = 0
                if first:
                    for s in range(4):
                        piece(s, s, w[s], 1024)
                        if s == 0:
                            for k in range(0, KC, 2):
                                sp.dma_start(big[:, 20 + k:22 + k, :], A["xT"][:, k:k + 2, :]).then_inc(x_in[k // 2], 16)
                    start = 1
                if name == "out1":
                    piece(PB[name], 0, w[0], 1024)
                    sp.wait_ge(XD.sem, XD.at("ov", 3))
                    for s in range(1, 4):
                        piece(PB[name] + s, s, w[s], 1024)
                    start = 1
                with sp.Fori(start, count // 4) as i:
                    for s in range(4):
                        piece(PB[name] + i * 4 + s, s, w[bass.ds(i * 4 + s, 1), :, :].rearrange("m p n -> (m p) n"), 1024)

            stream("in0", True)
            for name in ("out0", "up0", "down0"):
                stream(name)
            NSA_SP(sp, stream)
            for name in ("up1", "down1"):
                stream(name)

        @block.tensor
        def _(pe):
            def stripe(psum_set, slot, ks, rhs, start, stop, ready=None):
                for k in range(ks):
                    if ready:
                        ready(k)
                    for w_part, v_part in ((0, 0), (0, 1), (1, 0)):
                        for h in range(2):
                            mm = pe.matmul(ps[:, 2 * psum_set + h, 0:HT], split[:, slot % 2, w_part, k * 128:(k + 1) * 128],
                                           rhs(k)[v_part][:, h * HT:(h + 1) * HT],
                                           start=start and k == 0 and w_part + v_part == 0,
                                           stop=stop and k == ks - 1 and w_part == 1)
                return mm

            def product(name, rhs, ready=None):
                count = dict((g[0], g[1]) for g in GEMMS)[name]
                if name.startswith("down"):
                    layer = int(name[-1])
                    with pe.Fori(0, 2) as i:
                        for q in range(12):
                            m, part = q // 3, q % 3
                            pe.wait_ge(w_lo, PB[name] + i * 12 + (q + 1))
                            pe.wait_ge(hid_lo, FC * layer + (8, 16, FC)[part])
                            if part == 0:
                                pe.wait_ge(freed[m % 2], SB[name] + i * 2 + m // 2)
                            stripe(m % 2, q % 4, (8, 8, 6)[part], lambda k: rhs(part * 8 + k),
                                   part == 0, part == 2).then_inc(pieces, 1)
                    return

                def four(i, peeled):
                    for s in range(4):
                        pe.wait_ge(w_lo, PB[name] + i * 4 + (s + 1))
                        if not (peeled and name == "in0") or s >= 2:
                            pe.wait_ge(freed[s % 2], SB[name] + i * 2 + s // 2)
                        stripe(s % 2, s, KC, rhs, True, True, ready if peeled and s == 0 else None).then_inc(pieces, 1)

                if ready:
                    four(0, True)
                with pe.Fori(1 if ready else 0, count // 4) as i:
                    four(i, False)

            def norm_sums(r):
                pe.wait_ge(ln_sum, 8 * (r + 1))
                for h in range(2):
                    mm = pe.matmul(ps[:, 4 + h, 0:HT], K["mean_d"], ln_row(r, 0)[:, h * HT:(h + 1) * HT], start=True, stop=True)
                mm.then_inc(ln_mean, 1)
                for m in range(KC):
                    pe.wait_ge(ln_sq, 8 * r + m + 1)
                    for h in range(2):
                        mm = pe.matmul(ps[:, 6 + h, 0:HT], K["mean_d"], big[:, m, h * HT:(h + 1) * HT],
                                       start=m == 0, stop=m == KC - 1)
                mm.then_inc(ln_var, 1)

            def x_parts(k):
                return xhs[:, k, :], xls[:, k, :]

            def normed(r):
                return lambda k: pe.wait_ge(ln_x, 8 * r + k + 1)

            product("in0", x_parts, lambda k: pe.wait_ge(x0_lo, k + 1))

            pe.wait_ge(early_in, 16)
            pe.wait_ge(freed[0], 14)
            pe.wait_ge(freed[1], 14)
            for n in range(8):
                if n >= 2:
                    pe.wait_ge(RD.sem, RD.at("sin", n - 2))
                for h in range(2):
                    mm = pe.matmul(ps[:, 4 + 2 * (n % 2) + h, 0:HT], K["swap"], big[:, n, h * HT:(h + 1) * HT],
                                   start=True, stop=True)
                mm.then_inc(rope_pe, 1)

            pe.wait_ge(consts_in, 32)
            pe.wait_ge(RD.sem, RD.at("add", 7))
            for c in range(4):
                tok = slice(c * 128, c * 128 + 128)
                if c:
                    pe.wait_ge(RV.sem, RV.at("kn", c - 1))
                for h in range(RH):
                    mm = pe.transpose(ps[:, 4, h * 128:(h + 1) * 128], big[:, KZ + h, tok], K["ident"])
                mm.then_inc(RP.sem, 1)
                if c:
                    pe.wait_ge(RA.sem, RA.at("vn", c - 1))
                for h in range(RH):
                    mm = pe.transpose(ps[:, 5, h * 128:(h + 1) * 128], big[:, VZ + h, tok], K["ident"])
                mm.then_inc(RP.sem, 1)
                if c:
                    pe.wait_ge(RV.sem, RV.at("st", c - 1))
                for h in range(RH):
                    mm = pe.matmul(ps[:, 6, h * 128:(h + 1) * 128], big[:, KZ + h, tok], big[:, QZ + h, tok],
                                   start=True, stop=True)
                mm.then_inc(RP.sem, 1)
                pe.wait_ge(RV.sem, RV.at("qd", c))
                pe.wait_ge(RA.sem, RA.at("vn", c))
                if c:
                    pe.wait_ge(RA.sem, RA.at("o", c - 1))
                    pe.wait_ge(RV.sem, RV.at("state", c - 1))
                for h in range(RH):
                    hs = slice(h * 128, h * 128 + 128)
                    mm = pe.matmul(ps[:, 7, hs], v_nat[:, hs], s_dec[:, hs], start=True, stop=c == 0)
                    if c:
                        mm = pe.matmul(ps[:, 7, hs], state[:, hs], q_dec[:, hs], start=False, stop=True)
                mm.then_inc(RP.sem, 1)
                for h in range(RH):
                    hs = slice(h * 128, h * 128 + 128)
                    mm = pe.matmul(ps[:, 0, hs], k_nat[:, hs], v_nat[:, hs], start=True, stop=True)
                mm.then_inc(RP.sem, 1)

            tok = slice(SEQ, T)
            pe.wait_ge(RV.sem, RV.at("state", 3))
            pe.wait_ge(RA.sem, RA.at("o", 3))
            for h in range(RH):
                mm = pe.transpose(ps[0:32, 4, h * 128:(h + 1) * 128], big[:, KZ + h, tok], K["ident"])
            mm.then_inc(SP_.sem, 1)
            for h in range(RH):
                mm = pe.transpose(ps[0:32, 5, h * 128:(h + 1) * 128], big[:, VZ + h, tok], K["ident"])
            mm.then_inc(SP_.sem, 1)
            for h in range(RH):
                mm = pe.matmul(ps[0:32, 6, h * 32:(h + 1) * 32], big[:, KZ + h, tok], big[:, QZ + h, tok],
                               start=True, stop=True)
            mm.then_inc(SP_.sem, 1)
            pe.wait_ge(ret_in, 16)
            pe.wait_ge(SV.sem, SV.at("qd"))
            pe.wait_ge(SA.sem, SA.at("vn"))
            for h in range(RH):
                hs = slice(h * 128, h * 128 + 128)
                pe.matmul(ps[:, 7, h * 32:(h + 1) * 32], v_nat[0:32, hs], s_dec[0:32, h * 32:h * 32 + 32],
                          start=True, stop=True, skip_group_check=True)
                for b in range(NB):
                    cs = slice(h * 32 + b * NT, h * 32 + b * NT + NT)
                    mm = pe.matmul(ps[:, 7, cs], ret_states[:, b, h, :], q_dec[:, cs], start=False, stop=True,
                                   skip_group_check=True)
            mm.then_inc(SP_.sem, 1)
            for h in range(RH):
                pe.wait_ge(SV.sem, SV.at("vb") + h)
                for u in range(2):
                    n = 2 * h + u
                    if n >= 2:
                        pe.wait_ge(st_s, n - 1)
                    mm = pe.matmul(ps[:, n % 2, :], k_nat[0:32, h * 128:(h + 1) * 128], v_blk[0:32, u * 512:(u + 1) * 512],
                                   start=True, stop=True).then_inc(kv_s, 1)

            pe.wait_ge(SA.sem, SA.at("o"))
            def gn_mean(h):
                at = 4 if h % 2 == 0 else 0
                if h >= 2:
                    pe.wait_ge(GN["cen"], h - 1)
                elif h:
                    pe.wait_ge(st_s, 8)
                for u in range(2):
                    mm = pe.matmul(ps[:, at + u, 0:HT], K["mean_h"], big[:, QZ + h, u * HT:(u + 1) * HT], start=True, stop=True)
                mm.then_inc(GN["mean"], 1)

            def gn_var(h):
                at = 6 if h % 2 == 0 else 2
                pe.wait_ge(GN["sq"], h + 1)
                if h >= 2:
                    pe.wait_ge(GN["std"], h - 1)
                for u in range(2):
                    mm = pe.matmul(ps[:, at + u, 0:HT], K["mean_h"], gn_sq[h % 2][:, u * HT:(u + 1) * HT], start=True, stop=True)
                mm.then_inc(GN["var"], 1)

            gn_mean(0)
            gn_mean(1)
            gn_var(0)
            gn_mean(2)
            gn_var(1)
            gn_mean(3)
            gn_var(2)
            gn_var(3)

            product("out0", lambda k: (bigs[:, MIX_H + k, :], bigs[:, MIX_L[k], :]),
                    lambda k: pe.wait_ge(mix_lo, 1 if k < 4 else k - 2))
            norm_sums(0)
            for layer in range(2):
                product(f"up{layer}", x_parts, normed(2 * layer))
                product(f"down{layer}", lambda k: (bigs[:, k, :], hid_l[:, k, :]))
                norm_sums(2 * layer + 1)
                if layer == 0:
                    product("in1", x_parts, normed(1))
                    NSA_PE(pe, product)
                    norm_sums(2)

        @block.scalar
        def _(act):
            def hi(n, s, turn, size=1024):
                act.wait_ge(w_in[s], 16 * turn)
                if not (isinstance(n, int) and (n < 2 or n in (PB["out1"], PB["out1"] + 1))):
                    act.wait_ge(pieces, n - 1)
                act.activation(split[:, s % 2, 0, 0:size], raw[s][:, 0:size], ACT.Copy).then_inc(w_hi, 1)

            def take_even(name, i, s, scale=1.0):
                act.wait_ge(pieces, PB[name] + i * 4 + (s + 1))
                act.activation(half2(big[:, bass.ds(i * 4 + s, 1), :]), pset(0), ACT.Copy, scale=scale).then_inc(freed[0], 1)

            def half2(v):
                return v.rearrange("p a (h t) -> p (a h) t", h=2)

            hi(0, 0, 1)
            for k in range(KC):
                act.wait_ge(x_in[k // 2], 16)
                act.activation(xhs[:, k, :], big[:, 20 + k, :], ACT.Copy).then_inc(x0_hi, 1)
            hi(1, 1, 1)
            act.dma_start(keep_all, A["keep"]).then_inc(consts_in, 16)
            act.dma_start(vec_all, A["vecs"]).then_inc(consts_in, 16)
            act.dma_start(early_all, A["early"]).then_inc(early_in, 16)
            act.dma_start(ret_states, A["state_ret"]).then_inc(ret_in, 16)
            act.dma_start(sconv_hist, A["state_sconv"]).then_inc(hist_in, 16)
            act.dma_start(wg, A["w_gate"].rearrange("p k n -> p (k n)")).then_inc(nsa_in, 16)
            act.dma_start(w2, A["w2"]).then_inc(nsa_in, 16)
            feed(act, hi, "in0", lambda i, q: take_even("in0", i, q) if q % 2 == 0 else None)
            act.wait_ge(nsa_in, 32)
            act.activation(wg_h.rearrange("p k n -> p (k n)"), wg, ACT.Copy).then_inc(wg_hi, 1)
            for c in range(4):
                tok = slice(c * 128, c * 128 + 128)
                act.wait_ge(RP.sem, RP.at("vT", c))
                if c:
                    act.wait_ge(RP.sem, RP.at("kv", c - 1))
                act.activation(v_nat[:, :], ps[:, 5, :], ACT.Copy).then_inc(RA.sem, 1)
                act.wait_ge(RP.sem, RP.at("o", c))
                act.activation(big[:, QZ:QZ + 4, tok], ps[:, 7, :].rearrange("p (h n) -> p h n", h=4), ACT.Copy).then_inc(RA.sem, 1)
            act.wait_ge(SP_.sem, SP_.at("vT"))
            act.wait_ge(RP.sem, RP.at("kv", 3))
            act.activation(v_nat[0:32, :], ps[0:32, 5, :], ACT.Copy).then_inc(SA.sem, 1)
            act.wait_ge(SP_.sem, SP_.at("o"))
            act.activation(big[:, QZ:QZ + 4, SEQ:T], ps[:, 7, 0:128].rearrange("p (h n) -> p h n", h=4), ACT.Copy).then_inc(SA.sem, 1)
            act.wait_ge(freed[1], 14)
            act.wait_ge(RP.sem, RP.at("kv", 3))
            act.activation(big[:, GZ:GZ + 4, :], big[:, GZ:GZ + 4, :], ACT.Silu).then_inc(gn_gate, 1)
            act.wait_ge(ya.sem, ya.at("ys", 3))
            act.activation(bigs[:, MIX_H:MIX_H + 4, :], big[:, HZ:HZ + 4, :], ACT.Copy).then_inc(mix_hi, 1)
            act.wait_ge(pool_set, 1)

            def head_hi(h):
                act.wait_ge(GN["mul"], h + 1)
                act.activation(bigs[:, MIX_H + 4 + h, :], big[:, QZ + h, :], ACT.Copy).then_inc(mix_hi, 1)

            def gn_square(h):
                act.wait_ge(GN["cen"], h + 1)
                if h >= 2:
                    act.wait_ge(GN["var"], h - 1)
                act.activation(gn_sq[h % 2], big[:, QZ + h, :], ACT.Square).then_inc(GN["sq"], 1)

            def gn_std(h):
                at = 6 if h % 2 == 0 else 2
                act.wait_ge(GN["var"], h + 1)
                if h >= 2:
                    act.wait_ge(GN["nrm"], h - 1)
                act.activation(half(gn_sd[h % 2]), ps[:, at:at + 2, 0:HT], ACT.Sqrt, bias=eps[:, 0:1]).then_inc(GN["std"], 1)

            gn_square(0)
            gn_square(1)
            gn_std(0)
            gn_std(1)
            for h in range(2, RH):
                gn_square(h)
                head_hi(h - 2)
                gn_std(h)
            head_hi(RH - 2)
            head_hi(RH - 1)

            def norm(r):
                for m in range(KC):
                    act.wait_ge(ln_cen, 8 * r + m + 1)
                    act.activation(big[:, m, :], y[:, m, :], ACT.Square).then_inc(ln_sq, 1)
                act.wait_ge(ln_var, r + 1)
                act.activation(half(ln_row(r, 1)), ps[:, 6:8, 0:HT], ACT.Sqrt, bias=eps[:, 0:1]).then_inc(ln_std, 1)
                for m in range(KC):
                    g, b = (K[v][:, 8 * r + m:8 * r + m + 1] for v in ("ln_g", "ln_b"))
                    act.wait_ge(ln_nrm, 8 * r + m + 1)
                    op = act.activation(big[:, m, :], y[:, m, :], ACT.Identity, scale=g, bias=b)
                    if r < 3:
                        op = act.activation(xhs[:, m, :], y[:, m, :], ACT.Identity, scale=g, bias=b)
                    op.then_inc(ln_hi, 1)

            def ffn(layer):
                name = f"up{layer}"
                base = layer * FC

                def row(jb, u, peeled):
                    j = jb * 2 + u
                    hi(PB[name] + jb * 4 + (2 * u + 2), (2 * u + 2) % 4, PB[name] // 4 + jb + (1 + (u + 1) // 2))
                    if not peeled:
                        act.wait_ge(fd.sem, fd.at("c2", j + base - 2))
                        act.wait_ge(fp.sem, fp.at("out", j + base - 2))
                    act.activation(ffn_a[:, u, 2:2 + HT], ps[:, 0, 0:HT], ACT.Copy)
                    act.activation(ffn_a[:, u, 2 + HT:SO], ps[:, 1, 0:SEQ - HT], ACT.Copy)
                    act.activation(ffn_a[:, u, SO:CW].rearrange("p (b w) -> p b w", b=NB)[:, :, 2:6],
                                   ps[:, 1, SEQ - HT:HT].rearrange("p (b w) -> p b w", b=NB), ACT.Copy).then_inc(freed[0], 1)

                def gelu(jb, u, peeled):
                    j = jb * 2 + u
                    act.wait_ge(fd.sem, fd.at("c2", j + base))
                    if not peeled:
                        act.wait_ge(freed[1], SB[name] + j - 1)
                    act.activation(ffn_g[:, u, 0:SEQ], ffn_c[:, u, 0:SEQ], ACT.Gelu_apprx_tanh)
                    act.activation(ffn_g[:, u, SEQ:T].rearrange("p (b w) -> p b w", b=NB),
                                   conv_sample(ffn_c[:, u, :]),
                                   ACT.Gelu_apprx_tanh).then_inc(fa.sem, 1)
                    hi(PB[name] + jb * 4 + (2 * u + 3), (2 * u + 3) % 4, PB[name] // 4 + jb + (1 + (u + 1) // 2))
                    act.wait_ge(freed[1], SB[name] + j + 1)
                    act.activation(bigs[:, bass.ds(j, 1), :], big[:, 22 + u:23 + u, :], ACT.Copy).then_inc(hid_hi, 1)

                row(0, 0, True)
                gelu(0, 0, True)
                row(0, 1, True)
                gelu(0, 1, True)
                with act.Fori(1, FC // 2) as jb:
                    row(jb, 0, False)
                    gelu(jb, 0, False)
                    row(jb, 1, False)
                    gelu(jb, 1, False)

            feed(act, hi, "out0", None)
            norm(0)
            ffn(0)
            feed(act, hi, "down0", None)
            norm(1)
            NSA_ACT(act, take_even, hi)
            feed(act, hi, "out1", None)
            norm(2)
            ffn(1)
            feed(act, hi, "down1", None, True)
            norm(3)
            act.wait_ge(ln_hi, 32)
            act.dma_start(A["o_x"], big[:, 0:KC, :]).then_inc(out_done, 16)
            act.wait_ge(out_done, 16)

        @block.vector
        def _(ve):
            def lo(n, s, turn, size=1024):
                ve.wait_ge(w_hi, n + 1)
                ve.tensor_tensor(split[:, s % 2, 1, 0:size], raw[s][:, 0:size], as_f32(split[:, s % 2, 0, 0:size]),
                                 ALU.subtract).then_inc(w_lo, 1)

            def take_odd(name, i, s, scale=None):
                ve.wait_ge(pieces, PB[name] + i * 4 + (s + 1))
                dst = big[:, bass.ds(i * 4 + s, 1), :].rearrange("p a (h t) -> p (a h) t", h=2)
                if scale is None:
                    ve.tensor_copy(dst, pset(1)).then_inc(freed[1], 1)
                else:
                    ve.tensor_scalar(dst, pset(1), scale, None, ALU.mult).then_inc(freed[1], 1)

            lo(0, 0, 1)
            for k in range(KC):
                ve.wait_ge(x0_hi, k + 1)
                ve.tensor_tensor(xls[:, k, :], big[:, 20 + k, :], as_f32(xhs[:, k, :]), ALU.subtract).then_inc(x0_lo, 1)
            lo(1, 1, 1)
            feed(ve, lo, "in0", lambda i, q: take_odd("in0", i, q) if q % 2 else None)
            ve.wait_ge(early_in, 16)
            ve.wait_ge(freed[0], 14)
            for n in range(8):
                ve.wait_ge(rope_pe, n + 1)
                if n:
                    ve.wait_ge(RD.sem, RD.at("add", n - 1))
                ve.tensor_tensor(half(rope_t), ps[:, 4 + 2 * (n % 2):6 + 2 * (n % 2), 0:HT], half(K["rope_sin"]),
                                 ALU.mult).then_inc(RD.sem, 1)
                ve.tensor_tensor(big[:, n, :], big[:, n, :], K["rope_cos"], ALU.mult).then_inc(RD.sem, 1)
                ve.wait_ge(RD.sem, RD.at("cos", n))
                ve.tensor_tensor(big[:, n, :], big[:, n, :], rope_t, ALU.add).then_inc(RD.sem, 1)
            ve.wait_ge(RD.sem, RD.at("add", 7))
            gam = np.exp(128 * np.log1p(-np.exp2(-5.0 - np.arange(RH))))
            gam4 = np.exp(NT * np.log1p(-np.exp2(-5.0 - np.arange(RH))))

            def by_head(v, n=128):
                return v.rearrange("p (h n) -> p h n", h=RH)

            for c in range(4):
                tok = slice(c * 128, c * 128 + 128)
                ve.wait_ge(RP.sem, RP.at("kT", c))
                if c:
                    ve.wait_ge(RP.sem, RP.at("kv", c - 1))
                ve.tensor_tensor(by_head(k_nat), by_head(ps[:, 4, :]),
                                 K["kdec"].unsqueeze(2).to_broadcast([128, RH, 128]), ALU.mult).then_inc(RV.sem, 1)
                ve.wait_ge(RP.sem, RP.at("sc", c))
                ve.tensor_tensor(s_dec, ps[:, 6, :], K["decay"], ALU.mult).then_inc(RV.sem, 1)
                ve.tensor_tensor(by_head(q_dec), big[:, QZ:QZ + 4, tok], by_head(K["qdec"]), ALU.mult).then_inc(RV.sem, 1)
                ve.wait_ge(RP.sem, RP.at("kv", c))
                if c == 0:
                    ve.tensor_copy(state, ps[:, 0, :]).then_inc(RV.sem, 1)
                else:
                    ve.wait_ge(RV.sem, RV.at("state", c - 1))
                    for h in range(RH):
                        hs = slice(h * 128, h * 128 + 128)
                        op = ve.scalar_tensor_tensor(out=state[:, hs], in0=state[:, hs], scalar=float(gam[h]),
                                                     in1=ps[:, 0, hs], op0=ALU.mult, op1=ALU.add)
                    op.then_inc(RV.sem, 1)
            ve.wait_ge(SP_.sem, SP_.at("kT"))
            ve.tensor_tensor(k_nat[0:32, :].rearrange("p (h n) -> p h n", h=RH), ps[0:32, 4, :].rearrange("p (h n) -> p h n", h=RH),
                             K["kdec_s"][0:32, :].unsqueeze(2).to_broadcast([32, RH, 128]), ALU.mult).then_inc(SV.sem, 1)
            ve.wait_ge(SP_.sem, SP_.at("sc"))
            ve.tensor_tensor(s_dec[0:32, 0:128], ps[0:32, 6, 0:128], K["decay_s"][0:32, :], ALU.mult).then_inc(SV.sem, 1)
            ve.tensor_tensor(q_dec[:, 0:128].rearrange("p (h n) -> p h n", h=RH), big[:, QZ:QZ + 4, SEQ:T],
                             K["qdec_s"].rearrange("p (h n) -> p h n", h=RH), ALU.mult).then_inc(SV.sem, 1)
            ve.wait_ge(SA.sem, SA.at("vn"))
            for h in range(RH):
                if h:
                    ve.wait_ge(kv_s, 2 * h)
                ve.tensor_tensor(v_blk[0:32, :].rearrange("p (b e) -> p b e", b=NB),
                                 v_nat[0:32, h * 128:(h + 1) * 128].unsqueeze(1).to_broadcast([32, NB, 128]),
                                 K["seq_of"][0:32, :].unsqueeze(2).to_broadcast([32, NB, 128]), ALU.mult).then_inc(SV.sem, 1)
                for u in range(2):
                    ve.wait_ge(kv_s, 2 * h + u + 1)
                    ve.wait_ge(SP_.sem, SP_.at("o"))
                    st = ret_states[:, 4 * u:4 * u + 4, h, :]
                    ve.scalar_tensor_tensor(out=st, in0=st, scalar=float(gam4[h]),
                                            in1=ps[:, (2 * h + u) % 2, :].rearrange("p (b e) -> p b e", b=4),
                                            op0=ALU.mult, op1=ALU.add).then_inc(st_s, 1)
            ve.wait_ge(mix_hi, 1)
            ve.tensor_tensor(bigs[:, MIX_L[0]:MIX_L[3] + 1, :], big[:, HZ:HZ + 4, :], as_f32(bigs[:, MIX_H:MIX_H + 4, :]),
                             ALU.subtract).then_inc(mix_lo, 1)
            ve.wait_ge(wg_hi, 1)
            ve.tensor_tensor(wg_l.rearrange("p k n -> p (k n)"), wg, as_f32(wg_h.rearrange("p k n -> p (k n)")), ALU.subtract).then_inc(wg_lo, 1)

            def head_lo(h):
                ve.wait_ge(mix_hi, 2 + h)
                ve.tensor_tensor(bigs[:, MIX_L[4 + h], :], big[:, QZ + h, :], as_f32(bigs[:, MIX_H + 4 + h, :]),
                                 ALU.subtract).then_inc(mix_lo, 1)

            def gn_center(h):
                o, at = big[:, QZ + h, :], 4 if h % 2 == 0 else 0
                ve.wait_ge(GN["mean"], h + 1)
                ve.tensor_tensor(half(o), half(o), ps[:, at:at + 2, 0:HT], ALU.subtract).then_inc(GN["cen"], 1)

            ve.wait_ge(consts_in, 32)
            gn_center(0)
            gn_center(1)
            for h in range(RH):
                o, sd = big[:, QZ + h, :], gn_sd[h % 2]
                ve.wait_ge(GN["std"], h + 1)
                ve.reciprocal(sd, sd).then_inc(GN["rs"], 1)
                ve.wait_ge(GN["rs"], h + 1)
                ve.wait_ge(GN["sq"], h + 1)
                ve.scalar_tensor_tensor(out=o, in0=o, scalar=K["gn_g"][:, h:h + 1], in1=sd, op0=ALU.mult,
                                        op1=ALU.mult).then_inc(GN["nrm"], 1)
                ve.wait_ge(GN["nrm"], h + 1)
                ve.wait_ge(gn_gate, 1)
                ve.tensor_tensor(o, o, big[:, GZ + h, :], ALU.mult).then_inc(GN["mul"], 1)
                if h + 2 < RH:
                    gn_center(h + 2)
                if h:
                    head_lo(h - 1)
            head_lo(RH - 1)

            def residual(name, stop=False):
                pp = 3 if name.startswith("down") else 1

                def take(i, q):
                    if q % pp != pp - 1:
                        return
                    m = q // pp
                    ve.wait_ge(pieces, PB[name] + i * 4 * pp + (q + 1))
                    row, rh, rl = (v[:, bass.ds(i * 4 + m, 1), :] for v in (y, xhs, xls))
                    ve.scalar_tensor_tensor(out=half1(row), in0=half1(as_f32(rh)), scalar=float(ALPHA), in1=pset(m % 2),
                                            op0=ALU.mult, op1=ALU.add).then_inc(freed[m % 2], 1)
                    ve.wait_ge(freed[m % 2], SB[name] + i * 2 + (m // 2 + 1))
                    ve.scalar_tensor_tensor(out=row, in0=as_f32(rl), scalar=float(ALPHA), in1=row,
                                            op0=ALU.mult, op1=ALU.add).then_inc(y_done, 1)

                feed(ve, lo, name, take, stop)

            def norm(r, name):
                residual(name, r == 3)
                ve.wait_ge(ln_mean, r + 1)
                for m in range(KC):
                    ve.tensor_tensor(half(y[:, m, :]), half(y[:, m, :]), ps[:, 4:6, 0:HT], ALU.subtract).then_inc(ln_cen, 1)
                ve.wait_ge(ln_std, r + 1)
                ve.reciprocal(ln_row(r, 1), ln_row(r, 1)).then_inc(ln_rs, 1)
                ve.wait_ge(ln_rs, r + 1)
                ve.wait_ge(ln_sq, 8 * r + 8)
                for m in range(KC + 1):
                    if m < KC:
                        ve.tensor_tensor(y[:, m, :], y[:, m, :], ln_row(r, 1), ALU.mult).then_inc(ln_nrm, 1)
                    if m and r < 3:
                        ve.wait_ge(ln_hi, 8 * r + m)
                        ve.tensor_tensor(xls[:, m - 1, :], big[:, m - 1, :], as_f32(xhs[:, m - 1, :]), ALU.subtract).then_inc(ln_x, 1)

            def ffn(layer):
                name = f"up{layer}"
                base = layer * FC
                cw = K["fconv"].rearrange("p (l c w) -> p l c w", l=2, c=FC)[:, layer, :, :]

                def row(jb, u, peeled):
                    j = jb * 2 + u
                    a, c = ffn_a[:, u, :], ffn_c[:, u, 0:CO]
                    w = cw[:, bass.ds(j, 1), :].rearrange("p a w -> p (a w)")
                    lo(PB[name] + jb * 4 + (2 * u + 2), (2 * u + 2) % 4, None)
                    ve.wait_ge(freed[0], SB[name] + j + 1)
                    ve.wait_ge(fp.sem, fp.at("in", j + base))
                    if not peeled:
                        ve.wait_ge(fa.sem, j + base - 1)
                    ve.tensor_scalar(c, a[:, 0:CO], w[:, 0:1], w[:, 3:4], ALU.mult, ALU.add).then_inc(fd.sem, 1)
                    for q in (1, 2):
                        ve.wait_ge(fd.sem, fd.at(f"c{q - 1}", j + base))
                        ve.scalar_tensor_tensor(out=c, in0=a[:, q:q + CO], scalar=w[:, q:q + 1], in1=c,
                                                op0=ALU.mult, op1=ALU.add).then_inc(fd.sem, 1)
                    lo(PB[name] + jb * 4 + (2 * u + 3), (2 * u + 3) % 4, None)
                    ve.wait_ge(pieces, PB[name] + jb * 4 + (2 * u + 2))
                    ve.wait_ge(fa.sem, j + base + 1)
                    h = big[:, 22 + u, :]
                    ve.tensor_tensor(half(h), half(ffn_g[:, u, :]), pset(1), ALU.mult).then_inc(freed[1], 1)
                    ve.wait_ge(hid_hi, j + base + 1)
                    ve.tensor_tensor(hid_l[:, bass.ds(j, 1), :], h.unsqueeze(1), as_f32(bigs[:, bass.ds(j, 1), :]),
                                     ALU.subtract).then_inc(hid_lo, 1)

                row(0, 0, True)
                row(0, 1, True)
                with ve.Fori(1, FC // 2) as jb:
                    row(jb, 0, False)
                    row(jb, 1, False)

            norm(0, "out0")
            ffn(0)
            ve.wait_ge(hist_store, 16 * 4)
            norm(1, "down0")
            NSA_DVE(ve, take_odd, lo)
            norm(2, "out1")
            ffn(1)
            ve.wait_ge(hist_store, 16 * 5)
            norm(3, "down1")

        @block.gpsimd
        def _(po):
            po.memset(eps, EPS).then_inc(pool_set, 1)
            po.memset(conv_u, 0.0).then_inc(zero_u, 1)
            po.wait_ge(zero_u, 1)
            po.wait_ge(hist_in, 16)
            po.wait_ge(consts_in, 32)
            sw = K["sconv"].rearrange("p (c w) -> p c w", c=4)
            us = conv_u[:, SO:CW].rearrange("p (b w) -> p b w", b=NB)
            for c in range(4):
                C_, H_, B_ = big[:, CZ + c, :], big[:, HZ + c, :], big[:, BZ + c, :]

                def sample(v):
                    return v[:, SEQ:T].rearrange("p (b w) -> p b w", b=NB)
                if c:
                    po.wait_ge(ya.sem, ya.at("ys", c - 1))
                po.tensor_copy(us[:, :, 0:2], sconv_hist[:, c, :, :]).then_inc(ya.sem, 1)
                po.wait_ge(freed[0], 14)
                po.wait_ge(freed[1], 14)
                po.tensor_tensor(conv_u[:, 2:SO], C_[:, 0:SEQ], H_[:, 0:SEQ], ALU.mult).then_inc(ya.sem, 1)
                po.tensor_tensor(us[:, :, 2:6], sample(C_), sample(H_), ALU.mult).then_inc(ya.sem, 1)
                po.wait_ge(ya.sem, ya.at("us", c))
                po.tensor_scalar(conv_c[:, 0:CO], conv_u[:, 0:CO], sw[:, c, 0:1], sw[:, c, 3:4], ALU.mult, ALU.add).then_inc(ya.sem, 1)
                for q in (1, 2):
                    po.tensor_scalar(conv_d, conv_u[:, q:q + CO], sw[:, c, q:q + 1], None, ALU.mult).then_inc(ya.sem, 1)
                    po.wait_ge(ya.sem, ya.at(f"t{q}", c))
                    po.tensor_tensor(conv_c[:, 0:CO], conv_c[:, 0:CO], conv_d, ALU.add).then_inc(ya.sem, 1)
                    po.wait_ge(ya.sem, ya.at(f"s{q}", c))
                po.tensor_copy(sconv_out[:, c, 0:2], conv_u[:, SEQ:SEQ + 2])
                po.tensor_copy(sconv_out[:, c, 2:18].rearrange("p (b w) -> p b w", b=NB), us[:, :, 4:6]).then_inc(ya.sem, 1)
                po.tensor_tensor(H_[:, 0:SEQ], conv_c[:, 0:SEQ], B_[:, 0:SEQ], ALU.mult).then_inc(ya.sem, 1)
                po.tensor_tensor(sample(H_), conv_sample(conv_c), sample(B_), ALU.mult).then_inc(ya.sem, 1)
            po.wait_ge(ya.sem, ya.at("ys", 3))
            po.dma_start(A["o_sconv"], sconv_out).then_inc(hist_store, 16)
            po.wait_ge(RV.sem, RV.at("state", 3))
            po.dma_start(A["o_ret_p"], state).then_inc(hist_store, 16)
            po.wait_ge(st_s, 8)
            po.dma_start(A["o_ret_s"], ret_states).then_inc(hist_store, 16)
            stores = 3

            def sums(r, name, stores):
                po.wait_ge(hist_store, 16 * stores)
                if r:
                    po.wait_ge(ln_mean, r)
                po.wait_ge(pieces, PB[name] + 1)
                po.memset(ln_row(r, 0), 0.0).then_inc(ln_zero, 1)
                po.wait_ge(ln_zero, r + 1)
                for m in range(KC):
                    po.wait_ge(y_done, 8 * r + m + 1)
                    if m:
                        po.wait_ge(ln_sum, 8 * r + m)
                    po.tensor_tensor(ln_row(r, 0), ln_row(r, 0), y[:, m, :], ALU.add).then_inc(ln_sum, 1)

            def ffn(layer, stores):
                name = f"up{layer}"
                base = layer * FC
                po.wait_ge(hist_store, 16 * stores)
                po.wait_ge(ln_x, 8 * (2 * layer + 1))
                po.memset(ffn_a[:, 0, 0:2], 0.0).then_inc(ffn_zero, 1)
                po.memset(ffn_a[:, 1, 0:2], 0.0).then_inc(ffn_zero, 1)
                po.dma_start(ffn_hist, A["state_ffn"][layer]).then_inc(hist_load, 16)
                po.wait_ge(ffn_zero, 2 * layer + 2)
                po.wait_ge(hist_load, 16 * (layer + 1))

                def row(jb, u, peeled):
                    j = jb * 2 + u
                    s = ffn_a[:, u, SO:CW].rearrange("p (b w) -> p b w", b=NB)
                    if not peeled:
                        po.wait_ge(fd.sem, fd.at("c2", j + base - 2))
                        po.wait_ge(fp.sem, fp.at("out", j + base - 2))
                    po.tensor_copy(s[:, :, 0:2], ffn_hist[:, bass.ds(j, 1), :, :].rearrange("p a b w -> p (a b) w")).then_inc(fp.sem, 1)
                    po.wait_ge(freed[0], SB[name] + j + 1)
                    fo = ffn_out[:, bass.ds(j, 1), :]
                    po.tensor_copy(fo[:, :, 0:2].rearrange("p a w -> p (a w)"), ffn_a[:, u, SEQ:SEQ + 2])
                    po.tensor_copy(fo[:, :, 2:18].rearrange("p a (b w) -> p (a b) w", b=NB), s[:, :, 4:6]).then_inc(fp.sem, 1)

                row(0, 0, True)
                row(0, 1, True)
                with po.Fori(1, FC // 2) as jb:
                    row(jb, 0, False)
                    row(jb, 1, False)
                po.wait_ge(fp.sem, fp.at("out", base + FC - 1))
                po.dma_start(A["o_ffn"][layer], ffn_out).then_inc(hist_store, 16)
                return stores + 1

            sums(0, "out0", stores)
            stores = ffn(0, stores)
            sums(1, "down0", stores)
            stores = NSA_POOL(po, stores, hist_store)
            sums(2, "out1", stores)
            stores = ffn(1, stores)
            sums(3, "down1", stores)
            po.wait_ge(hist_store, 16 * stores)


OUTS = {
    "o_x": (128, KC, T), "o_sconv": (128, 4, 18), "o_ret_p": (128, RH * 128), "o_ret_s": (128, NB, RH, 128),
    "o_ffn": (2, 128, FC, 18),
    "o_kv": (128, 12, T), "o_win_k": (NB, 128, 2, W), "o_win_v": (NB, W, 256),
}


def pieces_of(w):
    k, n = w.shape
    return np.ascontiguousarray(w.reshape(k // 128, 128, n // 128, 128).transpose(2, 1, 0, 3)).reshape(n // 128, 128, k)


def by_part(v):
    f = v.shape[-1]
    u = v.reshape(v.shape[:-1] + (f // 128, 128))
    return np.moveaxis(u, -1, 0)


def kernel(**inputs):
    import concourse.bacc as bacc
    from concourse.bass_utils import run_bass_kernel_spmd

    I = {k: np.asarray(v) for k, v in inputs.items()}
    A = {}
    xs = np.concatenate([I["x_prompt"][0], I["x_sample"].reshape(NS, D)])
    A["xT"] = xs.T.reshape(KC, 128, T).transpose(1, 0, 2)
    we = I["w_in_even"][0]
    h, b, c, q, k, v, g = (we[:, 512 * n:512 * n + 512] for n in range(7))
    A["w_in0"] = pieces_of(np.concatenate([q, k, v, g, c, h, b], 1))
    A["w_out0"] = pieces_of(I["w_out_even"][0])
    for l in range(2):
        up = I["ffn_w_up"][l].reshape(D, 2, FC, 128).transpose(0, 2, 1, 3).reshape(D, 2 * DFF)
        A[f"w_up{l}"] = pieces_of(up)
        A[f"w_down{l}"] = pieces_of(I["ffn_w_down"][l])
    wo = I["w_in_odd"][0]

    def heads(w, axis):
        s = w.shape
        if axis == 1:
            return w.reshape(s[0], 2, 2, 4, -1).transpose(0, 1, 3, 2, 4).reshape(s)
        return w.reshape(2, 2, 4, -1, s[1]).transpose(0, 2, 1, 3, 4).reshape(s)

    A["w_in1"] = pieces_of(np.concatenate([heads(wo[:, 0:1024], 1), wo[:, 1024:2560]], 1))
    gates = wo[:, 2560:2608].reshape(D, 3, 2, 2, 4).transpose(0, 1, 2, 4, 3).reshape(D, 48)
    A["w_gate"] = gates.reshape(KC, 128, 48).transpose(1, 0, 2)
    A["w_out1"] = pieces_of(heads(I["w_out_odd"][0], 0))
    A["w1"] = I["cmp_w1"][0].reshape(2, 16, 128, 128).transpose(2, 0, 1, 3).reshape(128, 2, 2048)
    A["w2"] = I["cmp_w2"][0].transpose(1, 0, 2)
    A["state_ret"] = I["state_ret"][0].transpose(2, 0, 1, 3)
    A["state_sconv"] = I["state_sconv"][0].reshape(NB, 2, 4, 128).transpose(3, 2, 0, 1)
    A["state_ffn"] = I["state_ffn_conv"].reshape(2, NB, 2, FC, 128).transpose(0, 4, 3, 1, 2)
    A["keep"] = np.concatenate([CONSTS[k] for k in KEEP], 1)
    A["early"] = np.concatenate([CONSTS[k] for k in EARLY], 1)
    sconv = np.concatenate([I["sconv_w"][0], I["sconv_b"]], 0)
    fconv = np.concatenate([I["ffn_conv_w"], I["ffn_conv_b"][:, None]], 1)
    ln_g = np.stack([I["ln_mix_g"][0], I["ln_ffn_g"][0], I["ln_mix_g"][1], I["ln_ffn_g"][1]])
    ln_b = np.stack([I["ln_mix_b"][0], I["ln_ffn_b"][0], I["ln_mix_b"][1], I["ln_ffn_b"][1]])
    vecs = [by_part(sconv).transpose(0, 2, 1), by_part(I["ret_gn_g"][0]), by_part(ln_g), by_part(ln_b),
            by_part(fconv).transpose(0, 1, 3, 2), I["cmp_pe"][0].reshape(2, 16, 128).transpose(2, 0, 1)]
    A["vecs"] = np.concatenate([v.reshape(128, -1) for v in vecs], 1)
    pages_k = I["cache_cmp_k"][0], I["cache_cmp_v"][0]
    for n, p in zip(("cmp_k", "cmp_v"), pages_k):
        A[n] = p.reshape(NPHYS, 8, 8, 2, 4, 64).transpose(0, 3, 5, 2, 4, 1).reshape(NPHYS, 128, 256)
    A["slc_k"] = I["cache_slc_k"][0].reshape(NPHYS, 128, 2, 128).transpose(0, 3, 2, 1).reshape(NPHYS, 128, 256)
    A["slc_v"] = I["cache_slc_v"][0].reshape(NPHYS, 128, 256)
    A["win_k"] = I["cache_win_k"][0].reshape(NB, W, 2, 128).transpose(0, 3, 2, 1)
    A["win_v"] = I["cache_win_v"][0].reshape(NB, 4, 128, 256)
    A["page_table"] = I["page_table"].reshape(1, NB * NPG)

    nc = bacc.Bacc("TRN2", target_bir_lowering=False, num_devices=1)
    arrays, aps = {}, {}
    for name, a in A.items():
        a = np.ascontiguousarray(a)
        arrays["in_" + name] = a
        aps[name] = nc.dram_tensor("in_" + name, a.shape, mybir.dt.from_np(a.dtype), kind="ExternalInput").ap()
    for name, shape in OUTS.items():
        aps[name] = nc.dram_tensor("out_" + name, shape, F32, kind="ExternalOutput").ap()
    build(nc, aps)
    R = run_bass_kernel_spmd(nc, [arrays], core_ids=[0]).results[0]
    R = {n: np.asarray(R["out_" + n]) for n in OUTS}

    yT = R["o_x"].transpose(2, 1, 0).reshape(T, D)

    def conv_states(v, n):
        rows = v.transpose(2, 1, 0).reshape(18, n)
        return rows[0:2][None], rows[2:18].reshape(NB, 2, n)

    sp_, ss = conv_states(R["o_sconv"], 512)
    ret_p = R["o_ret_p"].reshape(128, RH, 128).transpose(1, 0, 2)[None]
    ret_s = R["o_ret_s"].transpose(1, 2, 0, 3)
    ff = [conv_states(R["o_ffn"][l], DFF) for l in range(2)]
    kvT = R["o_kv"].transpose(2, 1, 0).reshape(T, 6, 4, 64)
    p = [kvT[:SEQ, n][None, None] for n in range(6)]
    s = [kvT[SEQ:, n].reshape(1, NB, NT, 4, 64) for n in range(6)]
    wk = R["o_win_k"].transpose(0, 3, 2, 1).reshape(1, NB, W, 4, 64)
    wv = R["o_win_v"].reshape(1, NB, W, 4, 64)
    out = [yT[None, :SEQ], yT[SEQ:].reshape(NB, NT, D), sp_[None], ss[None], ret_p[None], ret_s[None],
           p[0], p[1], p[2], p[3], s[0], s[1], s[2], s[3], p[4], p[5], wk, wv,
           np.stack([ff[0][0], ff[1][0]]), np.stack([ff[0][1], ff[1][1]])]
    return tuple(np.ascontiguousarray(o) for o in out)
```
